# Optimizing a Trainium2 kernel written in Bass

```python
import math
import jax, jax.numpy as jnp
from jax import lax
import numpy as np

D_MODEL = 1024
BATCH = 1
SEQ = 512
DEPTH = 2

CHUNK = 64
N_MIXERS = 2
EPS = 1e-6

RET_HEADS = 4
RET_QK_DIM = D_MODEL // RET_HEADS
RET_V_DIM = 2 * D_MODEL // RET_HEADS
RET_QK_WIDTH = RET_HEADS * RET_QK_DIM
RET_WIDTH = RET_HEADS * RET_V_DIM
ROPE_BASE = 10000.0

ATT_HEADS = 16
ATT_HEAD_DIM = 2 * D_MODEL // ATT_HEADS
ATT_WIDTH = ATT_HEADS * ATT_HEAD_DIM
LEFT_CHUNKS = 8
BAND = (LEFT_CHUNKS + 1) * CHUNK
MAX_REL = 2 * CHUNK

N_RET_LAYERS = (DEPTH + 1) // 2
N_ATT_LAYERS = DEPTH // 2


def rms_norm_f32(t, gain):
    t32 = t.astype(jnp.float32)
    return t32 * lax.rsqrt(jnp.mean(t32 * t32, axis=-1, keepdims=True) + EPS) * gain.astype(jnp.float32)

def apply_rope(t, cos, sin):
    t1, t2 = jnp.split(t, 2, axis=-1)
    return jnp.concatenate([t1 * cos - t2 * sin, t1 * sin + t2 * cos], axis=-1)

def retention_mixer(h, positions, w_in, gn_g, w_out):
    B, S, _ = h.shape
    nc = S // CHUNK
    proj = h @ w_in
    q, k, v, g = jnp.split(proj, [RET_QK_WIDTH, 2 * RET_QK_WIDTH, 2 * RET_QK_WIDTH + RET_WIDTH], axis=-1)
    q = q.reshape(B, S, RET_HEADS, RET_QK_DIM).astype(jnp.float32)
    k = k.reshape(B, S, RET_HEADS, RET_QK_DIM).astype(jnp.float32)
    v = v.reshape(B, S, RET_HEADS, RET_V_DIM).astype(jnp.float32)

    inv_freq = 1.0 / (ROPE_BASE ** (jnp.arange(0, RET_QK_DIM, 2, dtype=jnp.float32) / RET_QK_DIM))
    ang = positions.astype(jnp.float32)[..., None] * inv_freq
    cos, sin = jnp.cos(ang)[:, :, None, :], jnp.sin(ang)[:, :, None, :]
    q = apply_rope(q, cos, sin)
    k = apply_rope(k, cos, sin) * (RET_QK_DIM ** -0.5)

    def to_chunks(t):
        return t.reshape(B, nc, CHUNK, RET_HEADS, t.shape[-1]).transpose(0, 3, 1, 2, 4)

    qc, kc, vc = to_chunks(q), to_chunks(k), to_chunks(v)

    log_gamma = jnp.log(1.0 - 2.0 ** (-5.0 - jnp.arange(RET_HEADS, dtype=jnp.float32)))
    idx = jnp.arange(CHUNK, dtype=jnp.float32)
    intra_decay = jnp.exp(log_gamma[:, None, None] * jnp.abs(idx[:, None] - idx[None, :]))
    q_decay = jnp.exp(log_gamma[:, None] * (idx + 1.0))
    k_decay = jnp.exp(log_gamma[:, None] * (CHUNK - 1.0 - idx))
    chunk_decay = jnp.exp(log_gamma * CHUNK)

    scores = jnp.einsum('bhncd,bhnkd->bhnck', qc, kc) * intra_decay[:, None]
    o_intra = jnp.einsum('bhnck,bhnke->bhnce', scores, vc)

    def step(state, xs):
        q_j, k_j, v_j = xs
        o_j = jnp.einsum('bhcd,bhde->bhce', q_j * q_decay[:, :, None], state)
        state = chunk_decay[:, None, None] * state + jnp.einsum(
            'bhcd,bhce->bhde', k_j * k_decay[:, :, None], v_j)
        return state, o_j

    xs = (qc.transpose(2, 0, 1, 3, 4), kc.transpose(2, 0, 1, 3, 4), vc.transpose(2, 0, 1, 3, 4))
    state0 = jnp.zeros((B, RET_HEADS, RET_QK_DIM, RET_V_DIM), jnp.float32)
    _, o_inter = lax.scan(step, state0, xs)

    o = o_intra + o_inter.transpose(1, 2, 0, 3, 4)
    o = o.transpose(0, 2, 3, 1, 4).reshape(B, S, RET_HEADS, RET_V_DIM)
    o = rms_norm_f32(o, gn_g.reshape(RET_HEADS, RET_V_DIM))
    o = o.reshape(B, S, RET_WIDTH) * jax.nn.silu(g.astype(jnp.float32))
    return o.astype(h.dtype) @ w_out

def chunked_attention_mixer(h, w_in, q_g, k_g, rel_table, w_out):
    B, S, _ = h.shape
    nc = S // CHUNK
    proj = h @ w_in
    q, k, v, g = jnp.split(proj, 4, axis=-1)
    q = rms_norm_f32(q.reshape(B, S, ATT_HEADS, ATT_HEAD_DIM), q_g)
    k = rms_norm_f32(k.reshape(B, S, ATT_HEADS, ATT_HEAD_DIM), k_g)
    v = v.reshape(B, S, ATT_HEADS, ATT_HEAD_DIM).astype(jnp.float32)

    pad = LEFT_CHUNKS * CHUNK
    k_pad = jnp.pad(k, ((0, 0), (pad, 0), (0, 0), (0, 0)))
    v_pad = jnp.pad(v, ((0, 0), (pad, 0), (0, 0), (0, 0)))

    qi = jnp.arange(CHUNK)
    kb = jnp.arange(BAND)
    rel = qi[:, None] + pad - kb[None, :]
    bias = rel_table.astype(jnp.float32)[:, jnp.clip(rel, -MAX_REL, MAX_REL) + MAX_REL]
    scale = ATT_HEAD_DIM ** -0.5

    q_chunks = q.reshape(B, nc, CHUNK, ATT_HEADS, ATT_HEAD_DIM).transpose(1, 0, 2, 3, 4)

    def one_chunk(args):
        j, q_j = args
        k_j = lax.dynamic_slice_in_dim(k_pad, j * CHUNK, BAND, axis=1)
        v_j = lax.dynamic_slice_in_dim(v_pad, j * CHUNK, BAND, axis=1)
        s = jnp.einsum('bqhd,bkhd->bhqk', q_j, k_j) * scale + bias
        valid = kb >= (LEFT_CHUNKS - j) * CHUNK
        s = jnp.where(valid, s, jnp.float32(-1e30))
        p = jax.nn.softmax(s, axis=-1)
        return jnp.einsum('bhqk,bkhd->bqhd', p, v_j)

    o = lax.map(one_chunk, (jnp.arange(nc), q_chunks))
    o = o.transpose(1, 0, 2, 3, 4).reshape(B, S, ATT_WIDTH)
    o = o * jax.nn.silu(g.astype(jnp.float32))
    return o.astype(h.dtype) @ w_out

def first_inputs(seed: int = 0) -> dict:
    key = jax.random.key(seed)
    ks = jax.random.split(key, 16)
    D = D_MODEL
    x = jax.random.normal(ks[0], (BATCH, SEQ, D), jnp.float32)
    c = jax.random.normal(ks[1], (BATCH, D), jnp.float32)
    offsets = jax.random.randint(ks[2], (BATCH, 1), 0, 4096, dtype=jnp.int32)
    positions = offsets + jnp.arange(SEQ, dtype=jnp.int32)[None, :]
    norm_g = 1.0 + 0.1 * jax.random.normal(ks[3], (DEPTH, D), jnp.float32)
    ada_w = jax.random.normal(ks[4], (DEPTH, D, 3 * D), jnp.float32) * D ** -0.5
    ada_b = 0.02 * jax.random.normal(ks[5], (DEPTH, 3 * D), jnp.float32)
    ret_w_in = jax.random.normal(ks[6], (N_RET_LAYERS, D, 2 * RET_QK_WIDTH + 2 * RET_WIDTH), jnp.float32) * D ** -0.5
    ret_gn_g = 1.0 + 0.1 * jax.random.normal(ks[7], (N_RET_LAYERS, RET_WIDTH), jnp.float32)
    ret_w_out = jax.random.normal(ks[8], (N_RET_LAYERS, RET_WIDTH, D), jnp.float32) * RET_WIDTH ** -0.5
    att_w_in = jax.random.normal(ks[9], (N_ATT_LAYERS, D, 4 * ATT_WIDTH), jnp.float32) * D ** -0.5
    att_q_g = 1.0 + 0.1 * jax.random.normal(ks[10], (N_ATT_LAYERS, ATT_HEAD_DIM), jnp.float32)
    att_k_g = 1.0 + 0.1 * jax.random.normal(ks[11], (N_ATT_LAYERS, ATT_HEAD_DIM), jnp.float32)
    att_rel_bias = 0.5 * jax.random.normal(ks[12], (N_ATT_LAYERS, ATT_HEADS, 2 * MAX_REL + 1), jnp.float32)
    att_w_out = jax.random.normal(ks[13], (N_ATT_LAYERS, ATT_WIDTH, D), jnp.float32) * ATT_WIDTH ** -0.5
    return {"x": x, "c": c, "positions": positions, "norm_g": norm_g, "ada_w": ada_w,
            "ada_b": ada_b, "ret_w_in": ret_w_in, "ret_gn_g": ret_gn_g, "ret_w_out": ret_w_out,
            "att_w_in": att_w_in, "att_q_g": att_q_g, "att_k_g": att_k_g,
            "att_rel_bias": att_rel_bias, "att_w_out": att_w_out}

def first_block(x, c, positions, norm_g, ada_w, ada_b, ret_w_in, ret_gn_g, ret_w_out,
              att_w_in, att_q_g, att_k_g, att_rel_bias, att_w_out):
    cond = jax.nn.silu(c.astype(jnp.float32))
    for i in range(DEPTH):
        mod = cond @ ada_w[i].astype(jnp.float32) + ada_b[i].astype(jnp.float32)
        shift, scale, gate = jnp.split(mod[:, None, :], 3, axis=-1)
        h = (rms_norm_f32(x, norm_g[i]) * (1.0 + scale) + shift).astype(x.dtype)
        j = i // N_MIXERS
        if i % N_MIXERS == 0:
            out = retention_mixer(h, positions, ret_w_in[j], ret_gn_g[j], ret_w_out[j])
        else:
            out = chunked_attention_mixer(h, att_w_in[j], att_q_g[j], att_k_g[j],
                                          att_rel_bias[j], att_w_out[j])
        x = x + (gate * out.astype(jnp.float32)).astype(x.dtype)
    return x


DEPTH_2 = 1

D_MIX = 1024
GDN_HEADS = 4
GDN_HEAD_DIM = 128
GDN_WIDTH = 512
GDN_CONV = 4
GDN_CHUNK = 64
DSA_HEADS = 4
DSA_HEAD_DIM = 64
DSA_WIDTH = 256
DSA_Q_RANK = 256
DSA_KV_RANK = 128
IDX_HEADS = 4
IDX_DIM = 64
DSA_TOPK_MAX = 256
Q_BLOCK = 128
CONV_CH = 256
CONV_WIDTH = 31
MEM_LEN = 256
XA_HEADS = 4
XA_HEAD_DIM = 128
XA_WIDTH = 512
D_FF = 4 * D_MODEL

IN_SPLITS = (3 * GDN_WIDTH, GDN_WIDTH, GDN_HEADS, GDN_HEADS,
             DSA_Q_RANK, DSA_KV_RANK, IDX_DIM, IDX_HEADS, 2 * CONV_CH)
N_IN = 3 * GDN_WIDTH + GDN_WIDTH + 2 * GDN_HEADS + DSA_Q_RANK + DSA_KV_RANK + IDX_DIM + IDX_HEADS + 2 * CONV_CH


def rms_norm(x, g):
    xf = x.astype(jnp.float32)
    y = xf * lax.rsqrt(jnp.mean(xf * xf, axis=-1, keepdims=True) + EPS)
    return (y * g.astype(jnp.float32)).astype(x.dtype)

def layer_norm(x, g, b):
    xf = x.astype(jnp.float32)
    mu = jnp.mean(xf, axis=-1, keepdims=True)
    xc = xf - mu
    var = jnp.mean(xc * xc, axis=-1, keepdims=True)
    y = xc * lax.rsqrt(var + EPS) * g.astype(jnp.float32) + b.astype(jnp.float32)
    return y.astype(x.dtype)

def l2_norm(x):
    return x * lax.rsqrt(jnp.sum(x * x, axis=-1, keepdims=True) + EPS)

def split_cols(t, sizes):
    out = []
    off = 0
    for n in sizes:
        out.append(t[..., off:off + n])
        off += n
    return out

def causal_depthwise_conv(x, w):
    k, c = w.shape
    return lax.conv_general_dilated(
        x, w[:, None, :].astype(x.dtype), window_strides=(1,), padding=((k - 1, 0),),
        dimension_numbers=("NWC", "WIO", "NWC"), feature_group_count=c)

def gated_delta_rule(q, k, v, g, beta):
    b, s, h, dk = q.shape
    dv = v.shape[-1]
    c = GDN_CHUNK
    n = s // c
    q = q * (dk ** -0.5)

    def chunk(t):
        return jnp.moveaxis(t.reshape((b, n, c) + t.shape[2:]), 3, 2)

    qc, kc, vc = chunk(q), chunk(k), chunk(v)
    gc, bc = chunk(g), chunk(beta)
    decay = jnp.cumsum(gc, axis=-1)
    tril = jnp.tril(jnp.ones((c, c), bool))
    strict = jnp.tril(jnp.ones((c, c), bool), -1)
    diff = decay[..., :, None] - decay[..., None, :]
    gamma = jnp.where(tril, jnp.exp(jnp.where(tril, diff, 0.0)), 0.0)
    kb = kc * bc[..., None]
    a_mat = jnp.where(strict, jnp.einsum("bnhid,bnhjd->bnhij", kb, kc) * gamma, 0.0)
    lhs = a_mat + jnp.eye(c, dtype=a_mat.dtype)
    rhs = jnp.concatenate([vc * bc[..., None], kb * jnp.exp(decay)[..., None]], axis=-1)
    sol = lax.linalg.triangular_solve(lhs, rhs, left_side=True, lower=True, unit_diagonal=True)
    u, w = sol[..., :dv], sol[..., dv:]
    qk = jnp.where(tril, jnp.einsum("bnhid,bnhjd->bnhij", qc, kc) * gamma, 0.0)

    def step(state, inp):
        q_i, k_i, u_i, w_i, qk_i, dec_i = inp
        v_new = u_i - jnp.einsum("bhcd,bhde->bhce", w_i, state)
        o = (jnp.einsum("bhcd,bhde->bhce", q_i * jnp.exp(dec_i)[..., None], state)
             + jnp.einsum("bhij,bhje->bhie", qk_i, v_new))
        last = dec_i[..., -1]
        k_dec = k_i * jnp.exp(last[..., None] - dec_i)[..., None]
        state = state * jnp.exp(last)[..., None, None] + jnp.einsum("bhcd,bhce->bhde", k_dec, v_new)
        return state, o

    xs = tuple(jnp.moveaxis(t, 1, 0) for t in (qc, kc, u, w, qk, decay))
    _, o = lax.scan(step, jnp.zeros((b, h, dk, dv), jnp.float32), xs)
    o = jnp.swapaxes(jnp.moveaxis(o, 0, 1), 2, 3)
    return o.reshape(b, s, h, dv)

def gdn_mixer(qkv, z, a_g, b_g, conv_w, a_log, dt_bias, norm_g):
    b, s, _ = qkv.shape
    dt = qkv.dtype
    qkv = jax.nn.silu(causal_depthwise_conv(qkv, conv_w)).astype(jnp.float32)
    q, k, v = jnp.split(qkv, 3, axis=-1)
    shp = (b, s, GDN_HEADS, GDN_HEAD_DIM)
    q = l2_norm(q.reshape(shp))
    k = l2_norm(k.reshape(shp))
    v = v.reshape(shp)
    g = -jnp.exp(a_log.astype(jnp.float32)) * jax.nn.softplus(a_g.astype(jnp.float32) + dt_bias.astype(jnp.float32))
    beta = jax.nn.sigmoid(b_g.astype(jnp.float32))
    o = gated_delta_rule(q, k, v, g, beta)
    o = rms_norm(o, norm_g) * jax.nn.silu(z.astype(jnp.float32).reshape(shp))
    return o.reshape(b, s, GDN_WIDTH).astype(dt)

def dsa_mixer(c_q, c_kv, k_idx, w_idx, w_qb, w_qi, w_kvb, q_norm_g, k_norm_g):
    b, s, _ = c_q.shape
    q = rms_norm((c_q @ w_qb).reshape(b, s, DSA_HEADS, DSA_HEAD_DIM), q_norm_g)
    kv = c_kv @ w_kvb
    k = rms_norm(kv[..., :DSA_HEAD_DIM], k_norm_g)
    v = kv[..., DSA_HEAD_DIM:]
    q_idx = (c_q @ w_qi).reshape(b, s, IDX_HEADS, IDX_DIM)
    w_idx = w_idx.astype(jnp.float32) * (IDX_HEADS ** -0.5 * IDX_DIM ** -0.5)
    k_idx = k_idx.astype(jnp.float32)
    topk = min(DSA_TOPK_MAX, s // 4)
    nb = s // Q_BLOCK
    pos = jnp.arange(s, dtype=jnp.int32)

    def blk(t):
        return jnp.moveaxis(t.reshape((b, nb, Q_BLOCK) + t.shape[2:]), 1, 0)

    def attend(inp):
        q_b, qi_b, w_b, t_b = inp
        causal = pos[None, :] <= t_b[:, None]
        idx_logits = jnp.einsum("bqhd,bsd->bqhs", qi_b.astype(jnp.float32), k_idx)
        score = jnp.einsum("bqh,bqhs->bqs", w_b, jax.nn.relu(idx_logits))
        score = jnp.where(causal[None], score, -jnp.inf)
        _, sel = lax.top_k(score, topk)
        k_sel = jax.vmap(lambda kk, ii: kk[ii])(k, sel)
        v_sel = jax.vmap(lambda vv, ii: vv[ii])(v, sel)
        valid = sel <= t_b[None, :, None]
        logits = jnp.einsum("bqhd,bqkd->bqhk", q_b.astype(jnp.float32), k_sel.astype(jnp.float32)) * (DSA_HEAD_DIM ** -0.5)
        logits = jnp.where(valid[:, :, None, :], logits, -jnp.inf)
        p = jax.nn.softmax(logits, axis=-1)
        return jnp.einsum("bqhk,bqkd->bqhd", p, v_sel.astype(jnp.float32)).astype(q_b.dtype)

    o = lax.map(attend, (blk(q), blk(q_idx), blk(w_idx), pos.reshape(nb, Q_BLOCK)))
    return jnp.moveaxis(o, 0, 1).reshape(b, s, DSA_WIDTH)

def conv_mixer(ug, dw, dw_b, ln_g, ln_b):
    u, gate = jnp.split(ug, 2, axis=-1)
    y = u * jax.nn.sigmoid(gate)
    y = causal_depthwise_conv(y, dw) + dw_b
    y = layer_norm(y, ln_g, ln_b)
    return jax.nn.silu(y)

def memory_cross_attention(h, mem_n, wq, wkv, q_g, k_g, wo):
    b, s, _ = h.shape
    m = mem_n.shape[1]
    q = rms_norm((h @ wq).reshape(b, s, XA_HEADS, XA_HEAD_DIM), q_g)
    kv = mem_n @ wkv
    k = rms_norm(kv[..., :XA_WIDTH].reshape(b, m, XA_HEADS, XA_HEAD_DIM), k_g)
    v = kv[..., XA_WIDTH:].reshape(b, m, XA_HEADS, XA_HEAD_DIM)
    logits = jnp.einsum("bshd,bmhd->bhsm", q.astype(jnp.float32), k.astype(jnp.float32)) * (XA_HEAD_DIM ** -0.5)
    p = jax.nn.softmax(logits, axis=-1)
    o = jnp.einsum("bhsm,bmhd->bshd", p, v.astype(jnp.float32)).astype(h.dtype)
    return o.reshape(b, s, XA_WIDTH) @ wo

def second_inputs(seed: int = 0) -> dict:
    key = jax.random.key(seed)
    ks = jax.random.split(key, 32)
    f32 = jnp.float32

    def nrm(k, shape, scale):
        return jax.random.normal(k, shape, f32) * scale

    def gain(k, shape):
        return 1.0 + 0.02 * jax.random.normal(k, shape, f32)

    dt = jnp.exp(jax.random.uniform(ks[5], (DEPTH_2, GDN_HEADS), f32, math.log(1e-3), math.log(1e-1)))
    dt_bias = dt + jnp.log(-jnp.expm1(-dt))
    return {
        "x": nrm(ks[0], (BATCH, SEQ, D_MODEL), 1.0),
        "mem": nrm(ks[1], (BATCH, MEM_LEN, D_MODEL), 1.0),
        "norm_mix": gain(ks[2], (DEPTH_2, D_MODEL)),
        "w_in": nrm(ks[3], (DEPTH_2, D_MODEL, N_IN), D_MODEL ** -0.5),
        "gdn_conv": nrm(ks[4], (DEPTH_2, GDN_CONV, 3 * GDN_WIDTH), GDN_CONV ** -0.5),
        "gdn_a_log": jnp.log(jax.random.uniform(ks[6], (DEPTH_2, GDN_HEADS), f32, 1.0, 16.0)),
        "gdn_dt_bias": dt_bias,
        "gdn_norm": gain(ks[7], (DEPTH_2, GDN_HEAD_DIM)),
        "dsa_w_qb": nrm(ks[8], (DEPTH_2, DSA_Q_RANK, DSA_WIDTH), DSA_Q_RANK ** -0.5),
        "dsa_w_qi": nrm(ks[9], (DEPTH_2, DSA_Q_RANK, IDX_HEADS * IDX_DIM), DSA_Q_RANK ** -0.5),
        "dsa_w_kvb": nrm(ks[10], (DEPTH_2, DSA_KV_RANK, 2 * DSA_HEAD_DIM), DSA_KV_RANK ** -0.5),
        "dsa_q_norm": gain(ks[11], (DEPTH_2, DSA_HEAD_DIM)),
        "dsa_k_norm": gain(ks[12], (DEPTH_2, DSA_HEAD_DIM)),
        "conv_dw": nrm(ks[13], (DEPTH_2, CONV_WIDTH, CONV_CH), CONV_WIDTH ** -0.5),
        "conv_dw_b": nrm(ks[14], (DEPTH_2, CONV_CH), 0.02),
        "conv_ln_g": gain(ks[15], (DEPTH_2, CONV_CH)),
        "conv_ln_b": nrm(ks[16], (DEPTH_2, CONV_CH), 0.02),
        "w_out": nrm(ks[17], (DEPTH_2, D_MIX, D_MODEL), D_MIX ** -0.5),
        "norm_mem": gain(ks[18], (D_MODEL,)),
        "norm_cross": gain(ks[19], (DEPTH_2, D_MODEL)),
        "xa_wq": nrm(ks[20], (DEPTH_2, D_MODEL, XA_WIDTH), D_MODEL ** -0.5),
        "xa_wkv": nrm(ks[21], (DEPTH_2, D_MODEL, 2 * XA_WIDTH), D_MODEL ** -0.5),
        "xa_q_norm": gain(ks[22], (DEPTH_2, XA_HEAD_DIM)),
        "xa_k_norm": gain(ks[23], (DEPTH_2, XA_HEAD_DIM)),
        "xa_wo": nrm(ks[24], (DEPTH_2, XA_WIDTH, D_MODEL), XA_WIDTH ** -0.5),
        "norm_mlp": gain(ks[25], (DEPTH_2, D_MODEL)),
        "mlp_w1": nrm(ks[26], (DEPTH_2, D_MODEL, D_FF), D_MODEL ** -0.5),
        "mlp_w2": nrm(ks[27], (DEPTH_2, D_FF, D_MODEL), D_FF ** -0.5),
    }

def second_block(x, mem, norm_mix, w_in, gdn_conv, gdn_a_log, gdn_dt_bias, gdn_norm,
              dsa_w_qb, dsa_w_qi, dsa_w_kvb, dsa_q_norm, dsa_k_norm,
              conv_dw, conv_dw_b, conv_ln_g, conv_ln_b, w_out,
              norm_mem, norm_cross, xa_wq, xa_wkv, xa_q_norm, xa_k_norm, xa_wo,
              norm_mlp, mlp_w1, mlp_w2):
    mem_n = rms_norm(mem, norm_mem)
    for l in range(DEPTH_2):
        h = rms_norm(x, norm_mix[l])
        proj = h @ w_in[l]
        qkv, z, a_g, b_g, c_q, c_kv, k_idx, w_idx, ug = split_cols(proj, IN_SPLITS)
        y_a = gdn_mixer(qkv, z, a_g, b_g, gdn_conv[l], gdn_a_log[l], gdn_dt_bias[l], gdn_norm[l])
        y_b = dsa_mixer(c_q, c_kv, k_idx, w_idx, dsa_w_qb[l], dsa_w_qi[l], dsa_w_kvb[l],
                        dsa_q_norm[l], dsa_k_norm[l])
        y_c = conv_mixer(ug, conv_dw[l], conv_dw_b[l], conv_ln_g[l], conv_ln_b[l])
        x = x + jnp.concatenate([y_a, y_b, y_c], axis=-1) @ w_out[l]
        x = x + memory_cross_attention(rms_norm(x, norm_cross[l]), mem_n, xa_wq[l], xa_wkv[l],
                                       xa_q_norm[l], xa_k_norm[l], xa_wo[l])
        hm = rms_norm(x, norm_mlp[l]) @ mlp_w1[l]
        x = x + jnp.square(jax.nn.relu(hm)) @ mlp_w2[l]
    return x


def setup_inputs(seed=0):
    out = dict(first_inputs(seed))
    for name, value in second_inputs(seed + 1).items():
        if name != "x":
            out[name + "_2"] = value
    return out


def reference(
    x, c, positions, norm_g, ada_w, ada_b, ret_w_in, ret_gn_g, ret_w_out, att_w_in, att_q_g,
    att_k_g, att_rel_bias, att_w_out, mem_2, norm_mix_2, w_in_2, gdn_conv_2, gdn_a_log_2,
    gdn_dt_bias_2, gdn_norm_2, dsa_w_qb_2, dsa_w_qi_2, dsa_w_kvb_2, dsa_q_norm_2, dsa_k_norm_2,
    conv_dw_2, conv_dw_b_2, conv_ln_g_2, conv_ln_b_2, w_out_2, norm_mem_2, norm_cross_2,
    xa_wq_2, xa_wkv_2, xa_q_norm_2, xa_k_norm_2, xa_wo_2, norm_mlp_2, mlp_w1_2, mlp_w2_2,
):
    x = first_block(
        x, c, positions, norm_g, ada_w, ada_b, ret_w_in, ret_gn_g, ret_w_out, att_w_in, att_q_g,
        att_k_g, att_rel_bias, att_w_out,
    )
    return second_block(
        x, mem_2, norm_mix_2, w_in_2, gdn_conv_2, gdn_a_log_2, gdn_dt_bias_2, gdn_norm_2,
        dsa_w_qb_2, dsa_w_qi_2, dsa_w_kvb_2, dsa_q_norm_2, dsa_k_norm_2, conv_dw_2, conv_dw_b_2,
        conv_ln_g_2, conv_ln_b_2, w_out_2, norm_mem_2, norm_cross_2, xa_wq_2, xa_wkv_2,
        xa_q_norm_2, xa_k_norm_2, xa_wo_2, norm_mlp_2, mlp_w1_2, mlp_w2_2,
    )


_drawn_inputs = setup_inputs


def setup_inputs(seed=0):
    import zlib

    import numpy as np

    out = dict(_drawn_inputs(seed))
    spreads = {}
    factors = {'att_q_g': 6.611,
     'att_k_g': 7.118,
     'norm_mix_2': 3.734,
     'gdn_norm_2': 8.0,
     'dsa_q_norm_2': 8.0,
     'dsa_k_norm_2': 8.0,
     'conv_dw_b_2': 6.028,
     'conv_ln_g_2': 28.724,
     'conv_ln_b_2': 22.474,
     'norm_mem_2': 8.0,
     'norm_cross_2': 8.0,
     'xa_q_norm_2': 8.0,
     'xa_k_norm_2': 8.0,
     'norm_mlp_2': 12.751}
    for name, (base, spread) in spreads.items():
        noise = np.random.default_rng([zlib.crc32(name.encode()), seed]).standard_normal(out[name].shape)
        drawn = base * np.exp(spread * noise) if base else spread * noise
        out[name] = __import__('jax').numpy.asarray(drawn.astype(out[name].dtype))
    for name, factor in factors.items():
        out[name] = (out[name] * factor).astype(out[name].dtype)
    return out
```

```python
from contextlib import ExitStack

import numpy as np

import concourse.bass as bass
from concourse import mybir

ALU = mybir.AluOpType
ACT = mybir.ActivationFunctionType
AX = mybir.AxisListType
F32 = mybir.dt.float32
F32R = mybir.dt.float32r
I32 = mybir.dt.int32

P = 128
D = 1024
S = 512
KT = D // P
NT = S // P
CHUNK = 64
EPS = 1e-6
NEG = -1e30

RH, RQK, RV = 4, 256, 512
AH, AD = 16, 128
GH, GD = 4, 128
DH, DD = 4, 64
TOPK = min(256, S // 4)
CONVW = 31
MEM = 256
XH, XD = 4, 128
DFF = 4 * D
GDN_TAPS = 4

RING = 4
UNIT = KT * P
RSQRT_MAGIC = float(0x5F3759DF)
NEWTON = 3
BEFORE = 128
TURN = 6.283185307179586
TURN_PARTS = (6.28125, 4058 / 2**21, TURN - 6.28125 - 4058 / 2**21)
ROUND = 12582912.0
PI_BELOW = 3.1415925
FINAL = 'mlp_out1'
DIRECT_2 = ['mem_2', 'w_in_2', 'dsa_w_qb_2', 'dsa_w_qi_2', 'dsa_w_kvb_2', 'w_out_2', 'xa_wq_2', 'xa_wkv_2', 'xa_wo_2', 'mlp_w1_2', 'mlp_w2_2']
REGION = 108 * 1024

UNITS = [
    ("ret", RH * 12), ("ret_out", 16), ("att", AH // 2 * 8), ("att_out", 16),
    ("mix", 24), ("mix_out", 8), ("xa_q", 4), ("xa_kv", 8), ("xa_out", 8),
    ("mlp_in0", 16), ("mlp_out0", 16), ("mlp_in1", 16), ("mlp_out1", 16),
]

SMALL_WIDTHS = [
    ("c", KT), ("norm_g0", KT), ("norm_g1", KT), ("ada_b0", 3 * KT), ("ada_b1", 3 * KT),
    ("ret_gn_g", 2 * KT), ("att_q_g", 1), ("att_k_g", 1), ("norm_mix", KT), ("norm_mem", KT),
    ("norm_cross", KT), ("norm_mlp", KT), ("gdn_conv", 12 * GDN_TAPS), ("gdn_a_log", GH),
    ("gdn_dt_bias", GH), ("gdn_norm", 1), ("dsa_q_norm", 1), ("dsa_k_norm", 1),
    ("conv_dw", 2 * CONVW), ("conv_dw_b", 2), ("conv_ln_g", 2), ("conv_ln_b", 2),
    ("xa_q_norm", 1), ("xa_k_norm", 1), ("inv_freq", 1),
]
SMALL = {}
_at = 0
for _name, _n in SMALL_WIDTHS:
    SMALL[_name] = (_at, _n)
    _at += _n
NSMALL = _at

LEVELS = 7
CONST = {"ident": (0, P), "causal": (P, P), "cumsum": (2 * P, P), "halves": (3 * P, 2)}
NCONST = 3 * P + 2


class Steps:

    def __init__(self, sem, known):
        self.sem, self.known, self.marks = sem, known, {}
        self.count, self.loop = BEFORE, None

    def done(self, name=None):
        self.count += 1
        if name is not None:
            self.marks[name] = (self.count, self.loop)
        return self.sem, 1

    def enter(self, loop, i, first=0):
        self.loop, self.start, self.i, self.first = loop, self.count, i, first

    def leave(self, turns):
        per = self.count - self.start
        self.marks["loop " + self.loop] = (per, self.start, self.first)
        self.count = self.start + turns * per
        self.loop = None

    def at(self, name, i=None):
        value, loop = self.known.get(name, (1, None))
        if loop is None:
            return self.sem, value
        per, start, first = self.known["loop " + loop]
        return self.sem, (i - first) * per + value

    def last(self):
        if self.loop is None:
            return self.sem, self.count
        per, start, first = self.known.get("loop " + self.loop, (0, 0, 0))
        return self.sem, (self.i - self.first) * per + self.count

    def after(self, name, turns):
        value, loop = self.known.get(name, (1, None))
        per, start, first = self.known.get("loop " + str(loop), (0, 0, 0))
        return self.sem, (turns - 1) * per + value


def build(nc, ins, out, known):
    ctx = ExitStack()
    with ctx:
        def sb(name, shape, dt=F32, where=ctx):
            return where.enter_context(nc.sbuf_tensor(name, shape, dt))

        def sem(name):
            return ctx.enter_context(nc.semaphore(name))

        xT = sb("xT", [P, KT, S])
        hh = sb("hh", [P, KT, S], F32R)
        hl = sb("hl", [P, KT, S], F32R)
        raw = sb("raw", [P, RING, KT, P])
        wh = sb("wh", [P, RING, KT, P], F32R)
        wl = sb("wl", [P, RING, KT, P], F32R)
        small = sb("small", [P, NSMALL])
        const = sb("const", [P, NCONST])
        ones = sb("ones", [P, P])
        mod = sb("mod", [P, 2, 3, KT])
        gain = sb("gain", [P, 2, KT])
        cond = sb("cond", [P, 2, KT])
        sq = sb("sq", [P, 2, S])
        rs = sb("rs", [P, 3, 32])
        dg = sb("dg", [P, S])
        qk_gain = sb("qk_gain", [P, 4])
        ident = const[:, 0:P]

        def sm(name, a=0, n=None):
            c, w = SMALL[name]
            return small[:, c + a:c + a + (w if n is None else n)]

        def cst(name, a=0, n=None):
            c, w = CONST[name]
            return const[:, c + a:c + a + (w if n is None else n)]

        acc = [ctx.enter_context(nc.psum_tensor(f"acc{b}", [P, S], F32)) for b in range(2)]
        sc = [ctx.enter_context(nc.psum_tensor(f"sc{b}", [P, S], F32)) for b in range(2)]
        ob = [ctx.enter_context(nc.psum_tensor(f"ob{b}", [P, S], F32)) for b in range(2)]
        st = ctx.enter_context(nc.psum_tensor("st", [P, S], F32))
        bc = ctx.enter_context(nc.psum_tensor("bc", [P, S], F32))

        raw_full = [sem(f"raw_full{s}") for s in range(RING)]
        high_done = sem("high_done")
        split_done = sem("split_done")
        unit_used = sem("unit_used")
        slot_free = sem("slot_free")
        small_in, const_in, x_in, pos_in = sem("small_in"), sem("const_in"), sem("x_in"), sem("pos_in")
        decay_in, bias_in, mem_in = sem("decay_in"), [sem("bias_in0"), sem("bias_in1")], sem("mem_in")
        ada_in = [sem(f"ada_in{k}") for k in range(KT)]
        small_w_in = sem("small_w_in")
        ada1_in = [sem("ada1_in0"), sem("ada1_in1")]
        out_done = sem("out_done")
        PE = Steps(sem("tensor_steps"), known.get("PE", {}))
        AC = Steps(sem("scalar_steps"), known.get("AC", {}))
        V = Steps(sem("vector_steps"), known.get("V", {}))
        G = Steps(sem("gpsimd_steps"), known.get("G", {}))


        base = sb("region", [P, REGION // 4])
        region = nc.sbuf_base - REGION

        def at(name, shape, offset, dt=F32):
            size = 4
            for n in shape[1:]:
                size *= n
            assert offset + size <= REGION, (name, offset + size)
            return nc.alloc_sbuf_tensor_at(name, shape, dt, offset=region + offset)

        KB = 1024
        Yh = at("Yh", [P, 16, S], 0, F32R)
        Yl = at("Yl", [P, 16, S], 32 * KB, F32R)
        W = 64 * KB
        ada_w0 = at("ada_w0", [P, KT, 2 * D], 0)
        ada_g0 = at("ada_g0", [P, KT, D], 0)
        x_tok = at("x_tok", [P, NT, D], W)
        ada_acc0 = at("ada_acc0", [P, 2 * D], W + 16 * KB)
        ada_accg = at("ada_accg", [P, D], W + 39 * KB)
        ada_acc1 = at("ada_acc1", [P, 3 * D], W)
        ada_w1 = at("ada_w1", [P, 2, 3 * D], W + 12 * KB)
        q_ = at("ret_q", [P, 2, S], W)
        k_ = at("ret_k", [P, 2, S], W + 4 * KB)
        v_ = at("ret_v", [P, NT, RV], W + 8 * KB)
        s_ = at("ret_gate", [P, 4, S], W + 16 * KB)
        t_ = at("ret_scores", [P, 10 * P], W + 24 * KB)
        tmp = at("ret_tmp", [P, 2, S], W + 29 * KB)
        dec = at("ret_decay", [P, S], W + 33 * KB)
        cos_ = at("cos", [P, S], W + 35 * KB)
        sin_ = at("sin", [P, S], W + 37 * KB)
        ang = at("ang", [P, S], W + 24 * KB)
        pos = at("pos", [P, S], W + 26 * KB, I32)
        o_ = [q_[:, 0, :], q_[:, 1, :], k_[:, 0, :], k_[:, 1, :]]
        aq = at("att_q", [P, 2, S], W)
        ak = at("att_k", [P, 2, S], W + 4 * KB)
        av = at("att_v", [P, NT, 2 * AD], W + 8 * KB)
        ag = at("att_gate", [P, 2, S], W + 12 * KB)
        aS = at("att_scores", [P, 2, 10 * P], W + 16 * KB)
        aP = at("att_probs_t", [P, 2, 10 * P], W + 26 * KB)
        ab = at("att_bias", [P, 2, S], W + 36 * KB)
        ay = at("att_y", [P, 2, S], W + 40 * KB)
        amax = sb("amax", [P, 3, 16])

        Mh = at("Mh", [P, KT, S], 0, F32R)
        Ml = at("Ml", [P, KT, S], 16 * KB, F32R)
        cg = at("conv_gate", [P, 2, S], 77 * KB)
        cy = at("conv_in", [P, 2, CONVW - 1 + S], 81 * KB)
        co = at("conv_out", [P, 2, S], 86 * KB)
        kidx = at("dsa_kidx", [P, S], 32 * KB)
        cq = at("dsa_cq", [P, 2, S], 34 * KB)
        ckv = at("dsa_ckv", [P, S], 38 * KB)
        wqb = at("dsa_wqb", [P, 2, 256], 40 * KB)
        wqi = at("dsa_wqi", [P, 2, 256], 42 * KB)
        wkvb = at("dsa_wkvb", [P, 3 * DD], 44 * KB)
        dq = at("dsa_q", [P, 2, S], 45 * KB)
        dqi = at("dsa_qi", [P, 2, S], 49 * KB)
        dk = at("dsa_k", [P, S], 53 * KB)
        dv = at("dsa_v", [P, NT, DD], 55 * KB)
        score = at("dsa_score", [P, 3, S], 56 * KB)
        work = at("dsa_work", [P, 3, S], 62 * KB)
        dmask = at("dsa_mask", [P, 10 * P], 68 * KB)
        drelu = at("dsa_relu", [P, 2, S], 73 * KB)
        dS = at("dsa_scores", [P, 2, 10 * P], 77 * KB)
        dP = at("dsa_probs_t", [P, 2, 10 * P], 87 * KB)
        gqkv = at("gdn_qkv", [P, 12, S], 32 * KB)
        gz = at("gdn_gate", [P, 4, S], 56 * KB)
        gktok = at("gdn_k_tok", [P, NT, GH, P], 64 * KB)
        gvtok = at("gdn_v_tok", [P, NT, GH, P], 72 * KB)
        gQKT = at("gdn_qk_t", [P, NT, GH, P], 80 * KB)
        gTT = at("gdn_inv_t", [P, NT, GH, P], 88 * KB)
        gT = at("gdn_inv", [P, NT, GH, P], 40 * KB)
        gAT = at("gdn_a_t", [P, NT, GH, P], 48 * KB)
        gwT = at("gdn_w_t", [P, NT, GH, P], 40 * KB)
        gkdec = at("gdn_k_dec", [P, NT, GH, P], 48 * KB)
        goT = at("gdn_o_t", [P, GH, S], 64 * KB)
        gpre = at("gdn_conv_in", [P, 2, GDN_TAPS - 1 + S], 96 * KB)
        gth = at("gdn_tanh", [P, 2, S], 96 * KB + 4224)
        gG = at("gdn_g", [P, GH, P], 96 * KB)
        ggb = at("gdn_g_rows", [P, GH, P], 98 * KB)
        gA = at("gdn_a", [P, GH, P], 100 * KB)
        gQK = at("gdn_qk", [P, GH, P], 102 * KB)
        gMT = at("gdn_level", [P, 2, GH, P], 96 * KB)
        gX = at("gdn_x", [P, 2, GH, P], 100 * KB)
        gvn = at("gdn_v_new", [P, 2, GH, P], 96 * KB)
        gst = at("gdn_state", [P, GH, P], 100 * KB)
        gkbe = at("gdn_kbe", [P, GH, P], 102 * KB)
        glev = at("gdn_levels", [P, LEVELS, P], 104 * KB + 512)
        bankx = acc
        m_tok = at("mem_tok", [P, 2, D], 32 * KB)
        mT = at("mem_t", [P, KT, MEM], 40 * KB)
        mh = at("mem_high", [P, KT, MEM], 48 * KB, F32R)
        ml = at("mem_low", [P, KT, MEM], 56 * KB, F32R)
        xq = at("xa_q", [P, XH, S], 64 * KB)
        xk = at("xa_k", [P, XH, MEM], 72 * KB)
        xv = at("xa_v", [P, 2, XH * XD], 76 * KB)
        xS = at("xa_scores", [P, 2, NT, MEM], 80 * KB)
        xP = at("xa_probs_t", [P, 2, 2, S], 88 * KB)
        wab = sb("gdn_w_ab", [P, KT, 2 * GH])
        wab_high = sb("gdn_w_ab_high", [P, KT, 2 * GH], F32R)
        wab_low = sb("gdn_w_ab_low", [P, KT, 2 * GH], F32R)
        kidx_in, levels_in, dsa_w_in, wab_in = sem("kidx_in"), sem("levels_in"), sem("dsa_w_in"), sem("wab_in")
        tc = sb("tok_cols", [P, NT, 12])
        gc = sb("gdn_cols", [P, 10, 16])
        best = sb("best", [P, 3, 8])
        negs = sb("causal_negative", [P, P])
        strict = sb("strict", [P, P])

        QOFF = [0, 128, 384, 768]
        KOFF = [0, 512, 896, 1152]

        U = {}
        at_unit = 0
        for name, n in UNITS:
            U[name] = at_unit
            at_unit += n
        total_units = at_unit

        def rows(w, k0, k1, c0, n=P):
            return w[k0 * P:k1 * P, bass.ds(c0, n)].rearrange("(k p) n -> p k n", p=P)

        def product(e, bank, u, c, rhs_high, rhs_low, start=True, stop=True, k1=KT, col=0):
            s = c % RING
            e.wait_ge(split_done, u + 1)
            for k in range(k1):
                e.matmul(bank[:, :], wh[:, s, k, :], rhs_high(k), start=(start and k == 0), stop=False)
                e.matmul(bank[:, :], wh[:, s, k, :], rhs_low(k), start=False, stop=False)
                last = e.matmul(bank[:, :], wl[:, s, k, :], rhs_high(k), start=False,
                                stop=(stop and k == k1 - 1))
            last.then_inc(unit_used, 1)

        def feat(e, bank, u, c):
            product(e, bank, u, c, lambda k: hh[:, k, :], lambda k: hl[:, k, :])

        def tok(e, u, c, tag, free, lh=hh, ll=hl, tiles=NT):
            s = c % RING
            assert s % 2 == 0
            e.wait_ge(split_done, u + 2)
            for t in range(tiles):
                if t % 2 == 0:
                    e.wait_ge(*free[t // 2])
                o = acc[t // 2][:, (t % 2) * 256:(t % 2 + 1) * 256].rearrange("p (a n) -> p a n", a=2)
                for k in range(KT):
                    h, l = lh[:, k, t * P:(t + 1) * P], ll[:, k, t * P:(t + 1) * P]
                    e.matmul(o, h, wh[:, s:s + 2, k, :], start=(k == 0), stop=False)
                    e.matmul(o, h, wl[:, s:s + 2, k, :], start=False, stop=False)
                    last = e.matmul(o, l, wh[:, s:s + 2, k, :], start=False, stop=(k == KT - 1))
                if t == tiles - 1:
                    last.then_inc(unit_used, 2)
                elif t % 2 == 1:
                    last.then_inc(*PE.done(tag))

        def columns(e, x, c0, start, stop, name=None, n=NT, parts=P, of=None):
            for t in range(n):
                last = e.matmul(st[:, c0 + t:c0 + t + 1], x[:, t * P:(t + 1) * P],
                                (ones if of is None else of)[0:parts, 0:1],
                                start=(start is True or (start == "first" and t == 0)),
                                stop=(stop is True or (stop == "last" and t == n - 1)))
            if name is not None:
                last.then_inc(*PE.done(name))

        def step(e, ins, steps, name=None):
            ins.then_inc(*steps.done(name))
            e.wait_ge(*steps.last())

        def rsqrt(e, n, scale, name=None):
            y, x, z = rs[:, 0, 0:n], rs[:, 1, 0:n], rs[:, 2, 0:n]
            step(e, e.tensor_scalar(x, st[:, 0:n], scale, EPS, ALU.mult, ALU.add), V)
            step(e, e.tensor_scalar(y.bitcast(I32), x.bitcast(I32), 1, None, ALU.arith_shift_right), V)
            step(e, e.tensor_scalar(y.bitcast(I32), y.bitcast(I32), -1.0, RSQRT_MAGIC, ALU.mult, ALU.add), V)
            for r in range(NEWTON):
                step(e, e.tensor_tensor(z, y, y, ALU.mult), V)
                step(e, e.scalar_tensor_tensor(out=z, in0=z, scalar=-0.5, in1=x, op0=ALU.mult, op1=ALU.mult), V)
                step(e, e.scalar_tensor_tensor(out=y, in0=z, scalar=1.5, in1=y, op0=ALU.add, op1=ALU.mult), V,
                     name if r == NEWTON - 1 else None)

        def diagonal(e, c0, name, n=NT):
            e.tensor_tensor(dg[:, 0:n * P].rearrange("p (t n) -> p t n", t=n),
                            ident.unsqueeze(1).to_broadcast([P, n, P]),
                            rs[:, 0, c0:c0 + n].unsqueeze(2).to_broadcast([P, n, P]), ALU.mult)\
             .then_inc(*V.done(name))

        def spread(e, name, n=NT):
            e.matmul(bc[:, 0:n * P], ones[:, :], dg[:, 0:n * P], start=True, stop=True).then_inc(*PE.done(name))

        def norm_scalar(e, tag, bias, ready, xin=None, hhi=None, n=S):
            xin, hhi = (xT, hh) if xin is None else (xin, hhi)
            for k in range(KT):
                e.wait_ge(*ready(k))
                if k >= 2:
                    e.wait_ge(*PE.at(f"{tag}cols{k - 2}"))
                e.activation(sq[:, k % 2, 0:n], xin[:, k, :], ACT.Square).then_inc(*AC.done(f"{tag}sq{k}"))
            for k in range(KT):
                e.wait_ge(*V.at(f"{tag}t{k}"))
                if bias is not None:
                    step(e, e.activation(sq[:, k % 2, 0:n], sq[:, k % 2, 0:n], ACT.Identity,
                                         bias=bias(k)), AC)
                e.activation(hhi[:, k, :], sq[:, k % 2, 0:n], ACT.Copy).then_inc(*AC.done(f"{tag}hi{k}"))

        def norm_tensor(e, tag, nt=NT):
            for k in range(KT):
                e.wait_ge(*AC.at(f"{tag}sq{k}"))
                columns(e, sq[:, k % 2, :], 0, "first" if k == 0 else False,
                        "last" if k == KT - 1 else False, f"{tag}cols{k}", n=nt)
            e.wait_ge(*V.at(f"{tag}diag"))
            spread(e, f"{tag}bc", nt)

        def norm_vector(e, tag, g, xin=None, hhi=None, hlo=None, n=S):
            xin, hhi, hlo = (xT, hh, hl) if xin is None else (xin, hhi, hlo)
            e.wait_ge(*PE.at(f"{tag}cols{KT - 1}"))
            rsqrt(e, n // P, 1.0 / D)
            diagonal(e, 0, f"{tag}diag", n // P)
            e.wait_ge(*PE.at(f"{tag}bc"))

            def rest(k):
                e.wait_ge(*AC.at(f"{tag}hi{k}"))
                e.tensor_tensor(hlo[:, k, :], sq[:, k % 2, 0:n], hhi[:, k, :].bitcast(F32), ALU.subtract)\
                 .then_inc(*V.done(f"{tag}h{k}"))

            for k in range(KT):
                e.wait_ge(*V.last())
                e.scalar_tensor_tensor(out=sq[:, k % 2, 0:n], in0=xin[:, k, :], scalar=g(k), in1=bc[:, 0:n],
                                       op0=ALU.mult, op1=ALU.mult).then_inc(*V.done(f"{tag}t{k}"))
                if k >= 1:
                    rest(k - 1)
            rest(KT - 1)

        def out_tensor(e, tag, ready):
            c = U[tag]
            e.wait_ge(*ready)
            with e.Fori(0, KT // 2) as i:
                PE.enter(tag, i)
                for b in range(2):
                    e.wait_ge(*V.at(f"{tag}x{b}", i - 1))
                    for half in range(2):
                        product(e, acc[b], c + i * 4 + 2 * b + half, c + 2 * b + half,
                                lambda k: Yh[:, 8 * half + k, :], lambda k: Yl[:, 8 * half + k, :],
                                start=(half == 0), stop=(half == 1))
                PE.leave(KT // 2)

        def out_vector(e, tag, gate, between=None):
            c = U[tag]
            with e.Fori(0, KT // 2) as i:
                V.enter(tag, i)
                for b in range(2):
                    x = xT[:, bass.ds(i * 2 + b, 1), :]
                    p = acc[b][:, :].unsqueeze(1)
                    e.wait_ge(unit_used, c + i * 4 + 2 * b + 2)
                    if gate is None:
                        e.tensor_tensor(x, p, x, ALU.add).then_inc(*V.done(f"{tag}x{b}"))
                    else:
                        e.scalar_tensor_tensor(out=x, in0=p, scalar=gate(i * 2 + b), in1=x,
                                               op0=ALU.mult, op1=ALU.add).then_inc(*V.done(f"{tag}x{b}"))
                    if between is not None:
                        between(e, i, b)
                V.leave(KT // 2)

        def ada_sum(e, accum, w, k, name=None):
            if k == 0:
                step(e, e.tensor_scalar(accum, w, cond[:, 0, 0:1], None, ALU.mult), V, name)
            else:
                step(e, e.scalar_tensor_tensor(out=accum, in0=w, scalar=cond[:, 0, k:k + 1], in1=accum,
                                               op0=ALU.mult, op1=ALU.add), V, name)

        def ada_columns(e, accum, n0, n1, name):
            for n in range(n0, n1):
                last = e.matmul(st[:, n:n + 1], accum[:, (n - n0) * P:(n - n0 + 1) * P], ones[:, 0:1], start=True, stop=True)
            last.then_inc(*PE.done(name))

        def count_from(e, steps):
            e.sem_inc(steps.sem, BEFORE)

        block = ctx.enter_context(nc.Block())

        @block.sync
        def _(e):
            def load(u, c, turn, src, k1=KT, n=P, col=0, k0=0):
                s = c % RING
                if c >= RING or not isinstance(turn, int):
                    e.wait_ge(split_done, u - RING + 1)
                e.dma_start(raw[:, s, k0:k1, col:col + n], src).then_inc(raw_full[s], 16)

            for k in range(KT):
                e.dma_start(ada_w0[:, k, :], ins["ada_w"][0, k * P:(k + 1) * P, 0:2 * D]).then_inc(ada_in[k], 16)

            w = ins["ret_w_in"][0]
            columns_of = [(0, RQK, 0), (0, RQK, 1), (1, RQK, 0), (1, RQK, 1),
                          (2, RV, 0), (2, RV, 1), (2, RV, 2), (2, RV, 3),
                          (3, RV, 0), (3, RV, 1), (3, RV, 2), (3, RV, 3)]
            first = [0, D, 2 * D, 4 * D]

            def load_ret(i, js):
                for j in js:
                    part, width, tile = columns_of[j]
                    c = U["ret"] + j
                    load(c + i * 12, c, i, rows(w, 0, KT, first[part] + i * width + tile * P))

            load_ret(0, range(4))
            e.wait_ge(*V.at("ada0sum"))
            for k in range(KT):
                e.dma_start(ada_g0[:, k, :], ins["ada_w"][0, k * P:(k + 1) * P, 2 * D:3 * D]).then_inc(ada_in[k], 16)
            load_ret(0, range(4, 12))
            with e.Fori(1, RH) as i:
                load_ret(i, range(12))

            def load_out(name, w, r0=0):
                with e.Fori(0, KT // 2) as i:
                    for j in range(4):
                        c = U[name] + j
                        k0 = r0 + 8 * (j % 2)
                        load(c + i * 4, c, i, rows(w, k0, k0 + 8, (i * 2 + j // 2) * P))

            load_out("ret_out", ins["ret_w_out"][0])

            w1 = ins["att_w_in"][0]
            with e.Fori(0, AH // 2) as i:
                for j in range(8):
                    c = U["att"] + j
                    load(c + i * 8, c, i, rows(w1, 0, KT, (j // 2) * AH * AD + (i * 2 + j % 2) * AD))
            load_out("att_out", ins["att_w_out"][0])
            wm = ins["w_in_2"][0]

            def load_mix(j, c0):
                load(U["mix"] + j, U["mix"] + j, 0, wm[:, c0:c0 + P].rearrange("(k p) n -> p k n", p=P))

            for j, c0 in enumerate((2764, 2508, 2892, 2636, 2440, 2056, 2056 + P, 2312)):
                load_mix(j, c0)
            for j in range(16):
                load_mix(8 + j, j * P)

            def load_flat(name, w, k1, turns):
                with e.Fori(0, turns) as i:
                    for j in range(4):
                        c = U[name] + j
                        load(c + i * 4, c, i, rows(w, 0, k1, (i * 4 + j) * P), k1=k1)

            load_flat("mix_out", ins["w_out_2"][0], KT, 2)
            load_flat("xa_q", ins["xa_wq_2"][0], KT, 1)
            load_flat("xa_kv", ins["xa_wkv_2"][0], KT, 2)
            load_flat("xa_out", ins["xa_wo_2"][0], 4, 2)
            for half in range(2):
                w = ins["mlp_w1_2"][0][:, half * 2048:(half + 1) * 2048]
                load_flat(f"mlp_in{half}", w, KT, 4)
                load_out(f"mlp_out{half}", ins["mlp_w2_2"][0], 16 * half)
            e.wait_ge(*AC.at("out_copied"))
            e.dma_start(out.rearrange("b (t p) d -> p (b t) d", p=P), x_tok[:, :, :]).then_inc(out_done, 16)
            e.wait_ge(out_done, 16)

        @block.gpsimd
        def _(e):
            def split(s, turn):
                u = turn * RING + s
                e.wait_ge(raw_full[s], turn * 16 + 16)
                if not isinstance(turn, int):
                    e.wait_ge(unit_used, u - RING + 1)
                    e.sem_inc(slot_free, 1)
                e.tensor_scalar(wh[:, s, :, :], raw[:, s, :, :], 1.0, 1.0, ALU.mult, ALU.mult).then_inc(high_done, 1)
                e.wait_ge(high_done, u + 1)
                e.tensor_tensor(wl[:, s, :, :], raw[:, s, :, :], wh[:, s, :, :].bitcast(F32), ALU.subtract)\
                 .then_inc(split_done, 1)

            for s in range(RING):
                split(s, 0)
            with e.Fori(1, total_units // RING) as i:
                for s in range(RING):
                    split(s, i)

        @block.scalar
        def _(e):
            count_from(e, AC)
            e.dma_start(small[:, :], ins["small"]).then_inc(small_in, 16)
            e.dma_start(const[:, :], ins["const"]).then_inc(const_in, 16)
            e.dma_start(x_tok[:, :, :], ins["x"].rearrange("b (t p) d -> p (b t) d", p=P)).then_inc(x_in, 16)
            e.dma_start(pos[:, :], ins["positions"].to_broadcast([P, S])).then_inc(pos_in, 16)
            e.dma_start(dec[:, :], ins["decay"][0]).then_inc(decay_in, 16)
            e.wait_ge(small_in, 16)
            e.activation(cond[:, 1, :], sm("c"), ACT.Tanh, scale=0.5).then_inc(*AC.done("cond_tanh"))
            for k in range(KT):
                e.wait_ge(*PE.at(f"x{k}"))
                e.activation(xT[:, k, :], ob[k % 2][:, :], ACT.Copy).then_inc(*AC.done(f"x{k}"))
            e.wait_ge(*V.at("angles"))
            e.activation(sin_[:, :], ang[:, :], ACT.Sin).then_inc(*AC.done())
            e.activation(cos_[:, :], tmp[:, 1, :], ACT.Sin).then_inc(*AC.done("rope"))
            norm_scalar(e, "n0", lambda k: mod[:, 0, 0, k:k + 1], lambda k: AC.at(f"x{k}"))

            with e.Fori(0, RH) as i:
                AC.enter("ret_scalar", i)
                c = U["ret"] + i * 12
                e.wait_ge(*V.at("r_yl3", i - 1))
                for j, dst in enumerate((q_[:, 0, :], q_[:, 1, :], k_[:, 0, :], k_[:, 1, :])):
                    e.wait_ge(unit_used, c + j + 1)
                    e.activation(dst, acc[j % 2][:, :], ACT.Copy).then_inc(*AC.done(f"r_qk{j}"))
                for n in range(2):
                    for b in range(2):
                        if b == 0:
                            e.wait_ge(*PE.at(f"r_v{n}", i))
                        else:
                            e.wait_ge(unit_used, c + 6 + 2 * n)
                        e.activation(v_[:, 2 * b:2 * b + 2, n * 256:(n + 1) * 256],
                                     acc[b][:, :].rearrange("p (t n) -> p t n", t=2), ACT.Copy)\
                         .then_inc(*AC.done(f"r_v{n}{b}"))

                def gate(n):
                    e.wait_ge(unit_used, c + 9 + n)
                    e.activation(s_[:, n, :], acc[n % 2][:, :], ACT.Tanh, scale=0.5).then_inc(*AC.done(f"r_th{n}"))

                gate(0)
                gate(1)
                for n in range(4):
                    e.wait_ge(*PE.at(f"r_o{n}", i))
                    if n >= 2:
                        e.wait_ge(*PE.at(f"r_cols{n - 2}", i))
                    e.activation(sq[:, n % 2, :], ob[n % 2][:, :], ACT.Square).then_inc(*AC.done(f"r_sq{n}"))
                    e.activation(o_[n], ob[n % 2][:, :], ACT.Copy).then_inc(*AC.done(f"r_oc{n}"))
                gate(2)
                gate(3)
                for n in range(4):
                    e.wait_ge(*V.at(f"r_y{n}", i))
                    e.activation(Yh[:, bass.ds(i * 4 + n, 1), :], o_[n].unsqueeze(1), ACT.Copy)\
                     .then_inc(*AC.done(f"r_yh{n}"))
                e.wait_ge(*V.at("r_s3", i))
                e.dma_start(dec[:, :], ins["decay"][bass.ds(i + 1, 1)].rearrange("o p n -> (o p) n"))\
                 .then_inc(decay_in, 16)
                AC.leave(RH)

            e.wait_ge(*V.after("r_yl3", RH))
            e.wait_ge(decay_in, 16 * (RH + 1))
            with e.Fori(0, KT // 2) as i:
                for b in range(2):
                    e.wait_ge(*V.at(f"ada1sum{b}", i - 1))
                    e.dma_start(ada_w1[:, b, :], ins["ada_w"][1, bass.ds((i * 2 + b) * P, P), :])\
                     .then_inc(ada1_in[b], 16)
            norm_scalar(e, "n1", lambda k: mod[:, 1, 0, k:k + 1], lambda k: V.after("ret_outx1", KT // 2))

            def load_bias(h, head):
                for p0, p1, m in ((0, CHUNK, S - CHUNK), (CHUNK, P, S)):
                    e.dma_start(ab[p0:p1, h, 0:m],
                                ins["bias"][bass.ds(head, 1), p0:p1, 0:m].rearrange("o p n -> (o p) n"))\
                     .then_inc(bias_in[h], 16)

            def att_qk(i, t, prev):
                c = U["att"] + i * 8
                for j in range(4):
                    dst = (aq, ak)[j // 2][:, j % 2, :]
                    e.wait_ge(unit_used, c + j + 1)
                    if j >= 2:
                        e.wait_ge(*PE.at(f"{t}cols{j - 2}", i))
                    e.activation(sq[:, j % 2, :], acc[j % 2][:, :], ACT.Square).then_inc(*AC.done(f"{t}sq{j}"))
                    e.activation(dst, acc[j % 2][:, :], ACT.Copy,
                                 scale=(qk_gain[:, 0:1] if j < 2 else 1.0)).then_inc(*AC.done(f"{t}qk{j}"))

            def att_vg(i, t):
                c = U["att"] + i * 8
                for b in range(2):
                    e.wait_ge(*(PE.at(f"{t}v", i) if b == 0 else (unit_used, c + 6)))
                    e.activation(av[:, 2 * b:2 * b + 2, :], acc[b][:, :].rearrange("p (t n) -> p t n", t=2),
                                 ACT.Copy).then_inc(*AC.done(f"{t}v{b}"))
                for h in range(2):
                    e.wait_ge(unit_used, c + 7 + h)
                    e.activation(ag[:, h, :], acc[h][:, :], ACT.Tanh, scale=0.5).then_inc(*AC.done(f"{t}th{h}"))
                for h in range(2):
                    e.wait_ge(*V.at(f"{t}nm{h}", i))
                    for n in range(NT):
                        x = aS[:, h, QOFF[n]:QOFF[n] + (n + 1) * P]
                        r = h * 4 + n
                        e.activation(x, x, ACT.Exp, bias=amax[:, 0, r:r + 1], accum_out=amax[:, 1, r:r + 1])\
                         .then_inc(*AC.done(f"{t}exp{h}{n}"))
                    load_bias(h, i * 2 + 2 + h)

            def att_pv(pair, i, t, w):
                for h in range(2):
                    for n in range(NT):
                        e.wait_ge(*PE.at(f"{t}pt{h}{n}", i))
                        e.activation(aP[:, h, KOFF[n]:KOFF[n] + (NT - n) * P], sc[n % 2][:, 0:(NT - n) * P],
                                     ACT.Copy).then_inc(*AC.done(f"{t}pt{h}{n}"))
                for h in range(2):
                    e.wait_ge(*V.at(f"{t}y{h}", i))
                    e.activation(Yh[:, bass.ds(pair * 2 + h, 1), :], ay[:, h, :].unsqueeze(1), ACT.Copy)\
                     .then_inc(*AC.done(f"{t}yh{h}"))

            e.wait_ge(*V.at("n1t0"))
            e.wait_ge(*V.at("mask"))
            for h in range(2):
                load_bias(h, h)
            att_qk(0, "p", None)
            att_vg(0, "p")
            with e.Fori(1, AH // 2) as i:
                AC.enter("att_scalar", i, 1)
                att_qk(i, "a", None)
                att_pv(i - 1, i, "a", None)
                att_vg(i, "a")
                AC.leave(AH // 2 - 1)
            att_pv(AH // 2 - 1, 0, "z", None)
            for h in range(2):
                e.wait_ge(bias_in[h], 32 * (AH // 2 + 1))
            norm_scalar(e, "nm", None, lambda k: V.after("att_outx1", KT // 2))

            e.dma_start(wqb[:, :, :], ins["dsa_w_qb_2"][0].rearrange("(k p) n -> p k n", p=P)).then_inc(dsa_w_in, 16)
            e.dma_start(wqi[:, :, :], ins["dsa_w_qi_2"][0].rearrange("(k p) n -> p k n", p=P)).then_inc(dsa_w_in, 16)
            for a, b in ((0, 0), (DD, 0), (2 * DD, DD)):
                e.dma_start(wkvb[:, a:a + DD], ins["dsa_w_kvb_2"][0][:, b:b + DD]).then_inc(dsa_w_in, 16)
            e.dma_start(glev[:, :, :], ins["levels"].rearrange("p (l n) -> p l n", l=LEVELS)).then_inc(levels_in, 16)
            e.dma_start(wab[:, :, :], ins["w_in_2"][0][:, 2048:2056].rearrange("(k p) n -> p k n", p=P))\
             .then_inc(wab_in, 16)
            for j in range(2):
                e.wait_ge(unit_used, U["mix"] + 2 * j + 1)
                e.activation(cg[:, j, :], acc[0][:, :], ACT.Tanh, scale=0.5).then_inc(*AC.done(f"c_th{j}"))
            for j in range(2):
                if j == 0:
                    e.wait_ge(*V.at("c_centered"))
                e.activation(sq[:, j, :], co[:, j, :], ACT.Square).then_inc(*AC.done(f"c_sq{j}"))
            for j in range(2):
                e.wait_ge(*V.at(f"c_t{j}"))
                step(e, e.activation(co[:, j, :], co[:, j, :], ACT.Identity, bias=sm("conv_ln_b", j, 1)), AC)
                e.activation(cg[:, j, :], co[:, j, :], ACT.Tanh, scale=0.5).then_inc(*AC.done(f"c_sth{j}"))
            for j in range(2):
                e.wait_ge(*V.at(f"c_y{j}"))
                e.activation(Mh[:, 6 + j, :], co[:, j, :], ACT.Copy, scale=0.5).then_inc(*AC.done(f"c_hi{j}"))

            e.wait_ge(unit_used, U["mix"] + 5)
            e.activation(kidx[0:DD, :], acc[0][0:DD, :], ACT.Copy).then_inc(*AC.done("d_kidx"))
            e.wait_ge(*AC.at("d_kidx"))
            e.dma_start(kidx[DD:P, :], kidx[0:DD, :]).then_inc(kidx_in, 16)
            e.wait_ge(*PE.at("d_small"))
            e.activation(tc[:, :, :], acc[1][:, 0:12 * NT].rearrange("p (t n) -> p t n", t=NT), ACT.Copy)\
             .then_inc(*AC.done("tc"))
            for j, dst in enumerate((cq[:, 0, :], cq[:, 1, :], ckv[:, :])):
                e.wait_ge(unit_used, U["mix"] + 6 + j)
                e.activation(dst, acc[j % 2][:, :], ACT.Copy).then_inc(*AC.done(f"d_c{j}"))
            for j in range(2):
                e.wait_ge(*PE.at(f"d_q{j}"))
                e.activation(sq[:, j, :], ob[j][:, :], ACT.Square).then_inc(*AC.done(f"d_sq{j}"))
                e.activation(dq[:, j, :], ob[j][:, :], ACT.Copy, scale=qk_gain[:, 1:2]).then_inc(*AC.done(f"d_qc{j}"))
            e.wait_ge(*PE.at("d_k"))
            e.wait_ge(*PE.at("d_cols0"))
            e.activation(sq[:, 0, :], sc[0][:, :], ACT.Square).then_inc(*AC.done("d_sq2"))
            e.activation(dk[:, :], sc[0][:, :], ACT.Copy).then_inc(*AC.done("d_kc"))
            e.wait_ge(*PE.at("d_v"))
            e.activation(dv[:, :, :], sc[1][:, 0:NT * DD].rearrange("p (t n) -> p t n", t=NT), ACT.Copy)\
             .then_inc(*AC.done("d_vc"))
            for j in range(2):
                e.wait_ge(*PE.at(f"d_qi{j}"))
                e.activation(dqi[:, j, :], ob[j][:, :], ACT.Copy).then_inc(*AC.done(f"d_qic{j}"))
            for t in range(1, NT):
                for h in range(DH):
                    n = (t - 1) * DH + h
                    w_ = (t + 1) * P
                    e.wait_ge(*PE.at(f"d_idx{n}"))
                    if n >= 2:
                        e.wait_ge(*V.at(f"d_sum{n - 2}"))
                    e.activation(drelu[:, n % 2, 0:w_], sc[n % 2][:, 0:w_], ACT.Relu).then_inc(*AC.done(f"d_relu{n}"))
            for g in range(2):
                for h in range(2):
                    for n in range(NT):
                        r = h * 4 + n
                        x = dS[:, h, QOFF[n]:QOFF[n] + (n + 1) * P]
                        e.wait_ge(*V.at(f"d_nm{g}{h}"))
                        e.activation(x, x, ACT.Exp, bias=amax[:, 0, r:r + 1], accum_out=amax[:, 1, r:r + 1])\
                         .then_inc(*AC.done(f"d_exp{g}{h}{n}"))
                for h in range(2):
                    for n in range(NT):
                        e.wait_ge(*PE.at(f"d_pt{g}{h}{n}"))
                        e.activation(dP[:, h, KOFF[n]:KOFF[n] + (NT - n) * P], sc[n % 2][:, 0:(NT - n) * P],
                                     ACT.Copy).then_inc(*AC.done(f"d_ptc{g}{h}{n}"))
                e.wait_ge(*PE.at(f"d_o{g}"))
                e.activation(Mh[:, 4 + g, :], ob[g][:, :], ACT.Copy).then_inc(*AC.done(f"d_hi{g}"))

            def gdn_silu(e, j):
                e.wait_ge(*V.at(f"g_conv{j}"))
                if j >= 2:
                    e.wait_ge(*V.at(f"g_silu{j - 2}"))
                e.activation(gth[:, j % 2, :], gqkv[:, j, :], ACT.Tanh, scale=0.5).then_inc(*AC.done(f"g_th{j}"))

            e.activation(gc[:, 0, 0:GH], sm("gdn_a_log"), ACT.Exp).then_inc(*AC.done("g_ea"))
            e.wait_ge(*V.at("g_abs"))
            e.activation(gc[:, 2, :], gc[:, 2, :], ACT.Exp, scale=-1.0).then_inc(*AC.done("g_ex"))
            e.wait_ge(*AC.at("tc"))
            e.activation(gc[:, 3, :].rearrange("p (t h) -> p t h", t=NT), tc[:, :, 8:12], ACT.Tanh, scale=0.5)\
             .then_inc(*AC.done("g_bth"))
            e.wait_ge(*V.at("g_1p"))
            e.activation(gc[:, 2, :], gc[:, 2, :], ACT.Ln).then_inc(*AC.done("g_ln"))
            for j in range(12):
                b = j % 2
                e.wait_ge(unit_used, U["mix"] + 9 + j)
                if j >= 2:
                    e.wait_ge(*V.at(f"g_conv{j - 2}"))
                e.activation(gpre[:, b, GDN_TAPS - 1:], acc[b][:, :], ACT.Copy).then_inc(*AC.done(f"g_pre{j}"))
                if j >= 1:
                    gdn_silu(e, j - 1)
            gdn_silu(e, 11)
            for j in range(4):
                e.wait_ge(unit_used, U["mix"] + 21 + j)
                e.activation(gz[:, j, :], acc[j % 2][:, :], ACT.Tanh, scale=0.5).then_inc(*AC.done(f"g_zth{j}"))
            for j in range(8):
                e.wait_ge(*V.at(f"g_silu{j}"))
                if j >= 2:
                    e.wait_ge(*PE.at(f"g_cols{j - 2}"))
                e.activation(sq[:, j % 2, :], gqkv[:, j, :], ACT.Square).then_inc(*AC.done(f"g_sq{j}"))
            e.wait_ge(*PE.at("g_dl"))
            e.activation(gc[:, 6, :], st[:, 0:16], ACT.Copy).then_inc(*AC.done("g_d"))
            e.activation(gc[:, 7, :], st[:, 0:16], ACT.Exp).then_inc(*AC.done("g_ed"))
            e.activation(gc[:, 9, :], st[:, 16:32], ACT.Exp).then_inc(*AC.done("g_el"))
            e.wait_ge(*V.at("g_dld"))
            e.activation(gc[:, 8, :], gc[:, 8, :], ACT.Exp).then_inc(*AC.done("g_kd"))
            for t in range(NT):
                for a, (name, dst) in enumerate((("k", gktok), ("v", gvtok))):
                    e.wait_ge(*PE.at(f"g_{name}tok{t}"))
                    e.activation(dst[:, t, :, :], sc[a][:, :].rearrange("p (h n) -> p h n", h=GH), ACT.Copy)\
                     .then_inc(*AC.done(f"g_{name}tokc{t}"))
            for t in range(NT):
                e.wait_ge(*V.at(f"g_diff{t}"))
                e.activation(gG[:, :, :], gG[:, :, :], ACT.Exp).then_inc(*AC.done(f"g_G{t}"))
                e.activation(ggb[:, :, :], ob[0][:, :].rearrange("p (h n) -> p h n", h=GH), ACT.Exp)\
                 .then_inc(*AC.done(f"g_eD{t}"))
                e.wait_ge(*PE.at(f"g_AT{t}"))
                e.activation(gAT[:, t, :, :], acc[0][:, :].rearrange("p (h n) -> p h n", h=GH), ACT.Copy)\
                 .then_inc(*AC.done(f"g_ATc{t}"))
                e.wait_ge(*PE.at(f"g_QKT{t}"))
                e.activation(gQKT[:, t, :, :], acc[1][:, :].rearrange("p (h n) -> p h n", h=GH), ACT.Copy)\
                 .then_inc(*AC.done(f"g_QKTc{t}"))
            for t in range(NT):
                e.wait_ge(*PE.at(f"g_T0{t}"))
                e.activation(gT[:, t, :, :], sc[t % 2][:, :].rearrange("p (h n) -> p h n", h=GH), ACT.Copy)\
                 .then_inc(*AC.done(f"g_Tc{t}"))
            for l in range(1, LEVELS):
                for t in range(NT):
                    e.wait_ge(*PE.at(f"g_X{l}{t}"))
                    e.activation(gX[:, t % 2, :, :], sc[t % 2][:, :].rearrange("p (h n) -> p h n", h=GH), ACT.Copy)\
                     .then_inc(*AC.done(f"g_Xc{l}{t}"))
            for t in range(NT):
                e.wait_ge(*PE.at(f"g_w{t}"))
                e.activation(gwT[:, t, :, :], acc[t % 2][:, :].rearrange("p (h n) -> p h n", h=GH), ACT.Copy,
                             scale=-1.0).then_inc(*AC.done(f"g_wc{t}"))
            for t in range(NT):
                e.wait_ge(*PE.at(f"g_vn{t}"))
                e.activation(gvn[:, t % 2, :, :], ob[t % 2][:, :].rearrange("p (h n) -> p h n", h=GH), ACT.Copy)\
                 .then_inc(*AC.done(f"g_vnc{t}"))
                e.wait_ge(*PE.at(f"g_o{t}"))
                e.activation(goT[:, :, t * P:(t + 1) * P], sc[t % 2][:, :].rearrange("p (h n) -> p h n", h=GH),
                             ACT.Copy).then_inc(*AC.done(f"g_oc{t}"))
            e.wait_ge(*AC.last())
            for h in range(GH):
                if h >= 2:
                    e.wait_ge(*PE.at(f"g_ocols{h - 2}"))
                e.activation(sq[:, h % 2, :], goT[:, h, :], ACT.Square).then_inc(*AC.done(f"g_osq{h}"))
            for h in range(GH):
                e.wait_ge(*V.at(f"g_y{h}"))
                e.activation(Mh[:, h, :], goT[:, h, :], ACT.Copy).then_inc(*AC.done(f"g_hi{h}"))

            e.wait_ge(*V.at(f"g_lo{GH - 1}"))
            e.dma_start(m_tok[:, :, :], ins["mem_2"].rearrange("b (t p) d -> p (b t) d", p=P)).then_inc(mem_in, 16)
            for k in range(KT):
                e.wait_ge(*PE.at(f"m{k}"))
                e.activation(mT[:, k, :], ob[k % 2][:, 0:MEM], ACT.Copy).then_inc(*AC.done(f"m{k}"))
            norm_scalar(e, "nk", None, lambda k: AC.at(f"m{k}"), mT, mh, MEM)
            e.wait_ge(*V.at(f"nkh{KT - 1}"))
            norm_scalar(e, "nx", None, lambda k: V.after("mix_outx3", 2))
            for h in range(XH):
                e.wait_ge(unit_used, U["xa_q"] + 1 + h)
                if h >= 2:
                    e.wait_ge(*PE.at(f"x_cols{h - 2}"))
                e.activation(sq[:, h % 2, :], acc[h % 2][:, :], ACT.Square).then_inc(*AC.done(f"x_sq{h}"))
                e.activation(xq[:, h, :], acc[h % 2][:, :], ACT.Copy, scale=qk_gain[:, 2:3]).then_inc(*AC.done(f"x_q{h}"))
            for h in range(XH):
                e.wait_ge(unit_used, U["xa_kv"] + 1 + h)
                e.wait_ge(*PE.at(f"x_cols{h + 2}"))
                e.activation(sq[:, h % 2, 0:MEM], acc[h % 2][:, 0:MEM], ACT.Square).then_inc(*AC.done(f"x_sq{h + 4}"))
                e.activation(xk[:, h, :], acc[h % 2][:, 0:MEM], ACT.Copy).then_inc(*AC.done(f"x_k{h}"))
            for j in range(2):
                e.wait_ge(unit_used, U["xa_kv"] + 6 + 2 * j)
                e.activation(xv[:, :, j * 256:(j + 1) * 256], acc[0][:, :].rearrange("p (t n) -> p t n", t=2),
                             ACT.Copy).then_inc(*AC.done(f"x_v{j}"))
            for h in range(XH):
                e.wait_ge(*V.at(f"x_nm{h}"))
                for t in range(NT):
                    e.activation(xS[:, h % 2, t, :], xS[:, h % 2, t, :], ACT.Exp, bias=amax[:, 0, 4 * h + t:4 * h + t + 1],
                                 accum_out=amax[:, 1, 4 * h + t:4 * h + t + 1]).then_inc(*AC.done(f"x_exp{h}{t}"))
                for n in range(2):
                    e.wait_ge(*PE.at(f"x_pt{h}{n}"))
                    e.activation(xP[:, h % 2, n, :], bankx[n][:, :], ACT.Copy).then_inc(*AC.done(f"x_ptc{h}{n}"))
                e.wait_ge(*PE.at(f"x_o{h}"))
                e.activation(Mh[:, h, :], ob[h % 2][:, :], ACT.Copy).then_inc(*AC.done(f"x_hi{h}"))

            norm_scalar(e, "nf", None, lambda k: V.after("xa_outx3", 2))
            for half in range(2):
                if half:
                    e.wait_ge(unit_used, U["mlp_out0"] + 16)
                with e.Fori(0, 4) as i:
                    AC.enter(f"mlp{half}_scalar", i)
                    for j in range(4):
                        b = j % 2
                        e.wait_ge(unit_used, U[f"mlp_in{half}"] + j + 1 + i * 4)
                        e.wait_ge(*(V.at(f"f{half}yl{j + 2}", i - 1) if j < 2 else V.at(f"f{half}yl{j - 2}", i)))
                        e.activation(sq[:, b, :], acc[b][:, :], ACT.Relu).then_inc(*AC.done(f"f{half}r{j}"))
                        e.wait_ge(*V.at(f"f{half}y{j}", i))
                        e.activation(Yh[:, bass.ds(i * 4 + j, 1), :], sq[:, b, :].unsqueeze(1), ACT.Copy)\
                         .then_inc(*AC.done(f"f{half}yh{j}"))
                    AC.leave(4)
            for k in range(KT):
                e.wait_ge(*PE.at(f"out{k}"))
                e.activation(x_tok[:, :, k * P:(k + 1) * P], ob[k % 2][:, :].rearrange("p (t n) -> p t n", t=NT),
                             ACT.Copy).then_inc(*AC.done("out_copied" if k == KT - 1 else f"outc{k}"))

        @block.tensor
        def _(e):
            count_from(e, PE)
            e.wait_ge(const_in, 16)
            e.wait_ge(x_in, 16)
            for k in range(KT):
                if k >= 2:
                    e.wait_ge(*AC.at(f"x{k - 2}"))
                for t in range(NT):
                    last = e.transpose(ob[k % 2][:, t * P:(t + 1) * P], x_tok[:, t, k * P:(k + 1) * P], ident)
                last.then_inc(*PE.done(f"x{k}"))
            e.wait_ge(*V.at("ada0sum"))
            ada_columns(e, ada_acc0, 0, 16, "ada0cols")
            e.wait_ge(*V.at("mod0"))
            norm_tensor(e, "n0")

            e.wait_ge(*V.at(f"n0h{KT - 1}"))
            with e.Fori(0, RH) as i:
                PE.enter("ret_tensor", i)
                c = U["ret"] + i * 12
                for j in range(4):
                    e.wait_ge(*(V.at(f"r_g{j + 2}", i - 1) if j < 2 else AC.at(f"r_qk{j - 2}", i)))
                    feat(e, acc[j % 2], c + j, U["ret"] + j)
                tok(e, c + 4, U["ret"] + 4, "r_v0", [AC.at("r_qk2", i), AC.at("r_qk3", i)])
                tok(e, c + 6, U["ret"] + 6, "r_v1", [AC.at("r_v00", i), AC.at("r_v01", i)])
                e.wait_ge(*V.at("r_rope3", i))
                for n in range(NT):
                    if n >= 2:
                        e.wait_ge(*V.at(f"r_s{n - 2}", i))
                    for d in range(2):
                        last = e.matmul(sc[n % 2][:, 0:(NT - n) * P], k_[:, d, n * P:(n + 1) * P],
                                        q_[:, d, n * P:S], start=(d == 0), stop=(d == 1))
                    last.then_inc(*PE.done(f"r_sc{n}"))
                for n in range(2):
                    e.wait_ge(*AC.at(f"r_v1{n}", i))
                    feat(e, acc[n], c + 8 + n, U["ret"] + 8 + n)
                e.wait_ge(*V.at("r_s3", i))
                for n in range(4):
                    if n >= 2:
                        e.wait_ge(*AC.at(f"r_oc{n - 2}", i))
                    for t in range(NT):
                        last = e.matmul(ob[n % 2][:, t * P:S], v_[:, t, n * P:(n + 1) * P],
                                        t_[:, KOFF[t]:KOFF[t] + (NT - t) * P], start=(t == 0), stop=(t == NT - 1))
                    last.then_inc(*PE.done(f"r_o{n}"))
                    if n >= 1:
                        e.wait_ge(*AC.at(f"r_sq{n - 1}", i))
                        columns(e, sq[:, (n - 1) % 2, :], 0, "first" if n == 1 else False, False, f"r_cols{n - 1}")
                e.wait_ge(*V.at("r_g0", i))
                feat(e, acc[0], c + 10, U["ret"] + 10)
                e.wait_ge(*AC.at("r_sq3", i))
                columns(e, sq[:, 1, :], 0, False, "last", "r_cols3")
                e.wait_ge(*V.at("r_g1", i))
                feat(e, acc[1], c + 11, U["ret"] + 11)
                e.wait_ge(*V.at("r_diag", i))
                spread(e, "r_bc")
                PE.leave(RH)
            ada_columns(e, ada_accg, 16, 24, "ada0gate")
            out_tensor(e, "ret_out", V.after("r_yl3", RH))
            e.wait_ge(*V.after("ada1sum1", KT // 2))
            ada_columns(e, ada_acc1, 0, 24, "ada1cols")
            e.wait_ge(*V.at("mod1"))
            norm_tensor(e, "n1")

            def att_qk(i, t, free):
                c = U["att"] + i * 8
                for j in range(4):
                    e.wait_ge(*(free(j) if j < 2 else AC.at(f"{t}qk{j - 2}", i)))
                    feat(e, acc[j % 2], c + j, U["att"] + j)
                    if j >= 1:
                        e.wait_ge(*AC.at(f"{t}sq{j - 1}", i))
                        columns(e, sq[:, (j - 1) % 2, :], 4 * (j - 1), True, True, f"{t}cols{j - 1}")
                e.wait_ge(*AC.at(f"{t}sq3", i))
                columns(e, sq[:, 1, :], 12, True, True, f"{t}cols3")

            def att_vg(i, t):
                c = U["att"] + i * 8
                tok(e, c + 4, U["att"] + 4, f"{t}v", [AC.at(f"{t}qk2", i), AC.at(f"{t}qk3", i)])
                for h in range(2):
                    e.wait_ge(*V.at(f"{t}diag{h}", i))
                    spread(e, f"{t}bc{h}")
                    e.wait_ge(*AC.at(f"{t}v{h}", i))
                    feat(e, acc[h], c + 6 + h, U["att"] + 6 + h)
                for h in range(2):
                    e.wait_ge(*V.at(f"{t}k{h}", i))
                    for n in range(NT):
                        b = (h * NT + n) % 2
                        if h * NT + n >= 2:
                            r = h * NT + n - 2
                            e.wait_ge(*V.at(f"{t}s{r // NT}{r % NT}", i))
                        e.matmul(sc[b][:, 0:(n + 1) * P], aq[:, h, n * P:(n + 1) * P], ak[:, h, 0:(n + 1) * P],
                                 start=True, stop=True).then_inc(*PE.done(f"{t}sc{h}{n}"))

            def att_pv(i, t, ready):
                for h in range(2):
                    e.wait_ge(*ready(h))
                    for n in range(NT):
                        r = h * NT + n
                        if r >= 2:
                            e.wait_ge(*AC.at(f"{t}pt{(r - 2) // NT}{(r - 2) % NT}", i))
                        for m in range(n, NT):
                            last = e.transpose(sc[n % 2][:, (m - n) * P:(m - n + 1) * P],
                                               aS[:, h, QOFF[m] + n * P:QOFF[m] + (n + 1) * P], ident)
                        last.then_inc(*PE.done(f"{t}pt{h}{n}"))
                for h in range(2):
                    e.wait_ge(*AC.at(f"{t}pt{h}3", i))
                    for n in range(NT):
                        last = e.matmul(ob[h][:, n * P:S], av[:, n, h * P:(h + 1) * P],
                                        aP[:, h, KOFF[n]:KOFF[n] + (NT - n) * P], start=(n == 0), stop=(n == NT - 1))
                    last.then_inc(*PE.done(f"{t}o{h}"))

            e.wait_ge(*V.at(f"n1h{KT - 1}"))
            att_qk(0, "p", lambda j: V.at(f"n1h{KT - 1}"))
            att_vg(0, "p")
            with e.Fori(1, AH // 2) as i:
                PE.enter("att_tensor", i, 1)
                att_qk(i, "a", lambda j: V.at(f"ag{j}", i - 1))
                att_pv(i, "a", lambda h: V.at(f"anorm{h}", i - 1))
                att_vg(i, "a")
                PE.leave(AH // 2 - 1)
            att_pv(0, "z", lambda h: V.at(f"anorm{h}", AH // 2 - 1))
            out_tensor(e, "att_out", V.at("zyl1"))
            norm_tensor(e, "nm")
            e.wait_ge(*V.at(f"nmh{KT - 1}"))

            for j in range(4):
                if j >= 2:
                    e.wait_ge(*V.at(f"c_in{0}"))
                feat(e, acc[j % 2], U["mix"] + j, U["mix"] + j)
            e.wait_ge(*V.at("c_conv"))
            for j in range(2):
                columns(e, co[:, j, :], 0, "first" if j == 0 else False, "last" if j == 1 else False, f"c_cols{j}")
            e.wait_ge(*V.at("c_mean"))
            spread(e, "c_mbc")
            for j in range(2):
                e.wait_ge(*AC.at(f"c_sq{j}"))
                columns(e, sq[:, j, :], 0, "first" if j == 0 else False, "last" if j == 1 else False, f"c_vcols{j}")
            e.wait_ge(*V.at("c_diag"))
            spread(e, "c_bc")

            u = U["mix"] + 4
            s = u % RING
            e.wait_ge(*V.at("c_in1"))
            e.wait_ge(*V.at("wab"))
            e.wait_ge(split_done, u + 1)
            for t in range(NT):
                for o, high, low in ((acc[1][:, 12 * t:12 * t + 4], lambda k: wh[:, s, k, DD:DD + 4],
                                      lambda k: wl[:, s, k, DD:DD + 4]),
                                     (acc[1][:, 12 * t + 4:12 * t + 12], lambda k: wab_high[:, k, :],
                                      lambda k: wab_low[:, k, :])):
                    for k in range(KT):
                        a, b = hh[:, k, t * P:(t + 1) * P], hl[:, k, t * P:(t + 1) * P]
                        e.matmul(o, a, high(k), start=(k == 0), stop=False)
                        e.matmul(o, a, low(k), start=False, stop=False)
                        last = e.matmul(o, b, high(k), start=False, stop=(k == KT - 1))
            last.then_inc(*PE.done("d_small"))
            feat(e, acc[0], u, u)
            for j in range(3):
                e.wait_ge(*(AC.at("d_kidx"), AC.at("tc"), AC.at("d_c0"))[j])
                feat(e, acc[j % 2], u + 1 + j, u + 1 + j)
            e.wait_ge(dsa_w_in, 80)
            e.wait_ge(*AC.at("d_c1"))
            for j in range(2):
                for k in range(2):
                    last = e.matmul(ob[j][:, :], wqb[:, k, j * P:(j + 1) * P], cq[:, k, :], start=(k == 0), stop=(k == 1))
                last.then_inc(*PE.done(f"d_q{j}"))
            e.wait_ge(*AC.at("d_c2"))
            e.matmul(sc[0][:, :], wkvb[:, 0:P], ckv[:, :], start=True, stop=True).then_inc(*PE.done("d_k"))
            for t in range(NT):
                last = e.matmul(sc[1][:, t * DD:(t + 1) * DD], ckv[:, t * P:(t + 1) * P], wkvb[:, P:P + DD],
                                start=True, stop=True)
            last.then_inc(*PE.done("d_v"))
            for j in range(2):
                e.wait_ge(*AC.at(f"d_sq{j}"))
                for t in range(NT):
                    last = e.matmul(st[:, 8 * j + 2 * t:8 * j + 2 * t + 2], sq[:, j, t * P:(t + 1) * P], cst("halves"),
                                    start=True, stop=True)
                last.then_inc(*PE.done(f"d_cols{j}"))
            for j in range(2):
                e.wait_ge(*AC.at(f"d_qc{j}"))
                for k in range(2):
                    last = e.matmul(ob[j][:, :], wqi[:, k, j * P:(j + 1) * P], cq[:, k, :], start=(k == 0), stop=(k == 1))
                last.then_inc(*PE.done(f"d_qi{j}"))
            e.wait_ge(*AC.at("d_sq2"))
            columns(e, sq[:, 0, :], 16, True, True, "d_cols2", of=cst("halves"))
            e.wait_ge(*V.at("d_diag"))
            spread(e, "d_bc")
            e.wait_ge(*AC.at("d_qic1"))
            e.wait_ge(*AC.at("d_vc"))
            e.wait_ge(kidx_in, 16)
            for t in range(1, NT):
                for h in range(DH):
                    n = (t - 1) * DH + h
                    r0 = (h % 2) * DD
                    if n >= 2:
                        e.wait_ge(*AC.at(f"d_relu{n - 2}"))
                    e.matmul(sc[n % 2][:, 0:(t + 1) * P], dqi[r0:r0 + DD, h // 2, t * P:(t + 1) * P],
                             kidx[r0:r0 + DD, 0:(t + 1) * P], start=True, stop=True).then_inc(*PE.done(f"d_idx{n}"))
            e.wait_ge(*V.at("d_kn"))
            e.wait_ge(*AC.at("d_relu11"))
            for g in range(2):
                for h in range(2):
                    r0 = h * DD
                    for n in range(NT):
                        r = h * NT + n
                        if r >= 2:
                            e.wait_ge(*V.at(f"d_s{g}{r - 2}"))
                        elif g:
                            e.wait_ge(*AC.at(f"d_ptc01{n + 2}"))
                        e.matmul(sc[r % 2][:, 0:(n + 1) * P], dq[r0:r0 + DD, g, n * P:(n + 1) * P],
                                 dk[r0:r0 + DD, 0:(n + 1) * P], start=True, stop=True).then_inc(*PE.done(f"d_sc{g}{r}"))
                for h in range(2):
                    e.wait_ge(*V.at(f"d_norm{g}{h}"))
                    for n in range(NT):
                        r = h * NT + n
                        if r >= 2:
                            e.wait_ge(*AC.at(f"d_ptc{g}{(r - 2) // NT}{(r - 2) % NT}"))
                        for m in range(n, NT):
                            last = e.transpose(sc[n % 2][:, (m - n) * P:(m - n + 1) * P],
                                               dS[:, h, QOFF[m] + n * P:QOFF[m] + (n + 1) * P], ident)
                        last.then_inc(*PE.done(f"d_pt{g}{h}{n}"))
                for h in range(2):
                    e.wait_ge(*AC.at(f"d_ptc{g}{h}3"))
                    for n in range(NT):
                        last = e.matmul(ob[g][h * DD:(h + 1) * DD, n * P:S], dv[:, n, :],
                                        dP[:, h, KOFF[n]:KOFF[n] + (NT - n) * P], start=(n == 0), stop=(n == NT - 1))
                last.then_inc(*PE.done(f"d_o{g}"))

            for j in range(12):
                u = U["mix"] + 8 + j
                e.wait_ge(*(AC.at(f"g_pre{j - 2}") if j >= 2 else AC.at(f"d_c{2 - j}")))
                feat(e, acc[j % 2], u, u)
            for j in range(4):
                u = U["mix"] + 20 + j
                e.wait_ge(*(V.at(f"g_z{j - 2}") if j >= 2 else AC.at(f"g_pre{10 + j}")))
                feat(e, acc[j % 2], u, u)
            for j in range(8):
                e.wait_ge(*AC.at(f"g_sq{j}"))
                columns(e, sq[:, j % 2, :], 4 * j, True, True, f"g_cols{j}")
            for j in range(8):
                e.wait_ge(*V.at(f"g_diag{j}"))
                spread(e, f"g_bc{j}")
            e.wait_ge(*V.at("g_g"))
            e.matmul(st[:, 0:16], cst("cumsum"), gc[:, 5, :], start=True, stop=True)
            e.matmul(st[:, 16:32], ones[:, :], gc[:, 5, :], start=True, stop=True).then_inc(*PE.done("g_dl"))
            e.wait_ge(*V.at("g_n7"))
            e.wait_ge(*V.at("g_silu11"))
            for t in range(NT):
                for a, name in enumerate("kv"):
                    if t:
                        e.wait_ge(*AC.at(f"g_{name}tokc{t - 1}"))
                    for h in range(GH):
                        last = e.transpose(sc[a][:, h * P:(h + 1) * P], gqkv[:, 4 + 4 * a + h, t * P:(t + 1) * P], ident)
                    last.then_inc(*PE.done(f"g_{name}tok{t}"))
            for t in range(NT):
                e.wait_ge(*V.at(f"g_gb{t}"))
                if t:
                    e.wait_ge(*AC.at(f"g_eD{t - 1}"))
                for h in range(GH):
                    last = e.matmul(ob[0][:, h * P:(h + 1) * P], ggb[:, h, :], cst("cumsum"), start=True, stop=True)
                last.then_inc(*PE.done(f"g_D{t}"))
                e.wait_ge(*(V.at(f"g_QK{t - 1}") if t else AC.at("g_vtokc3")))
                for h in range(GH):
                    k = gqkv[:, 4 + h, t * P:(t + 1) * P]
                    last = e.matmul(sc[0][:, h * P:(h + 1) * P], k, k, start=True, stop=True)
                last.then_inc(*PE.done(f"g_kk{t}"))
                for h in range(GH):
                    last = e.matmul(sc[1][:, h * P:(h + 1) * P], gqkv[:, h, t * P:(t + 1) * P],
                                    gqkv[:, 4 + h, t * P:(t + 1) * P], start=True, stop=True)
                last.then_inc(*PE.done(f"g_qk{t}"))
                e.wait_ge(*V.at(f"g_A{t}"))
                if t:
                    e.wait_ge(*AC.at(f"g_ATc{t - 1}"))
                for h in range(GH):
                    last = e.transpose(acc[0][:, h * P:(h + 1) * P], gA[:, h, :], ident)
                last.then_inc(*PE.done(f"g_AT{t}"))
                e.wait_ge(*V.at(f"g_QK{t}"))
                if t:
                    e.wait_ge(*AC.at(f"g_QKTc{t - 1}"))
                for h in range(GH):
                    last = e.transpose(acc[1][:, h * P:(h + 1) * P], gQK[:, h, :], ident)
                last.then_inc(*PE.done(f"g_QKT{t}"))
            for t in range(NT):
                e.wait_ge(*V.at(f"g_TT0{t}"))
                if t >= 2:
                    e.wait_ge(*AC.at(f"g_Tc{t - 2}"))
                for h in range(GH):
                    last = e.transpose(sc[t % 2][:, h * P:(h + 1) * P], gTT[:, t, h, :], ident)
                last.then_inc(*PE.done(f"g_T0{t}"))
            for l in range(1, LEVELS):
                def inverse(t):
                    if t < 2 and l > 1:
                        e.wait_ge(*V.at(f"g_TT{l - 1}{t + 2}"))
                    e.wait_ge(*AC.at(f"g_Xc{l}{t}"))
                    if l < LEVELS - 1:
                        for h in range(GH):
                            last = e.matmul(ob[t % 2][:, h * P:(h + 1) * P], gTT[:, t, h, :], gX[:, t % 2, h, :],
                                            start=True, stop=True)
                        last.then_inc(*PE.done(f"g_P{l}{t}"))
                    for h in range(GH):
                        last = e.matmul(acc[t % 2][:, h * P:(h + 1) * P], gX[:, t % 2, h, :], gTT[:, t, h, :],
                                        start=True, stop=True)
                    last.then_inc(*PE.done(f"g_R{l}{t}"))

                for t in range(NT):
                    e.wait_ge(*V.at(f"g_M{l}{t}"))
                    e.wait_ge(*(V.at(f"g_TT{l - 1}{t}") if l > 1 else AC.at(f"g_Tc{t}")))
                    if l == 1 and t < 2:
                        e.wait_ge(*AC.at(f"g_Tc{t + 2}"))
                    for h in range(GH):
                        last = e.matmul(sc[t % 2][:, h * P:(h + 1) * P], gMT[:, t % 2, h, :], gT[:, t, h, :],
                                        start=True, stop=True)
                    last.then_inc(*PE.done(f"g_X{l}{t}"))
                    if t >= 1:
                        if t >= 3:
                            e.wait_ge(*V.at(f"g_TT{l}{t - 3}"))
                        inverse(t - 1)
                e.wait_ge(*V.at(f"g_TT{l}1"))
                inverse(3)
            for t in range(NT):
                e.wait_ge(*V.at(f"g_kbe{t}"))
                e.wait_ge(*(AC.at(f"g_wc{t - 2}") if t >= 2 else V.at(f"g_TT{LEVELS - 1}3")))
                for h in range(GH):
                    last = e.matmul(acc[t % 2][:, h * P:(h + 1) * P], gkbe[:, h, :], gTT[:, t, h, :], start=True, stop=True)
                last.then_inc(*PE.done(f"g_w{t}"))
            e.wait_ge(*V.at("g_vb"))
            e.wait_ge(*AC.at("g_wc3"))
            for t in range(NT):
                if t:
                    e.wait_ge(*V.at(f"g_S{t - 1}"))
                for h in range(GH):
                    o = ob[t % 2][:, h * P:(h + 1) * P]
                    last = e.matmul(o, gTT[:, t, h, :], gvtok[:, t, h, :], start=True, stop=(t == 0))
                    if t:
                        last = e.matmul(o, gwT[:, t, h, :], gst[:, h, :], start=False, stop=True)
                last.then_inc(*PE.done(f"g_vn{t}"))
                e.wait_ge(*AC.at(f"g_vnc{t}"))
                if t == 0:
                    e.wait_ge(*V.at("g_qe"))
                    e.wait_ge(*V.at("g_kdec"))
                if t < NT - 1:
                    for h in range(GH):
                        last = e.matmul(acc[t % 2][:, h * P:(h + 1) * P], gkdec[:, t, h, :], gvn[:, t % 2, h, :],
                                        start=True, stop=True)
                    last.then_inc(*PE.done(f"g_U{t}"))
                for h in range(GH):
                    o = sc[t % 2][:, h * P:(h + 1) * P]
                    last = e.matmul(o, gvn[:, t % 2, h, :], gQKT[:, t, h, :], start=True, stop=(t == 0))
                    if t:
                        last = e.matmul(o, gst[:, h, :], gqkv[:, h, t * P:(t + 1) * P], start=False, stop=True)
                last.then_inc(*PE.done(f"g_o{t}"))
            for h in range(GH):
                e.wait_ge(*AC.at(f"g_osq{h}"))
                columns(e, sq[:, h % 2, :], 4 * h, True, True, f"g_ocols{h}")
            for h in range(GH):
                e.wait_ge(*V.at(f"g_odiag{h}"))
                spread(e, f"g_obc{h}")

            def out_flat(name, ready, k1):
                e.wait_ge(*ready)
                c = U[name]
                with e.Fori(0, 2) as i:
                    PE.enter(name, i)
                    for j in range(4):
                        e.wait_ge(*(V.at(f"{name}x{j + 2}", i - 1) if j < 2 else V.at(f"{name}x{j - 2}", i)))
                        product(e, acc[j % 2], c + j + i * 4, c + j, lambda k: Mh[:, k, :], lambda k: Ml[:, k, :], k1=k1)
                    PE.leave(2)

            out_flat("mix_out", V.at(f"g_lo{GH - 1}"), KT)

            e.wait_ge(mem_in, 16)
            for k in range(KT):
                e.wait_ge(*(AC.at(f"m{k - 2}") if k >= 2 else V.at(f"g_lo{GH - 1}")))
                for t in range(2):
                    last = e.transpose(ob[k % 2][:, t * P:(t + 1) * P], m_tok[:, t, k * P:(k + 1) * P], ident)
                last.then_inc(*PE.done(f"m{k}"))
            norm_tensor(e, "nk", 2)
            norm_tensor(e, "nx")
            e.wait_ge(*V.at(f"nxh{KT - 1}"))
            for h in range(XH):
                if h >= 2:
                    e.wait_ge(*AC.at(f"x_q{h - 2}"))
                feat(e, acc[h % 2], U["xa_q"] + h, U["xa_q"] + h)
                if h >= 1:
                    e.wait_ge(*AC.at(f"x_sq{h - 1}"))
                    columns(e, sq[:, (h - 1) % 2, :], 4 * (h - 1), True, True, f"x_cols{h - 1}")
            for h in range(XH):
                u = U["xa_kv"] + h
                e.wait_ge(*(AC.at(f"x_q{h + 2}") if h < 2 else AC.at(f"x_k{h - 2}")))
                e.wait_ge(split_done, u + 1)
                for k in range(KT):
                    o = acc[h % 2][:, 0:MEM]
                    e.matmul(o, wh[:, u % RING, k, :], mh[:, k, :], start=(k == 0), stop=False)
                    e.matmul(o, wh[:, u % RING, k, :], ml[:, k, :], start=False, stop=False)
                    last = e.matmul(o, wl[:, u % RING, k, :], mh[:, k, :], start=False, stop=(k == KT - 1))
                last.then_inc(unit_used, 1)
                if h == 0:
                    e.wait_ge(*AC.at("x_sq3"))
                    columns(e, sq[:, 1, :], 12, True, True, "x_cols3")
                else:
                    e.wait_ge(*AC.at(f"x_sq{h + 3}"))
                    columns(e, sq[:, (h - 1) % 2, :], 16 + 2 * (h - 1), True, True, f"x_cols{h + 3}", n=2)
            e.wait_ge(*AC.at("x_sq7"))
            columns(e, sq[:, 1, :], 22, True, True, "x_cols7", n=2)
            for j in range(2):
                tok(e, U["xa_kv"] + 4 + 2 * j, U["xa_kv"] + 4 + 2 * j, "", [AC.at("x_v0") if j else AC.at("x_k2")],
                    mh, ml, 2)
            for h in range(XH):
                e.wait_ge(*V.at(f"x_diag{h}"))
                spread(e, f"x_bc{h}", 2)
            e.wait_ge(*AC.at("x_v1"))

            def cross_scores(h):
                e.wait_ge(*V.at(f"x_kn{h}"))
                for n in range(2):
                    if h:
                        e.wait_ge(*V.at(f"x_s{h - 1}{n}"))
                    for t in range(2 * n, 2 * n + 2):
                        last = e.matmul(sc[n][:, (t % 2) * MEM:(t % 2 + 1) * MEM], xq[:, h, t * P:(t + 1) * P],
                                        xk[:, h, :], start=True, stop=True)
                    last.then_inc(*PE.done(f"x_sc{h}{n}"))

            cross_scores(0)
            for h in range(XH):
                if h < XH - 1:
                    cross_scores(h + 1)
                e.wait_ge(*V.at(f"x_norm{h}"))
                for n in range(2):
                    if h:
                        e.wait_ge(*AC.at(f"x_ptc{h - 1}{n}"))
                    for t in range(NT):
                        last = e.transpose(bankx[n][:, t * P:(t + 1) * P], xS[:, h % 2, t, n * P:(n + 1) * P], ident)
                    last.then_inc(*PE.done(f"x_pt{h}{n}"))
                if h >= 2:
                    e.wait_ge(*V.at(f"x_lo{h - 2}"))
                for n in range(2):
                    e.wait_ge(*AC.at(f"x_ptc{h}{n}"))
                    last = e.matmul(ob[h % 2][:, :], xv[:, n, h * P:(h + 1) * P], xP[:, h % 2, n, :],
                                    start=(n == 0), stop=(n == 1))
                last.then_inc(*PE.done(f"x_o{h}"))
            out_flat("xa_out", V.at("x_lo3"), 4)

            norm_tensor(e, "nf")
            e.wait_ge(*V.at(f"nfh{KT - 1}"))
            for half in range(2):
                c = U[f"mlp_in{half}"]
                if half:
                    e.wait_ge(*V.after("mlp_out0x1", KT // 2))
                with e.Fori(0, 4) as i:
                    PE.enter(f"mlp_in{half}", i)
                    for j in range(4):
                        e.wait_ge(*(AC.at(f"f{half}r{j + 2}", i - 1) if j < 2 else AC.at(f"f{half}r{j - 2}", i)))
                        feat(e, acc[j % 2], c + j + i * 4, c + j)
                    PE.leave(4)
                out_tensor(e, f"mlp_out{half}", V.after(f"f{half}yl3", 4))
            e.wait_ge(*V.after(FINAL + "x1", KT // 2))
            for k in range(KT):
                if k >= 2:
                    e.wait_ge(*AC.at(f"outc{k - 2}"))
                for t in range(NT):
                    last = e.transpose(ob[k % 2][:, t * P:(t + 1) * P], xT[:, k, t * P:(t + 1) * P], ident)
                last.then_inc(*PE.done(f"out{k}"))

        @block.vector
        def _(e):
            count_from(e, V)
            e.memset(ones[:, :], 1.0).then_inc(*V.done("ones"))
            e.wait_ge(small_in, 16)
            e.wait_ge(*AC.at("cond_tanh"))
            step(e, e.scalar_tensor_tensor(out=cond[:, 1, :], in0=cond[:, 1, :], scalar=1.0, in1=sm("c"),
                                           op0=ALU.add, op1=ALU.mult), V)
            step(e, e.tensor_scalar(cond[:, 0, :], cond[:, 1, :], 0.5, None, ALU.mult), V)
            step(e, e.tensor_tensor(qk_gain[:, 0:1], sm("att_q_g"), sm("att_k_g"), ALU.mult), V)
            e.wait_ge(pos_in, 16)
            step(e, e.tensor_copy(ang[:, :], pos[:, :]), V)
            step(e, e.tensor_scalar(ang[:, :], ang[:, :], sm("inv_freq"), None, ALU.mult), V)
            step(e, e.tensor_scalar(tmp[:, 0, :], ang[:, :], 1.0 / TURN, ROUND, ALU.mult, ALU.add), V)
            step(e, e.tensor_scalar(tmp[:, 0, :], tmp[:, 0, :], -ROUND, None, ALU.add), V)
            for part in TURN_PARTS:
                step(e, e.scalar_tensor_tensor(out=ang[:, :], in0=tmp[:, 0, :], scalar=-part, in1=ang[:, :],
                                               op0=ALU.mult, op1=ALU.add), V)
            step(e, e.tensor_scalar(ang[:, :], ang[:, :], PI_BELOW, -PI_BELOW, ALU.min, ALU.max), V)
            step(e, e.scalar_tensor_tensor(out=tmp[:, 1, :], in0=ang[:, :], scalar=-1.0, in1=ang[:, :],
                                           op0=ALU.mult, op1=ALU.max), V)
            step(e, e.tensor_scalar(tmp[:, 1, :], tmp[:, 1, :], -1.0, TURN / 4, ALU.mult, ALU.add), V, "angles")
            for k in range(KT):
                e.wait_ge(ada_in[k], 16)
                ada_sum(e, ada_acc0[:, 0:2 * D], ada_w0[:, k, :], k, "ada0sum" if k == KT - 1 else None)

            def modulation(layer, n0, n1, name):
                cols = mod[:, layer, :, :].rearrange("p a k -> p (a k)")
                step(e, e.tensor_tensor(cols[:, n0:n1], st[:, n0:n1], sm(f"ada_b{layer}", n0, n1 - n0), ALU.add),
                     V, name)

            def gains(layer):
                step(e, e.scalar_tensor_tensor(out=gain[:, layer, :], in0=mod[:, layer, 1, :], scalar=1.0,
                                               in1=sm(f"norm_g{layer}"), op0=ALU.add, op1=ALU.mult), V)

            e.wait_ge(*PE.at("ada0cols"))
            modulation(0, 0, 16, "mod0")
            gains(0)
            norm_vector(e, "n0", lambda k: gain[:, 0, k:k + 1])
            for k in range(KT):
                e.wait_ge(ada_in[k], 32)
                ada_sum(e, ada_accg[:, :], ada_g0[:, k, :], k, "ada0gsum" if k == KT - 1 else None)

            e.wait_ge(*AC.at("rope"))
            with e.Fori(0, RH) as i:
                V.enter("ret_vector", i)
                c = U["ret"] + i * 12
                for a, x in ((0, q_), (2, k_)):
                    e.wait_ge(*AC.at(f"r_qk{a + 1}", i))
                    x1, x2, t1, t2 = x[:, 0, :], x[:, 1, :], tmp[:, 0, :], tmp[:, 1, :]
                    e.wait_ge(*V.last())
                    e.tensor_tensor(t1, x1, sin_[:, :], ALU.mult).then_inc(*V.done())
                    step(e, e.tensor_tensor(t2, x2, sin_[:, :], ALU.mult), V)
                    e.tensor_tensor(x1, x1, cos_[:, :], ALU.mult).then_inc(*V.done())
                    step(e, e.tensor_tensor(x2, x2, cos_[:, :], ALU.mult), V)
                    e.tensor_tensor(x1, x1, t2, ALU.subtract).then_inc(*V.done(f"r_rope{a}"))
                    step(e, e.tensor_tensor(x2, x2, t1, ALU.add), V, f"r_rope{a + 1}")
                e.wait_ge(decay_in, i * 16 + 16)
                for n in range(NT):
                    e.wait_ge(*PE.at(f"r_sc{n}", i))
                    e.tensor_tensor(t_[:, KOFF[n]:KOFF[n] + (NT - n) * P], sc[n % 2][:, 0:(NT - n) * P],
                                    dec[:, 0:(NT - n) * P], ALU.mult).then_inc(*V.done(f"r_s{n}"))

                def gate(n):
                    e.wait_ge(*AC.at(f"r_th{n}", i))
                    e.scalar_tensor_tensor(out=s_[:, n, :], in0=s_[:, n, :], scalar=1.0, in1=acc[n % 2][:, :],
                                           op0=ALU.add, op1=ALU.mult).then_inc(*V.done(f"r_g{n}"))

                gate(0)
                gate(1)
                e.wait_ge(*PE.at("r_cols3", i))
                rsqrt(e, NT, 1.0 / RV)
                diagonal(e, 0, "r_diag")
                gate(2)
                gate(3)
                e.wait_ge(*PE.at("r_bc", i))

                def rest(n):
                    e.wait_ge(*AC.at(f"r_yh{n}", i))
                    e.tensor_tensor(Yl[:, bass.ds(i * 4 + n, 1), :], o_[n].unsqueeze(1),
                                    Yh[:, bass.ds(i * 4 + n, 1), :].bitcast(F32), ALU.subtract)\
                     .then_inc(*V.done(f"r_yl{n}"))

                for n in range(4):
                    g0 = SMALL["ret_gn_g"][0]
                    step(e, e.scalar_tensor_tensor(out=o_[n], in0=o_[n], scalar=small[:, bass.ds(i * 4 + n + g0, 1)],
                                                   in1=bc[:, :], op0=ALU.mult, op1=ALU.mult), V)
                    e.scalar_tensor_tensor(out=o_[n], in0=o_[n], scalar=0.5, in1=s_[:, n, :],
                                           op0=ALU.mult, op1=ALU.mult).then_inc(*V.done(f"r_y{n}"))
                    if n >= 1:
                        rest(n - 1)
                rest(3)
                V.leave(RH)
            e.wait_ge(*PE.at("ada0gate"))
            modulation(0, 16, 24, "mod0gate")
            step(e, e.memset(ada_acc1[:, :], 0.0), V)

            def ada1(e, i, b):
                e.wait_ge(ada1_in[b], i * 16 + 16)
                step(e, e.scalar_tensor_tensor(out=ada_acc1[:, :], in0=ada_w1[:, b, :],
                                               scalar=cond[:, 0, bass.ds(i * 2 + b, 1)], in1=ada_acc1[:, :],
                                               op0=ALU.mult, op1=ALU.add), V, f"ada1sum{b}")

            out_vector(e, "ret_out", lambda n: mod[:, 0, 2, bass.ds(n, 1)], ada1)
            e.wait_ge(*PE.at("ada1cols"))
            modulation(1, 0, 24, "mod1")
            gains(1)
            norm_vector(e, "n1", lambda k: gain[:, 1, k:k + 1])
            for h in range(2):
                e.memset(ab[0:CHUNK, h, S - CHUNK:S], NEG).then_inc(*V.done("mask"))

            def att_vg(i, t, turn):
                e.wait_ge(*PE.at(f"{t}cols3", i))
                rsqrt(e, 16, 1.0 / AD)
                step(e, e.tensor_scalar(rs[:, 0, 0:8], rs[:, 0, 0:8], AD ** -0.5, None, ALU.mult), V)
                for h in range(2):
                    diagonal(e, 8 + 4 * h, f"{t}diag{h}")
                    e.wait_ge(*PE.at(f"{t}bc{h}", i))
                    step(e, e.tensor_tensor(ak[:, h, :], ak[:, h, :], bc[:, :], ALU.mult), V, f"{t}k{h}")
                for h in range(2):
                    e.wait_ge(*AC.at(f"{t}th{h}", i))
                    e.scalar_tensor_tensor(out=ag[:, h, :], in0=ag[:, h, :], scalar=1.0, in1=acc[h][:, :],
                                           op0=ALU.add, op1=ALU.mult).then_inc(*V.done(f"{t}g{h}"))
                for h in range(2):
                    e.wait_ge(bias_in[h], i * 32 + 32)
                    for n in range(NT):
                        x = aS[:, h, QOFF[n]:QOFF[n] + (n + 1) * P]
                        r = h * 4 + n
                        e.wait_ge(*PE.at(f"{t}sc{h}{n}", i))
                        step(e, e.scalar_tensor_tensor(out=x, in0=sc[r % 2][:, 0:(n + 1) * P], scalar=rs[:, 0, r:r + 1],
                                                       in1=ab[:, h, S - (n + 1) * P:S], op0=ALU.mult, op1=ALU.add),
                             V, f"{t}s{h}{n}")
                        e.tensor_reduce(amax[:, 2, r:r + 1], x, AX.X, ALU.max).then_inc(*V.done())
                    e.wait_ge(*V.last())
                    e.tensor_scalar(amax[:, 0, 4 * h:4 * h + 4], amax[:, 2, 4 * h:4 * h + 4], -1.0, None, ALU.mult)\
                     .then_inc(*V.done(f"{t}nm{h}"))
                for h in range(2):
                    e.wait_ge(*AC.at(f"{t}exp{h}3", i))
                    step(e, e.reciprocal(amax[:, 2, 4 * h:4 * h + 4], amax[:, 1, 4 * h:4 * h + 4]), V)
                    for n in range(NT):
                        x = aS[:, h, QOFF[n]:QOFF[n] + (n + 1) * P]
                        e.tensor_scalar(x, x, amax[:, 2, 4 * h + n:4 * h + n + 1], None, ALU.mult)\
                         .then_inc(*V.done(f"{t}norm{h}" if n == NT - 1 else None))

            def att_pv(pair, i, t):
                for h in range(2):
                    e.wait_ge(*PE.at(f"{t}o{h}", i))
                    e.scalar_tensor_tensor(out=ay[:, h, :], in0=ob[h][:, :], scalar=0.5, in1=ag[:, h, :],
                                           op0=ALU.mult, op1=ALU.mult).then_inc(*V.done(f"{t}y{h}"))
                for h in range(2):
                    e.wait_ge(*AC.at(f"{t}yh{h}", i))
                    e.tensor_tensor(Yl[:, bass.ds(pair * 2 + h, 1), :], ay[:, h, :].unsqueeze(1),
                                    Yh[:, bass.ds(pair * 2 + h, 1), :].bitcast(F32), ALU.subtract)\
                     .then_inc(*V.done(f"{t}yl{h}"))

            att_vg(0, "p", 0)
            with e.Fori(1, AH // 2) as i:
                V.enter("att_vector", i, 1)
                att_pv(i - 1, i, "a")
                att_vg(i, "a", i)
                V.leave(AH // 2 - 1)
            att_pv(AH // 2 - 1, 0, "z")
            out_vector(e, "att_out", lambda n: mod[:, 1, 2, bass.ds(n, 1)])
            norm_vector(e, "nm", lambda k: sm("norm_mix", k, 1))

            step(e, e.tensor_scalar(negs[:, :], cst("causal"), -1.0, -NEG, ALU.add, ALU.mult), V)
            step(e, e.tensor_tensor(strict[:, :], cst("causal"), ident, ALU.subtract), V)
            e.wait_ge(wab_in, 16)
            step(e, e.tensor_copy(wab_high[:, :, :], wab[:, :, :]), V)
            step(e, e.tensor_tensor(wab_low[:, :, :], wab[:, :, :], wab_high[:, :, :].bitcast(F32), ALU.subtract), V, "wab")
            step(e, e.tensor_tensor(qk_gain[:, 1:2], sm("dsa_q_norm"), sm("dsa_k_norm"), ALU.mult), V)
            step(e, e.tensor_tensor(qk_gain[:, 2:3], sm("xa_q_norm"), sm("xa_k_norm"), ALU.mult), V)
            e.memset(cy[:, :, 0:CONVW - 1], 0.0).then_inc(*V.done())
            for j in range(2):
                e.wait_ge(*AC.at(f"c_th{j}"))
                e.wait_ge(unit_used, U["mix"] + 2 * j + 2)
                e.scalar_tensor_tensor(out=cy[:, j, CONVW - 1:], in0=cg[:, j, :], scalar=1.0, in1=acc[1][:, :],
                                       op0=ALU.add, op1=ALU.mult).then_inc(*V.done(f"c_in{j}"))
            e.wait_ge(*V.last())
            cw = SMALL["conv_dw"][0]
            for k in range(CONVW):
                for j in range(2):
                    w_ = small[:, cw + j * CONVW + k:cw + j * CONVW + k + 1]
                    if k == 0:
                        e.tensor_scalar(co[:, j, :], cy[:, j, 0:S], w_, None, ALU.mult).then_inc(*V.done(f"c_{k}{j}"))
                    else:
                        e.wait_ge(*V.at(f"c_{k - 1}{j}"))
                        e.scalar_tensor_tensor(out=co[:, j, :], in0=cy[:, j, k:k + S], scalar=w_, in1=co[:, j, :],
                                               op0=ALU.mult, op1=ALU.add).then_inc(*V.done(f"c_{k}{j}"))
            e.wait_ge(*V.last())
            for j in range(2):
                e.tensor_scalar(co[:, j, :], co[:, j, :], 0.5, sm("conv_dw_b", j, 1), ALU.mult, ALU.add)\
                 .then_inc(*V.done("c_conv"))
            e.wait_ge(*PE.at("c_cols1"))
            step(e, e.tensor_scalar(rs[:, 0, 0:NT], st[:, 0:NT], 1.0 / (2 * P), None, ALU.mult), V)
            diagonal(e, 0, "c_mean")
            e.wait_ge(*PE.at("c_mbc"))
            for j in range(2):
                e.tensor_tensor(co[:, j, :], co[:, j, :], bc[:, :], ALU.subtract).then_inc(*V.done("c_centered"))
            e.wait_ge(*PE.at("c_vcols1"))
            rsqrt(e, NT, 1.0 / (2 * P))
            diagonal(e, 0, "c_diag")
            e.wait_ge(*PE.at("c_bc"))
            for j in range(2):
                e.scalar_tensor_tensor(out=co[:, j, :], in0=co[:, j, :], scalar=sm("conv_ln_g", j, 1), in1=bc[:, :],
                                       op0=ALU.mult, op1=ALU.mult).then_inc(*V.done(f"c_t{j}"))
            for j in range(2):
                e.wait_ge(*AC.at(f"c_sth{j}"))
                e.scalar_tensor_tensor(out=co[:, j, :], in0=cg[:, j, :], scalar=1.0, in1=co[:, j, :],
                                       op0=ALU.add, op1=ALU.mult).then_inc(*V.done(f"c_y{j}"))
            for j in range(2):
                e.wait_ge(*AC.at(f"c_hi{j}"))
                e.scalar_tensor_tensor(out=Ml[:, 6 + j, :], in0=co[:, j, :], scalar=0.5,
                                       in1=Mh[:, 6 + j, :].bitcast(F32), op0=ALU.mult, op1=ALU.subtract)\
                 .then_inc(*V.done(f"c_lo{j}"))

            e.wait_ge(*PE.at("d_cols2"))
            rsqrt(e, 20, 1.0 / DD)
            step(e, e.tensor_scalar(rs[:, 0, 0:16], rs[:, 0, 0:16], DD ** -0.5, None, ALU.mult), V)
            diagonal(e, 16, "d_diag")
            e.wait_ge(*PE.at("d_bc"))
            e.wait_ge(*AC.at("d_kc"))
            e.tensor_tensor(dk[:, :], dk[:, :], bc[:, :], ALU.mult).then_inc(*V.done("d_kn"))
            e.wait_ge(*AC.at("tc"))
            step(e, e.tensor_scalar(gc[:, 1, :].rearrange("p (t h) -> p t h", t=NT), tc[:, :, 0:4],
                                    DH ** -0.5 * DD ** -0.5, None, ALU.mult), V)
            for t in range(1, NT):
                w_ = (t + 1) * P
                x = score[:, t - 1, 0:w_]
                for h in range(DH):
                    n = (t - 1) * DH + h
                    wcol = gc[:, 1, t * 4 + h:t * 4 + h + 1]
                    e.wait_ge(*AC.at(f"d_relu{n}"))
                    if h == 0:
                        step(e, e.tensor_scalar(x, drelu[:, n % 2, 0:w_], wcol, None, ALU.mult), V, f"d_sum{n}")
                    else:
                        step(e, e.scalar_tensor_tensor(out=x, in0=drelu[:, n % 2, 0:w_], scalar=wcol, in1=x,
                                                       op0=ALU.mult, op1=ALU.add), V, f"d_sum{n}")
                d = score[:, t - 1, t * P:w_]
                step(e, e.tensor_tensor(d, d, cst("causal"), ALU.mult), V)
                step(e, e.tensor_tensor(d, d, negs[:, :], ALU.add), V)
            for r in range(TOPK // 8):
                for t in range(1, NT):
                    w_ = (t + 1) * P
                    src = (work if r else score)[:, t - 1, 0:w_]
                    if r:
                        e.wait_ge(*V.at(f"d_rep{r - 1}{t}"))
                    e.max(best[:, t - 1, :], src).then_inc(*V.done(f"d_max{r}{t}"))
                for t in range(1, NT):
                    w_ = (t + 1) * P
                    src = (work if r else score)[:, t - 1, 0:w_]
                    e.wait_ge(*V.at(f"d_max{r}{t}"))
                    e.match_replace(work[:, t - 1, 0:w_], best[:, t - 1, :], src, -3.0e38)\
                     .then_inc(*V.done(f"d_rep{r}{t}"))
            e.wait_ge(*V.last())
            e.tensor_copy(dmask[:, 0:P], negs[:, :]).then_inc(*V.done())
            for t in range(1, NT):
                w_ = (t + 1) * P
                m = dmask[:, QOFF[t]:QOFF[t] + w_]
                step(e, e.tensor_tensor(m, work[:, t - 1, 0:w_], score[:, t - 1, 0:w_], ALU.not_equal), V)
                step(e, e.tensor_scalar(m, m, -1.0, -NEG, ALU.add, ALU.mult), V)
            for g in range(2):
                for h in range(2):
                    for n in range(NT):
                        r = h * 4 + n
                        x = dS[:, h, QOFF[n]:QOFF[n] + (n + 1) * P]
                        col = g * 8 + 2 * n + h
                        e.wait_ge(*PE.at(f"d_sc{g}{r}"))
                        step(e, e.scalar_tensor_tensor(out=x, in0=sc[r % 2][:, 0:(n + 1) * P],
                                                       scalar=rs[:, 0, col:col + 1],
                                                       in1=dmask[:, QOFF[n]:QOFF[n] + (n + 1) * P],
                                                       op0=ALU.mult, op1=ALU.add), V, f"d_s{g}{r}")
                        e.tensor_reduce(amax[:, 2, r:r + 1], x, AX.X, ALU.max).then_inc(*V.done())
                    e.wait_ge(*V.last())
                    e.tensor_scalar(amax[:, 0, 4 * h:4 * h + 4], amax[:, 2, 4 * h:4 * h + 4], -1.0, None, ALU.mult)\
                     .then_inc(*V.done(f"d_nm{g}{h}"))
                for h in range(2):
                    e.wait_ge(*AC.at(f"d_exp{g}{h}3"))
                    step(e, e.reciprocal(amax[:, 2, 4 * h:4 * h + 4], amax[:, 1, 4 * h:4 * h + 4]), V)
                    for n in range(NT):
                        x = dS[:, h, QOFF[n]:QOFF[n] + (n + 1) * P]
                        e.tensor_scalar(x, x, amax[:, 2, 4 * h + n:4 * h + n + 1], None, ALU.mult)\
                         .then_inc(*V.done(f"d_norm{g}{h}"))
                e.wait_ge(*AC.at(f"d_hi{g}"))
                e.tensor_tensor(Ml[:, 4 + g, :], ob[g][:, :], Mh[:, 4 + g, :].bitcast(F32), ALU.subtract)\
                 .then_inc(*V.done(f"d_lo{g}"))

            def by_head(x):
                return x.unsqueeze(1).to_broadcast([P, NT, GH])

            def grid(n):
                return gc[:, n, :].rearrange("p (t h) -> p t h", t=NT)

            step(e, e.tensor_tensor(grid(1), tc[:, :, 4:8], by_head(sm("gdn_dt_bias")), ALU.add), V)
            step(e, e.scalar_tensor_tensor(out=gc[:, 2, :], in0=gc[:, 1, :], scalar=-1.0, in1=gc[:, 1, :],
                                           op0=ALU.mult, op1=ALU.max), V, "g_abs")
            e.wait_ge(*AC.at("g_ex"))
            step(e, e.tensor_scalar(gc[:, 2, :], gc[:, 2, :], 1.0, None, ALU.add), V, "g_1p")
            e.wait_ge(*AC.at("g_bth"))
            step(e, e.tensor_scalar(gc[:, 4, :], gc[:, 3, :], 1.0, 0.5, ALU.add, ALU.mult), V)
            e.wait_ge(*AC.at("g_ln"))
            step(e, e.scalar_tensor_tensor(out=gc[:, 1, :], in0=gc[:, 1, :], scalar=0.0, in1=gc[:, 2, :],
                                           op0=ALU.max, op1=ALU.add), V)
            step(e, e.scalar_tensor_tensor(out=grid(5), in0=grid(1), scalar=-1.0, in1=by_head(gc[:, 0, 0:GH]),
                                           op0=ALU.mult, op1=ALU.mult), V, "g_g")
            step(e, e.memset(gpre[:, :, 0:GDN_TAPS - 1], 0.0), V)
            w0 = SMALL["gdn_conv"][0]

            def conv(j):
                c = gqkv[:, j, :]
                for k in range(GDN_TAPS):
                    w_ = small[:, w0 + j * GDN_TAPS + k:w0 + j * GDN_TAPS + k + 1]
                    if k == 0:
                        step(e, e.tensor_scalar(c, gpre[:, j % 2, 0:S], w_, None, ALU.mult), V)
                    else:
                        step(e, e.scalar_tensor_tensor(out=c, in0=gpre[:, j % 2, k:k + S], scalar=w_, in1=c,
                                                       op0=ALU.mult, op1=ALU.add), V,
                             f"g_conv{j}" if k == GDN_TAPS - 1 else None)

            def silu(j):
                e.wait_ge(*AC.at(f"g_th{j}"))
                e.scalar_tensor_tensor(out=gqkv[:, j, :], in0=gth[:, j % 2, :], scalar=1.0, in1=gqkv[:, j, :],
                                       op0=ALU.add, op1=ALU.mult).then_inc(*V.done(f"g_silu{j}"))

            for j in range(12):
                e.wait_ge(*AC.at(f"g_pre{j}"))
                conv(j)
                if j:
                    silu(j - 1)
            silu(11)
            for j in range(4):
                e.wait_ge(*AC.at(f"g_zth{j}"))
                e.scalar_tensor_tensor(out=gz[:, j, :], in0=gz[:, j, :], scalar=1.0, in1=acc[j % 2][:, :],
                                       op0=ALU.add, op1=ALU.mult).then_inc(*V.done(f"g_z{j}"))
            e.wait_ge(*PE.at("g_cols7"))
            rsqrt(e, 32, 0.25)
            step(e, e.tensor_scalar(rs[:, 0, 0:16], rs[:, 0, 0:16], 0.5 * GD ** -0.5, None, ALU.mult), V)
            step(e, e.tensor_scalar(rs[:, 0, 16:32], rs[:, 0, 16:32], 0.5, None, ALU.mult), V)
            for j in range(8):
                if j:
                    e.wait_ge(*PE.at(f"g_bc{j - 1}"))
                diagonal(e, 4 * j, f"g_diag{j}")
                e.wait_ge(*PE.at(f"g_bc{j}"))
                e.tensor_tensor(gqkv[:, j, :], gqkv[:, j, :], bc[:, :], ALU.mult).then_inc(*V.done(f"g_n{j}"))
            e.wait_ge(*AC.at("g_el"))
            step(e, e.tensor_tensor(gc[:, 8, :], st[:, 16:32], gc[:, 6, :], ALU.subtract), V, "g_dld")

            def wide(n, t):
                return gc[:, n, 4 * t:4 * t + 4].unsqueeze(2).to_broadcast([P, GH, P])

            def every(x):
                return x.unsqueeze(1).to_broadcast([P, GH, P])

            def bank(x):
                return x[:, :].rearrange("p (h n) -> p h n", h=GH)

            for t in range(NT):
                e.wait_ge(*V.last())
                e.tensor_copy(ggb[:, :, :], wide(5, t)).then_inc(*V.done(f"g_gb{t}"))
                e.wait_ge(*PE.at(f"g_D{t}"))
                if t:
                    e.wait_ge(*AC.at(f"g_QKTc{t - 1}"))
                step(e, e.tensor_tensor(gG[:, :, :], wide(6, t), bank(ob[0]), ALU.subtract), V)
                step(e, e.tensor_scalar(gG[:, :, :], gG[:, :, :], 0.0, None, ALU.min), V, f"g_diff{t}")
                e.wait_ge(*AC.at(f"g_G{t}"))
                step(e, e.tensor_tensor(gG[:, :, :], gG[:, :, :], every(cst("causal")), ALU.mult), V)
                e.wait_ge(*PE.at(f"g_kk{t}"))
                step(e, e.tensor_tensor(gA[:, :, :], bank(sc[0]), gG[:, :, :], ALU.mult), V)
                step(e, e.tensor_tensor(gA[:, :, :], gA[:, :, :], every(strict[:, :]), ALU.mult), V)
                step(e, e.tensor_tensor(gA[:, :, :], gA[:, :, :], wide(4, t), ALU.mult), V, f"g_A{t}")
                e.wait_ge(*PE.at(f"g_qk{t}"))
                e.tensor_tensor(gQK[:, :, :], bank(sc[1]), gG[:, :, :], ALU.mult).then_inc(*V.done(f"g_QK{t}"))
                e.wait_ge(*AC.at(f"g_eD{t}"))
                q = gqkv[:, 0:GH, t * P:(t + 1) * P]
                step(e, e.tensor_tensor(q, q, ggb[:, :, :], ALU.mult), V, "g_qe" if t == NT - 1 else None)
                e.wait_ge(*PE.at(f"g_AT{t}"))
                e.wait_ge(*PE.at(f"g_QKT{t}"))
                if t == 0:
                    e.wait_ge(levels_in, 16)
                e.wait_ge(*AC.at(f"g_ATc{t}"))
                step(e, e.tensor_tensor(gTT[:, t, :, :], gAT[:, t, :, :], every(glev[:, 0, :]), ALU.mult), V)
                step(e, e.tensor_tensor(gTT[:, t, :, :], every(ident), gTT[:, t, :, :], ALU.subtract), V, f"g_TT0{t}")
            for l in range(1, LEVELS):
                def update(t):
                    if l < LEVELS - 1:
                        e.wait_ge(*PE.at(f"g_P{l}{t}"))
                        e.tensor_tensor(gT[:, t, :, :], gT[:, t, :, :], bank(ob[t % 2]), ALU.subtract)\
                         .then_inc(*V.done(f"g_T{l}{t}"))
                    e.wait_ge(*PE.at(f"g_R{l}{t}"))
                    e.tensor_tensor(gTT[:, t, :, :], gTT[:, t, :, :], bank(acc[t % 2]), ALU.subtract)\
                     .then_inc(*V.done(f"g_TT{l}{t}"))

                for t in range(NT):
                    if t >= 2:
                        e.wait_ge(*PE.at(f"g_X{l}{t - 2}"))
                    elif l > 1:
                        e.wait_ge(*PE.at(f"g_X{l - 1}{t + 2}"))
                    e.tensor_tensor(gMT[:, t % 2, :, :], gAT[:, t, :, :], every(glev[:, l, :]), ALU.mult)\
                     .then_inc(*V.done(f"g_M{l}{t}"))
                    if t >= 2:
                        update(t - 2)
                update(2)
                update(3)
            e.wait_ge(*V.last())
            step(e, e.tensor_tensor(gc[:, 7, :], gc[:, 7, :], gc[:, 4, :], ALU.mult), V)
            step(e, e.tensor_scalar(gc[:, 3, :], gc[:, 4, :], 0.5, None, ALU.mult), V)
            for t in range(NT):
                if t:
                    e.wait_ge(*PE.at(f"g_w{t - 1}"))
                e.tensor_tensor(gkbe[:, :, :], gktok[:, t, :, :], wide(7, t), ALU.mult).then_inc(*V.done(f"g_kbe{t}"))
            for t in range(NT):
                e.tensor_tensor(gvtok[:, t, :, :], gvtok[:, t, :, :], wide(3, t), ALU.mult).then_inc(*V.done("g_vb"))
            for t in range(NT):
                e.tensor_tensor(gkdec[:, t, :, :], gktok[:, t, :, :], wide(8, t), ALU.mult).then_inc(*V.done("g_kdec"))
            for t in range(NT - 1):
                e.wait_ge(*PE.at(f"g_U{t}"))
                if t == 0:
                    e.tensor_copy(gst[:, :, :], bank(acc[0])).then_inc(*V.done("g_S0"))
                    continue
                e.wait_ge(*PE.at(f"g_o{t}"))
                step(e, e.tensor_tensor(gst[:, :, :], gst[:, :, :], wide(9, t), ALU.mult), V)
                e.tensor_tensor(gst[:, :, :], gst[:, :, :], bank(acc[t % 2]), ALU.add).then_inc(*V.done(f"g_S{t}"))
            e.wait_ge(*PE.at("g_ocols3"))
            rsqrt(e, 16, 1.0 / GD)
            for h in range(GH):
                if h:
                    e.wait_ge(*PE.at(f"g_obc{h - 1}"))
                diagonal(e, 4 * h, f"g_odiag{h}")
                e.wait_ge(*PE.at(f"g_obc{h}"))
                step(e, e.scalar_tensor_tensor(out=goT[:, h, :], in0=goT[:, h, :], scalar=sm("gdn_norm"), in1=bc[:, :],
                                               op0=ALU.mult, op1=ALU.mult), V)
                e.scalar_tensor_tensor(out=goT[:, h, :], in0=goT[:, h, :], scalar=0.5, in1=gz[:, h, :],
                                       op0=ALU.mult, op1=ALU.mult).then_inc(*V.done(f"g_y{h}"))
            for h in range(GH):
                e.wait_ge(*AC.at(f"g_hi{h}"))
                e.tensor_tensor(Ml[:, h, :], goT[:, h, :], Mh[:, h, :].bitcast(F32), ALU.subtract)\
                 .then_inc(*V.done(f"g_lo{h}"))

            def add_flat(name):
                with e.Fori(0, 2) as i:
                    V.enter(name, i)
                    for j in range(4):
                        x = xT[:, bass.ds(i * 4 + j, 1), :]
                        e.wait_ge(unit_used, U[name] + j + 1 + i * 4)
                        e.tensor_tensor(x, acc[j % 2][:, :].unsqueeze(1), x, ALU.add).then_inc(*V.done(f"{name}x{j}"))
                    V.leave(2)

            add_flat("mix_out")

            norm_vector(e, "nk", lambda k: sm("norm_mem", k, 1), mT, mh, ml, MEM)
            norm_vector(e, "nx", lambda k: sm("norm_cross", k, 1))
            e.wait_ge(*PE.at("x_cols7"))
            rsqrt(e, 24, 1.0 / XD)
            step(e, e.tensor_scalar(rs[:, 0, 0:16], rs[:, 0, 0:16], XD ** -0.5, None, ALU.mult), V)
            for h in range(XH):
                if h:
                    e.wait_ge(*PE.at(f"x_bc{h - 1}"))
                diagonal(e, 16 + 2 * h, f"x_diag{h}", 2)
                e.wait_ge(*PE.at(f"x_bc{h}"))
                e.tensor_tensor(xk[:, h, :], xk[:, h, :], bc[:, 0:MEM], ALU.mult).then_inc(*V.done(f"x_kn{h}"))
            def cross_softmax(h):
                if h >= 2:
                    e.wait_ge(*PE.at(f"x_pt{h - 2}1"))
                for t in range(NT):
                    e.wait_ge(*PE.at(f"x_sc{h}{t // 2}"))
                    r = 4 * h + t
                    e.tensor_scalar(xS[:, h % 2, t, :], sc[t // 2][:, (t % 2) * MEM:(t % 2 + 1) * MEM],
                                    rs[:, 0, r:r + 1], None, ALU.mult)\
                     .then_inc(*V.done(f"x_s{h}{t // 2}"))
                e.wait_ge(*V.last())
                step(e, e.tensor_reduce(amax[:, 2, 4 * h:4 * h + 4], xS[:, h % 2, :, :], AX.X, ALU.max), V)
                e.tensor_scalar(amax[:, 0, 4 * h:4 * h + 4], amax[:, 2, 4 * h:4 * h + 4], -1.0, None, ALU.mult)\
                 .then_inc(*V.done(f"x_nm{h}"))

            cross_softmax(0)
            for h in range(XH):
                if h < XH - 1:
                    cross_softmax(h + 1)
                e.wait_ge(*AC.at(f"x_exp{h}3"))
                step(e, e.reciprocal(amax[:, 2, 4 * h:4 * h + 4], amax[:, 1, 4 * h:4 * h + 4]), V)
                for t in range(NT):
                    x = xS[:, h % 2, t, :]
                    e.tensor_scalar(x, x, amax[:, 2, 4 * h + t:4 * h + t + 1], None, ALU.mult)\
                     .then_inc(*V.done(f"x_norm{h}"))
                e.wait_ge(*AC.at(f"x_hi{h}"))
                e.tensor_tensor(Ml[:, h, :], ob[h % 2][:, :], Mh[:, h, :].bitcast(F32), ALU.subtract)\
                 .then_inc(*V.done(f"x_lo{h}"))
            add_flat("xa_out")

            norm_vector(e, "nf", lambda k: sm("norm_mlp", k, 1))
            for half in range(2):
                with e.Fori(0, 4) as i:
                    V.enter(f"mlp{half}_vector", i)
                    for j in range(4):
                        x = sq[:, j % 2, :]
                        y = bass.ds(i * 4 + j, 1)
                        e.wait_ge(*AC.at(f"f{half}r{j}", i))
                        e.tensor_tensor(x, x, x, ALU.mult).then_inc(*V.done(f"f{half}y{j}"))
                        e.wait_ge(*AC.at(f"f{half}yh{j}", i))
                        e.tensor_tensor(Yl[:, y, :], x.unsqueeze(1), Yh[:, y, :].bitcast(F32), ALU.subtract)\
                         .then_inc(*V.done(f"f{half}yl{j}"))
                    V.leave(4)
                out_vector(e, f"mlp_out{half}", None)

    return {"PE": (PE.marks), "AC": AC.marks, "V": V.marks, "G": G.marks}


def constants():
    import numpy as np
    const = np.zeros((P, NCONST), np.float32)
    i, j = np.arange(P)[:, None], np.arange(P)[None, :]

    def put(name, table):
        c, w = CONST[name]
        const[:, c:c + w] = table

    put("ident", i == j)
    put("causal", i >= j)
    put("cumsum", i <= j)
    put("halves", (i // DD) == np.arange(2)[None, :])
    level = [(i // (2 * b) == j // (2 * b)) & (i // b % 2 == 1) & (j // b % 2 == 0) for b in (1 << n for n in range(LEVELS))]
    levels = np.concatenate([m.T for m in level], axis=1).astype(np.float32)
    key, query = np.arange(P)[:, None], np.arange(S)[None, :]
    gamma = 1.0 - 2.0 ** (-5.0 - np.arange(RH))
    decay = np.where(key // CHUNK <= query // CHUNK, gamma[:, None, None] ** np.abs(query - key), 0.0) * RQK ** -0.5
    decay = np.concatenate([decay, decay[-1:]]).astype(np.float32)
    inv_freq = (np.float32(1) / np.power(np.float32(10000), np.arange(0, RQK, 2, dtype=np.float32) / np.float32(RQK)))
    return const, levels, decay, inv_freq.astype(np.float32)


def lay_out(x):
    import numpy as np
    const, levels, decay, inv_freq = constants()
    a = {name: np.asarray(value) for name, value in x.items()}

    def cols(v):
        return np.ascontiguousarray(v).reshape(-1, P).T

    def twice(v):
        return np.concatenate([v.reshape(-1), v.reshape(-1)])[:, None]

    def taps(w):
        t, c = w.shape
        return w.T.reshape(c // P, P, t).transpose(1, 0, 2).reshape(P, -1)

    small = {
        "c": cols(a["c"]), "norm_g0": cols(a["norm_g"][0]), "norm_g1": cols(a["norm_g"][1]),
        "ada_b0": cols(a["ada_b"][0]), "ada_b1": cols(a["ada_b"][1]), "ret_gn_g": cols(a["ret_gn_g"]),
        "att_q_g": cols(a["att_q_g"]), "att_k_g": cols(a["att_k_g"]), "norm_mix": cols(a["norm_mix_2"]),
        "norm_mem": cols(a["norm_mem_2"]), "norm_cross": cols(a["norm_cross_2"]), "norm_mlp": cols(a["norm_mlp_2"]),
        "gdn_conv": taps(a["gdn_conv_2"][0]), "gdn_a_log": np.repeat(a["gdn_a_log_2"], P, 0),
        "gdn_dt_bias": np.repeat(a["gdn_dt_bias_2"], P, 0), "gdn_norm": cols(a["gdn_norm_2"]),
        "dsa_q_norm": twice(a["dsa_q_norm_2"]), "dsa_k_norm": twice(a["dsa_k_norm_2"]),
        "conv_dw": taps(a["conv_dw_2"][0]), "conv_dw_b": cols(a["conv_dw_b_2"]),
        "conv_ln_g": cols(a["conv_ln_g_2"]), "conv_ln_b": cols(a["conv_ln_b_2"]),
        "xa_q_norm": cols(a["xa_q_norm_2"]), "xa_k_norm": cols(a["xa_k_norm_2"]), "inv_freq": inv_freq[:, None],
    }
    packed = np.concatenate([small[name] for name, _ in SMALL_WIDTHS], axis=1)
    reach = 2 * CHUNK
    distance = np.arange(P)[:, None] - np.arange(S)[None, :] + S - P
    bias = a["att_rel_bias"][0][:, np.clip(distance, -reach, reach) + reach]
    bias = np.concatenate([bias, bias[-2:]])
    given = {"small": packed, "const": const, "levels": levels, "decay": decay, "bias": bias}
    for name in DIRECT:
        given[name] = a[name]
    return {name: np.ascontiguousarray(v) for name, v in given.items()}


DIRECT = ["x", "positions", "ada_w", "ret_w_in", "ret_w_out", "att_w_in", "att_w_out"] + DIRECT_2


def program(nc, given):
    ins = {name: nc.dram_tensor(f"in_{name}", list(v.shape), mybir.dt.from_np(v.dtype), kind="ExternalInput").ap()
           for name, v in given.items()}
    out = nc.dram_tensor("out", [1, S, D], F32, kind="ExternalOutput").ap()
    return ins, out


def kernel(**inputs):
    import numpy as np
    import concourse.bacc as bacc
    from concourse.bass_utils import run_bass_kernel_spmd

    given = lay_out(inputs)
    known = {}
    for _ in range(2):
        nc = bacc.Bacc("TRN2", target_bir_lowering=False, num_devices=1, dynamic_dma_scratch_size=1024)
        ins, out = program(nc, given)
        known = build(nc, ins, out, known)
    r = run_bass_kernel_spmd(nc, [{f"in_{name}": v for name, v in given.items()}], core_ids=[0])
    return r.results[0]["out"]
```

```python
from contextlib import ExitStack

import numpy as np

import concourse.bass as bass
from concourse import mybir

ALU = mybir.AluOpType
ACT = mybir.ActivationFunctionType
AX = mybir.AxisListType
F32 = mybir.dt.float32
F32R = mybir.dt.float32r
I32 = mybir.dt.int32

P = 128
D = 1024
S = 512
KT = D // P
NT = S // P
CHUNK = 64
EPS = 1e-6
NEG = -1e30

RH, RQK, RV = 4, 256, 512
AH, AD = 16, 128
GH, GD = 4, 128
DH, DD = 4, 64
TOPK = min(256, S // 4)
CONVW = 31
MEM = 256
XH, XD = 4, 128
DFF = 4 * D
GDN_TAPS = 4

RING = 4
UNIT = KT * P
RSQRT_MAGIC = float(0x5F3759DF)
NEWTON = 3
BEFORE = 128
TURN = 6.283185307179586
TURN_PARTS = (6.28125, 4058 / 2**21, TURN - 6.28125 - 4058 / 2**21)
ROUND = 12582912.0
PI_BELOW = 3.1415925
FINAL = 'mlp_out1'
DIRECT_2 = ['mem_2', 'w_in_2', 'dsa_w_qb_2', 'dsa_w_qi_2', 'dsa_w_kvb_2', 'w_out_2', 'xa_wq_2', 'xa_wkv_2', 'xa_wo_2', 'mlp_w1_2', 'mlp_w2_2']
REGION = 108 * 1024

UNITS = [
    ("ret", RH * 12), ("ret_out", 16), ("att", AH // 2 * 8), ("att_out", 16),
    ("mix", 24), ("mix_out", 8), ("xa_q", 4), ("xa_kv", 8), ("xa_out", 8),
    ("mlp_in0", 16), ("mlp_out0", 16), ("mlp_in1", 16), ("mlp_out1", 16),
]

SMALL_WIDTHS = [
    ("c", KT), ("norm_g0", KT), ("norm_g1", KT), ("ada_b0", 3 * KT), ("ada_b1", 3 * KT),
    ("ret_gn_g", 2 * KT), ("att_q_g", 1), ("att_k_g", 1), ("norm_mix", KT), ("norm_mem", KT),
    ("norm_cross", KT), ("norm_mlp", KT), ("gdn_conv", 12 * GDN_TAPS), ("gdn_a_log", GH),
    ("gdn_dt_bias", GH), ("gdn_norm", 1), ("dsa_q_norm", 1), ("dsa_k_norm", 1),
    ("conv_dw", 2 * CONVW), ("conv_dw_b", 2), ("conv_ln_g", 2), ("conv_ln_b", 2),
    ("xa_q_norm", 1), ("xa_k_norm", 1), ("inv_freq", 1),
]
SMALL = {}
_at = 0
for _name, _n in SMALL_WIDTHS:
    SMALL[_name] = (_at, _n)
    _at += _n
NSMALL = _at

LEVELS = 7
CONST = {"ident": (0, P), "causal": (P, P), "cumsum": (2 * P, P), "halves": (3 * P, 2)}
NCONST = 3 * P + 2


class Steps:

    def __init__(self, sem, known):
        self.sem, self.known, self.marks = sem, known, {}
        self.count, self.loop = BEFORE, None

    def done(self, name=None):
        self.count += 1
        if name is not None:
            self.marks[name] = (self.count, self.loop)
        return self.sem, 1

    def enter(self, loop, i, first=0):
        self.loop, self.start, self.i, self.first = loop, self.count, i, first

    def leave(self, turns):
        per = self.count - self.start
        self.marks["loop " + self.loop] = (per, self.start, self.first)
        self.count = self.start + turns * per
        self.loop = None

    def at(self, name, i=None):
        value, loop = self.known.get(name, (1, None))
        if loop is None:
            return self.sem, value
        per, start, first = self.known["loop " + loop]
        return self.sem, (i - first) * per + value

    def last(self):
        if self.loop is None:
            return self.sem, self.count
        per, start, first = self.known.get("loop " + self.loop, (0, 0, 0))
        return self.sem, (self.i - self.first) * per + self.count

    def after(self, name, turns):
        value, loop = self.known.get(name, (1, None))
        per, start, first = self.known.get("loop " + str(loop), (0, 0, 0))
        return self.sem, (turns - 1) * per + value


def build(nc, ins, out, known):
    ctx = ExitStack()
    with ctx:
        def sb(name, shape, dt=F32, where=ctx):
            return where.enter_context(nc.sbuf_tensor(name, shape, dt))

        def sem(name):
            return ctx.enter_context(nc.semaphore(name))

        xT = sb("xT", [P, KT, S])
        hh = sb("hh", [P, KT, S], F32R)
        hl = sb("hl", [P, KT, S], F32R)
        hn = nc.alloc_sbuf_tensor_at("hn", [P, KT, S], F32, offset=nc.sbuf_base - KT * S * 4)
        raw = sb("raw", [P, RING, KT, P])
        wh = sb("wh", [P, RING, KT, P], F32R)
        wl = sb("wl", [P, RING, KT, P], F32R)
        small = sb("small", [P, NSMALL])
        const = sb("const", [P, NCONST])
        ones = sb("ones", [P, P])
        mod = sb("mod", [P, 2, 3, KT])
        gain = sb("gain", [P, 2, KT])
        cond = sb("cond", [P, 2, KT])
        sq = sb("sq", [P, 2, S])
        rs = sb("rs", [P, 3, 32])
        dg = sb("dg", [P, S])
        qk_gain = sb("qk_gain", [P, 4])
        ident = const[:, 0:P]

        def sm(name, a=0, n=None):
            c, w = SMALL[name]
            return small[:, c + a:c + a + (w if n is None else n)]

        def cst(name, a=0, n=None):
            c, w = CONST[name]
            return const[:, c + a:c + a + (w if n is None else n)]

        acc = [ctx.enter_context(nc.psum_tensor(f"acc{b}", [P, S], F32)) for b in range(2)]
        sc = [ctx.enter_context(nc.psum_tensor(f"sc{b}", [P, S], F32)) for b in range(2)]
        ob = [ctx.enter_context(nc.psum_tensor(f"ob{b}", [P, S], F32)) for b in range(2)]
        st = ctx.enter_context(nc.psum_tensor("st", [P, S], F32))
        bc = ctx.enter_context(nc.psum_tensor("bc", [P, S], F32))

        raw_full = [sem(f"raw_full{s}") for s in range(RING)]
        high_done = sem("high_done")
        split_done = sem("split_done")
        unit_used = sem("unit_used")
        slot_free = sem("slot_free")
        small_in, const_in, x_in, pos_in = sem("small_in"), sem("const_in"), sem("x_in"), sem("pos_in")
        decay_in, bias_in, mem_in = sem("decay_in"), [sem("bias_in0"), sem("bias_in1")], sem("mem_in")
        ada_in = [sem(f"ada_in{k}") for k in range(KT)]
        small_w_in = sem("small_w_in")
        ada1_in = [sem("ada1_in0"), sem("ada1_in1")]
        out_done = sem("out_done")
        PE = Steps(sem("tensor_steps"), known.get("PE", {}))
        AC = Steps(sem("scalar_steps"), known.get("AC", {}))
        V = Steps(sem("vector_steps"), known.get("V", {}))
        G = Steps(sem("gpsimd_steps"), known.get("G", {}))


        base = sb("region", [P, REGION // 4])
        region = nc.sbuf_base - REGION

        def at(name, shape, offset, dt=F32):
            size = 4
            for n in shape[1:]:
                size *= n
            assert offset + size <= REGION, (name, offset + size)
            return nc.alloc_sbuf_tensor_at(name, shape, dt, offset=region + offset)

        KB = 1024
        Yh = at("Yh", [P, 16, S], 0, F32R)
        Yl = at("Yl", [P, 16, S], 32 * KB, F32R)
        W = 64 * KB
        ada_w0 = at("ada_w0", [P, KT, 2 * D], 0)
        ada_g0 = at("ada_g0", [P, KT, D], 0)
        x_tok = at("x_tok", [P, NT, D], W)
        ada_acc0 = at("ada_acc0", [P, 2 * D], W + 16 * KB)
        ada_accg = at("ada_accg", [P, D], W + 39 * KB)
        ada_acc1 = at("ada_acc1", [P, 3 * D], W)
        ada_w1 = at("ada_w1", [P, 2, 3 * D], W + 12 * KB)
        q_ = at("ret_q", [P, 2, S], W)
        k_ = at("ret_k", [P, 2, S], W + 4 * KB)
        v_ = at("ret_v", [P, NT, RV], W + 8 * KB)
        s_ = at("ret_gate", [P, 4, S], W + 16 * KB)
        t_ = at("ret_scores", [P, 10 * P], W + 24 * KB)
        tmp = at("ret_tmp", [P, 2, S], W + 29 * KB)
        dec = at("ret_decay", [P, S], W + 33 * KB)
        cos_ = at("cos", [P, S], W + 35 * KB)
        sin_ = at("sin", [P, S], W + 37 * KB)
        ang = at("ang", [P, S], W + 24 * KB)
        pos = at("pos", [P, S], W + 26 * KB, I32)
        o_ = [q_[:, 0, :], q_[:, 1, :], k_[:, 0, :], k_[:, 1, :]]
        aq = at("att_q", [P, 2, S], W)
        ak = at("att_k", [P, 2, S], W + 4 * KB)
        av = at("att_v", [P, NT, 2 * AD], W + 8 * KB)
        ag = at("att_gate", [P, 2, S], W + 12 * KB)
        aS = at("att_scores", [P, 2, 10 * P], W + 16 * KB)
        aP = at("att_probs_t", [P, 2, 10 * P], W + 26 * KB)
        ab = at("att_bias", [P, 2, S], W + 36 * KB)
        ay = at("att_y", [P, 2, S], W + 40 * KB)
        amax = sb("amax", [P, 3, 16])

        Mh = at("Mh", [P, KT, S], 0, F32R)
        Ml = at("Ml", [P, KT, S], 16 * KB, F32R)
        PAD = GDN_TAPS - 1
        GROW = PAD + S + 1
        GQ = 108 * KB - 8 * KB - 12 * GROW * 4
        gqkv_pad = at("gdn_qkv", [P, 12, GROW], GQ)
        gqkv = gqkv_pad[:, :, PAD:PAD + S]
        gz = at("gdn_gate", [P, 4, S], 100 * KB)
        cg = at("conv_gate", [P, 2, S], 100 * KB)
        co = at("conv_out", [P, 2, S], 65 * KB + 512)
        cy = at("conv_in", [P, 2, CONVW - 1 + S], 69 * KB + 512)
        kidx = at("dsa_kidx", [P, S], 32 * KB)
        dq = at("dsa_q", [P, 2, S], 34 * KB)
        dk = at("dsa_k", [P, S], 38 * KB)
        dv = at("dsa_v", [P, NT, DD], 40 * KB)
        work = at("dsa_work", [P, 9 * P], 41 * KB)
        dqi = at("dsa_qi", [P, 2, S], 45 * KB + 512)
        score = at("dsa_score", [P, 9 * P], 49 * KB + 512)
        cq = at("dsa_cq", [P, 2, S], 54 * KB)
        drelu = at("dsa_relu", [P, 2, S], 54 * KB)
        ckv = at("dsa_ckv", [P, S], 58 * KB)
        wqb = at("dsa_wqb", [P, 2, 256], 60 * KB)
        wqi = at("dsa_wqi", [P, 2, 256], 62 * KB)
        wkvb = at("dsa_wkvb", [P, 3 * DD], 64 * KB)
        dS = at("dsa_scores", [P, 2, 10 * P], 45 * KB + 512)
        dP = at("dsa_probs_t", [P, 2, 10 * P], 55 * KB + 512)
        gcv = at("gdn_conv", [P, 3, S], 65 * KB + 512)
        gth = at("gdn_tanh", [P, 2, S], 71 * KB + 512)
        gtap = [None, sq[:, 0, :], sq[:, 1, :], dg[:, :]]
        gktok = at("gdn_k_tok", [P, NT, GH, P], 32 * KB)
        gvtok = at("gdn_v_tok", [P, NT, GH, P], 40 * KB)
        gQKT = at("gdn_qk_t", [P, NT, GH, P], 48 * KB)
        gTT = at("gdn_inv_t", [P, NT, GH, P], 56 * KB)
        gT = at("gdn_inv", [P, NT, GH, P], GQ + 4 * GROW * 4)
        gAT = at("gdn_a_t", [P, NT, GH, P], GQ + 8 * GROW * 4)
        gwT = at("gdn_w_t", [P, NT, GH, P], GQ + 4 * GROW * 4)
        gkdec = at("gdn_k_dec", [P, NT, GH, P], GQ + 8 * GROW * 4)
        goT = at("gdn_o_t", [P, GH, S], 32 * KB)
        gG = at("gdn_g", [P, 2, GH, P], 64 * KB)
        ggb = at("gdn_g_rows", [P, 2, GH, P], 68 * KB)
        gA = sq[:, 0, :].rearrange("p (h n) -> p h n", h=GH)
        gQK = sq[:, 1, :].rearrange("p (h n) -> p h n", h=GH)
        gMT = at("gdn_level", [P, 2, GH, P], 64 * KB)
        gX = at("gdn_x", [P, 2, GH, P], 68 * KB)
        gvn = at("gdn_v_new", [P, 2, GH, P], 64 * KB)
        gst = at("gdn_state", [P, GH, P], 68 * KB)
        gkbe = at("gdn_kbe", [P, GH, P], 70 * KB)
        glev = at("gdn_levels", [P, LEVELS, P], 72 * KB)
        bankx = acc
        m_tok = at("mem_tok", [P, 2, D], 32 * KB)
        mT = at("mem_t", [P, KT, MEM], 40 * KB)
        mh = at("mem_high", [P, KT, MEM], 48 * KB, F32R)
        ml = at("mem_low", [P, KT, MEM], 56 * KB, F32R)
        mn = at("mem_normed", [P, KT, MEM], 56 * KB)
        xq = at("xa_q", [P, XH, S], 64 * KB)
        xk = at("xa_k", [P, XH, MEM], 72 * KB)
        xv = at("xa_v", [P, 2, XH * XD], 76 * KB)
        xS = at("xa_scores", [P, XH, NT, MEM], 80 * KB)
        xP = at("xa_probs_t", [P, 2, 2, S], 96 * KB)
        kidx_in, levels_in, dsa_w_in = sem("kidx_in"), sem("levels_in"), sem("dsa_w_in")
        tc = sb("tok_cols", [P, NT, 12])
        gc = sb("gdn_cols", [P, 10, 16])
        best = sb("best", [P, 3, 8])
        negs = sb("causal_negative", [P, P])
        strict = sb("strict", [P, P])

        QOFF = [0, 128, 384, 768]
        KOFF = [0, 512, 896, 1152]

        U = {}
        at_unit = 0
        for name, n in UNITS:
            U[name] = at_unit
            at_unit += n
        total_units = at_unit

        def rows(w, k0, k1, c0, n=P):
            return w[k0 * P:k1 * P, bass.ds(c0, n)].rearrange("(k p) n -> p k n", p=P)

        def product(e, bank, u, c, rhs_high, rhs_low, start=True, stop=True, k1=KT, inputs=None):
            s = c % RING
            e.wait_ge(split_done, u + 1)
            for k in range(k1):
                if inputs is not None:
                    e.wait_ge(*V.at(f"{inputs}h{k}"))
                e.matmul(bank[:, :], wh[:, s, k, :], rhs_high(k), start=(start and k == 0), stop=False)
                e.matmul(bank[:, :], wh[:, s, k, :], rhs_low(k), start=False, stop=False)
                last = e.matmul(bank[:, :], wl[:, s, k, :], rhs_high(k), start=False,
                                stop=(stop and k == k1 - 1))
            last.then_inc(unit_used, 1)

        def feat(e, bank, u, c, inputs=None):
            product(e, bank, u, c, lambda k: hh[:, k, :], lambda k: hl[:, k, :], inputs=inputs)

        def tok(e, u, c, tag, free, lh=hh, ll=hl, tiles=NT):
            s = c % RING
            assert s % 2 == 0
            e.wait_ge(split_done, u + 2)
            for t in range(tiles):
                if t % 2 == 0:
                    e.wait_ge(*free[t // 2])
                o = acc[t // 2][:, (t % 2) * 256:(t % 2 + 1) * 256].rearrange("p (a n) -> p a n", a=2)
                for k in range(KT):
                    h, l = lh[:, k, t * P:(t + 1) * P], ll[:, k, t * P:(t + 1) * P]
                    e.matmul(o, h, wh[:, s:s + 2, k, :], start=(k == 0), stop=False)
                    e.matmul(o, h, wl[:, s:s + 2, k, :], start=False, stop=False)
                    last = e.matmul(o, l, wh[:, s:s + 2, k, :], start=False, stop=(k == KT - 1))
                if t == tiles - 1:
                    last.then_inc(unit_used, 2)
                elif t % 2 == 1:
                    last.then_inc(*PE.done(tag))

        def columns(e, x, c0, start, stop, name=None, n=NT, parts=P, of=None):
            for t in range(n):
                last = e.matmul(st[:, c0 + t:c0 + t + 1], x[:, t * P:(t + 1) * P],
                                (ones if of is None else of)[0:parts, 0:1],
                                start=(start is True or (start == "first" and t == 0)),
                                stop=(stop is True or (stop == "last" and t == n - 1)))
            if name is not None:
                last.then_inc(*PE.done(name))

        def step(e, ins, steps, name=None):
            ins.then_inc(*steps.done(name))
            e.wait_ge(*steps.last())

        def rsqrt(e, n, scale, name=None, c0=0):
            y, x, z = rs[:, 0, 0:n], rs[:, 1, 0:n], rs[:, 2, 0:n]
            step(e, e.tensor_scalar(x, st[:, c0:c0 + n], scale, EPS, ALU.mult, ALU.add), V)
            step(e, e.tensor_scalar(y.bitcast(I32), x.bitcast(I32), 1, None, ALU.arith_shift_right), V)
            step(e, e.tensor_scalar(y.bitcast(I32), y.bitcast(I32), -1.0, RSQRT_MAGIC, ALU.mult, ALU.add), V)
            for r in range(NEWTON):
                step(e, e.tensor_tensor(z, y, y, ALU.mult), V)
                step(e, e.scalar_tensor_tensor(out=z, in0=z, scalar=-0.5, in1=x, op0=ALU.mult, op1=ALU.mult), V)
                step(e, e.scalar_tensor_tensor(out=y, in0=z, scalar=1.5, in1=y, op0=ALU.add, op1=ALU.mult), V,
                     name if r == NEWTON - 1 else None)

        def diagonal(e, c0, name, n=NT, buf=None):
            e.tensor_tensor((dg if buf is None else buf)[:, 0:n * P].rearrange("p (t n) -> p t n", t=n),
                            ident.unsqueeze(1).to_broadcast([P, n, P]),
                            rs[:, 0, c0:c0 + n].unsqueeze(2).to_broadcast([P, n, P]), ALU.mult)\
             .then_inc(*V.done(name))

        def spread(e, name, n=NT, buf=None, bank=None):
            e.matmul((bc if bank is None else bank)[:, 0:n * P], ones[:, :], (dg if buf is None else buf)[:, 0:n * P],
                     start=True, stop=True).then_inc(*PE.done(name))

        def squares(e, tag, ready, xin=None, n=S):
            for k in range(KT):
                e.wait_ge(*ready(k))
                if k >= 2:
                    e.wait_ge(*PE.at(f"{tag}cols{k - 2}"))
                e.activation(sq[:, k % 2, 0:n], (xT if xin is None else xin)[:, k, :], ACT.Square)\
                 .then_inc(*AC.done(f"{tag}sq{k}"))

        def square_sums(e, tag, nt=NT):
            for k in range(KT):
                e.wait_ge(*AC.at(f"{tag}sq{k}"))
                columns(e, sq[:, k % 2, :], 0, "first" if k == 0 else False,
                        "last" if k == KT - 1 else False, f"{tag}cols{k}", n=nt)

        def stream_sums(e, tag, ready):
            e.wait_ge(*ready)
            columns(e, dg, 0, "first", "last", f"{tag}cols{KT - 1}")

        def norm_spread(e, tag, nt=NT):
            e.wait_ge(*V.at(f"{tag}diag"))
            spread(e, f"{tag}bc", nt)

        def norm_roots(e, tag, n=S):
            e.wait_ge(*PE.at(f"{tag}cols{KT - 1}"))
            rsqrt(e, n // P, 1.0 / D)
            diagonal(e, 0, f"{tag}diag", n // P)

        def norm_vector(e, tag, g, bias=None, xin=None, normed=None, hhi=None, hlo=None, n=S):
            xin, normed, hhi, hlo = (xT, hn, hh, hl) if xin is None else (xin, normed, hhi, hlo)
            e.wait_ge(*PE.at(f"{tag}bc"))

            def rest(k):
                e.wait_ge(*AC.at(f"{tag}hi{k}"))
                x, high = normed[:, k, :], hhi[:, k, :].bitcast(F32)
                if bias is None:
                    e.tensor_tensor(hlo[:, k, :], x, high, ALU.subtract).then_inc(*V.done(f"{tag}h{k}"))
                else:
                    e.scalar_tensor_tensor(out=hlo[:, k, :], in0=x, scalar=bias(k), in1=high,
                                           op0=ALU.add, op1=ALU.subtract).then_inc(*V.done(f"{tag}h{k}"))

            for k in range(KT):
                e.scalar_tensor_tensor(out=normed[:, k, :], in0=xin[:, k, :], scalar=g(k), in1=bc[:, 0:n],
                                       op0=ALU.mult, op1=ALU.mult).then_inc(*V.done(f"{tag}t{k}"))
                if k >= 2:
                    rest(k - 2)
            rest(KT - 2)
            rest(KT - 1)

        def norm_highs(e, tag, bias=None, normed=None, hhi=None):
            for k in range(KT):
                e.wait_ge(*V.at(f"{tag}t{k}"))
                x = (hn if normed is None else normed)[:, k, :]
                out_ = (hh if hhi is None else hhi)[:, k, :]
                if bias is None:
                    e.activation(out_, x, ACT.Copy).then_inc(*AC.done(f"{tag}hi{k}"))
                else:
                    e.activation(out_, x, ACT.Identity, bias=bias(k)).then_inc(*AC.done(f"{tag}hi{k}"))

        def out_squares(e, tag, turns, tiles, before=None):
            with e.Fori(0, turns) as i:
                AC.enter(f"{tag}_squares", i)
                if before is not None:
                    before(e, i)
                for b in range(tiles):
                    e.wait_ge(*V.at(f"{tag}x{b}", i))
                    e.activation(sq[:, b % 2, :].unsqueeze(1), xT[:, bass.ds(i * tiles + b, 1), :], ACT.Square)\
                     .then_inc(*AC.done(f"{tag}sq{b}"))
                AC.leave(turns)

        def add_squares(e, tag, b, i):
            e.wait_ge(*AC.at(f"{tag}sq{b}", i))
            e.wait_ge(*V.last())
            e.tensor_tensor(dg[:, :], dg[:, :], sq[:, b % 2, :], ALU.add).then_inc(*V.done(f"{tag}ss{b}"))

        def out_tensor(e, tag, ready):
            c = U[tag]
            e.wait_ge(*ready)
            with e.Fori(0, KT // 2) as i:
                PE.enter(tag, i)
                for b in range(2):
                    e.wait_ge(*V.at(f"{tag}x{b}", i - 1))
                    for half in range(2):
                        product(e, acc[b], c + i * 4 + 2 * b + half, c + 2 * b + half,
                                lambda k: Yh[:, 8 * half + k, :], lambda k: Yl[:, 8 * half + k, :],
                                start=(half == 0), stop=(half == 1))
                PE.leave(KT // 2)

        def out_vector(e, tag, gate, between=None, sums=True):
            c = U[tag]
            if sums:
                step(e, e.memset(dg[:, :], 0.0), V)
            with e.Fori(0, KT // 2) as i:
                V.enter(tag, i)
                for b in range(2):
                    x = xT[:, bass.ds(i * 2 + b, 1), :]
                    p = acc[b][:, :].unsqueeze(1)
                    e.wait_ge(unit_used, c + i * 4 + 2 * b + 2)
                    if gate is None:
                        e.tensor_tensor(x, p, x, ALU.add).then_inc(*V.done(f"{tag}x{b}"))
                    else:
                        e.scalar_tensor_tensor(out=x, in0=p, scalar=gate(i * 2 + b), in1=x,
                                               op0=ALU.mult, op1=ALU.add).then_inc(*V.done(f"{tag}x{b}"))
                    if sums:
                        add_squares(e, tag, b, i)
                    if between is not None:
                        between(e, i, b)
                V.leave(KT // 2)

        def ada_sum(e, accum, w, k, name=None):
            if k == 0:
                step(e, e.tensor_scalar(accum, w, cond[:, 0, 0:1], None, ALU.mult), V, name)
            else:
                step(e, e.scalar_tensor_tensor(out=accum, in0=w, scalar=cond[:, 0, k:k + 1], in1=accum,
                                               op0=ALU.mult, op1=ALU.add), V, name)

        def ada_columns(e, accum, n0, n1, name):
            for n in range(n0, n1):
                last = e.matmul(st[:, n:n + 1], accum[:, (n - n0) * P:(n - n0 + 1) * P], ones[:, 0:1], start=True, stop=True)
            last.then_inc(*PE.done(name))

        def count_from(e, steps):
            e.sem_inc(steps.sem, BEFORE)

        block = ctx.enter_context(nc.Block())

        @block.sync
        def _(e):
            def load(u, c, turn, src, k1=KT, n=P, col=0, k0=0):
                s = c % RING
                if c >= RING or not isinstance(turn, int):
                    e.wait_ge(split_done, u - RING + 1)
                e.dma_start(raw[:, s, k0:k1, col:col + n], src).then_inc(raw_full[s], 16)

            for k in range(KT):
                e.dma_start(ada_w0[:, k, :], ins["ada_w"][0, k * P:(k + 1) * P, 0:2 * D]).then_inc(ada_in[k], 16)

            w = ins["ret_w_in"][0]
            columns_of = [(0, RQK, 0), (0, RQK, 1), (1, RQK, 0), (1, RQK, 1),
                          (2, RV, 0), (2, RV, 1), (2, RV, 2), (2, RV, 3),
                          (3, RV, 0), (3, RV, 1), (3, RV, 2), (3, RV, 3)]
            first = [0, D, 2 * D, 4 * D]

            def load_ret(i, js):
                for j in js:
                    part, width, tile = columns_of[j]
                    c = U["ret"] + j
                    load(c + i * 12, c, i, rows(w, 0, KT, first[part] + i * width + tile * P))

            load_ret(0, range(4))
            load_ret(0, range(4, 6))
            e.wait_ge(*V.at("ada0sum"))
            for k in range(KT):
                e.dma_start(ada_g0[:, k, :], ins["ada_w"][0, k * P:(k + 1) * P, 2 * D:3 * D]).then_inc(ada_in[k], 16)
            load_ret(0, range(6, 12))
            with e.Fori(1, RH) as i:
                load_ret(i, range(12))

            def load_out(name, w, r0=0):
                with e.Fori(0, KT // 2) as i:
                    for j in range(4):
                        c = U[name] + j
                        k0 = r0 + 8 * (j % 2)
                        load(c + i * 4, c, i, rows(w, k0, k0 + 8, (i * 2 + j // 2) * P))

            load_out("ret_out", ins["ret_w_out"][0])

            w1 = ins["att_w_in"][0]
            with e.Fori(0, AH // 2) as i:
                for j in range(8):
                    c = U["att"] + j
                    load(c + i * 8, c, i, rows(w1, 0, KT, (j // 2) * AH * AD + (i * 2 + j % 2) * AD))
            load_out("att_out", ins["att_w_out"][0])
            wm = ins["w_in_2"][0]

            def load_mix(j, c0):
                load(U["mix"] + j, U["mix"] + j, 0, wm[:, c0:c0 + P].rearrange("(k p) n -> p k n", p=P))

            for j, c0 in enumerate((2764, 2508, 2892, 2636, None, 2056, 2056 + P, 2312)):
                if c0 is None:
                    load(U["mix"] + j, U["mix"] + j, 0, rows(ins["w_small"], 0, KT, 0))
                else:
                    load_mix(j, c0)
            for j in range(16):
                load_mix(8 + j, j * P)

            def load_flat(name, w, k1, turns):
                with e.Fori(0, turns) as i:
                    for j in range(4):
                        c = U[name] + j
                        load(c + i * 4, c, i, rows(w, 0, k1, (i * 4 + j) * P), k1=k1)

            load_flat("mix_out", ins["w_out_2"][0], KT, 2)
            load_flat("xa_q", ins["xa_wq_2"][0], KT, 1)
            load_flat("xa_kv", ins["xa_wkv_2"][0], KT, 2)
            load_flat("xa_out", ins["xa_wo_2"][0], 4, 2)
            for half in range(2):
                w = ins["mlp_w1_2"][0][:, half * 2048:(half + 1) * 2048]
                load_flat(f"mlp_in{half}", w, KT, 4)
                load_out(f"mlp_out{half}", ins["mlp_w2_2"][0], 16 * half)
            e.wait_ge(*AC.at("out_copied"))
            e.dma_start(out.rearrange("b (t p) d -> p (b t) d", p=P), x_tok[:, :, :]).then_inc(out_done, 16)
            e.wait_ge(out_done, 16)

        @block.gpsimd
        def _(e):
            def split(s, turn):
                u = turn * RING + s
                e.wait_ge(raw_full[s], turn * 16 + 16)
                if not isinstance(turn, int):
                    e.wait_ge(unit_used, u - RING + 1)
                    e.sem_inc(slot_free, 1)
                e.tensor_scalar(wh[:, s, :, :], raw[:, s, :, :], 1.0, 1.0, ALU.mult, ALU.mult).then_inc(high_done, 1)
                e.wait_ge(high_done, u + 1)
                e.tensor_tensor(wl[:, s, :, :], raw[:, s, :, :], wh[:, s, :, :].bitcast(F32), ALU.subtract)\
                 .then_inc(split_done, 1)

            def split_turns(first, end):
                with e.Fori(first, end) as i:
                    for s in range(RING):
                        split(s, i)

            count_from(e, G)
            for s in range(RING):
                split(s, 0)
            split_turns(1, U["mix_out"] // RING)
            def silu(j):
                e.wait_ge(*AC.at(f"g_th{j}"))
                e.tensor_tensor(gqkv[:, j, :], gth[:, j % 2, :], gcv[:, j % 3, :], ALU.mult)\
                 .then_inc(*G.done(f"g_silu{j}"))

            for j in range(12):
                c = gcv[:, j % 3, :]
                for k in range(1, GDN_TAPS):
                    e.wait_ge(*AC.at(f"g_tap{j}{k}"))
                    if k > 1:
                        e.wait_ge(*G.at(f"g_add{j}{k - 1}"))
                    e.tensor_tensor(c, c, gtap[k], ALU.add).then_inc(*G.done(f"g_add{j}{k}"))
                if j:
                    silu(j - 1)
            silu(11)
            def every(x):
                return x.unsqueeze(1).to_broadcast([P, GH, P])

            for t in range(NT):
                q = gqkv[:, 0:GH, t * P:(t + 1) * P]
                e.wait_ge(*AC.at(f"g_eD{t}"))
                e.wait_ge(*PE.at(f"g_qk{t}"))
                e.tensor_tensor(q, q, ggb[:, t % 2, :, :], ALU.mult).then_inc(*G.done(f"g_qe{t}"))
                e.wait_ge(*AC.at(f"g_ATc{t}"))
                if t == 0:
                    e.wait_ge(levels_in, 16)
                step(e, e.tensor_tensor(gTT[:, t, :, :], gAT[:, t, :, :], every(glev[:, 0, :]), ALU.mult), G)
                step(e, e.tensor_tensor(gTT[:, t, :, :], every(ident), gTT[:, t, :, :], ALU.subtract), G, f"g_TT0{t}")
            split_turns(U["mix_out"] // RING, total_units // RING)

        @block.scalar
        def _(e):
            count_from(e, AC)
            e.dma_start(small[:, :], ins["small"]).then_inc(small_in, 16)
            e.dma_start(const[:, :], ins["const"]).then_inc(const_in, 16)
            e.dma_start(x_tok[:, :, :], ins["x"].rearrange("b (t p) d -> p (b t) d", p=P)).then_inc(x_in, 16)
            e.dma_start(pos[:, :], ins["positions"].to_broadcast([P, S])).then_inc(pos_in, 16)
            e.dma_start(dec[:, :], ins["decay"][0]).then_inc(decay_in, 16)
            e.wait_ge(small_in, 16)
            e.activation(cond[:, 1, :], sm("c"), ACT.Tanh, scale=0.5).then_inc(*AC.done("cond_tanh"))
            for k in range(KT):
                e.wait_ge(*PE.at(f"x{k}"))
                e.activation(xT[:, k, :], ob[k % 2][:, :], ACT.Copy).then_inc(*AC.done(f"x{k}"))
            squares(e, "n0", lambda k: AC.at(f"x{k}"))
            norm_highs(e, "n0", lambda k: mod[:, 0, 0, k:k + 1])
            e.wait_ge(*V.at("angles"))
            e.activation(sin_[:, :], ang[:, :], ACT.Sin).then_inc(*AC.done())
            e.activation(cos_[:, :], tmp[:, 1, :], ACT.Sin).then_inc(*AC.done("rope"))

            with e.Fori(0, RH) as i:
                AC.enter("ret_scalar", i)
                c = U["ret"] + i * 12
                e.wait_ge(*V.at("r_yl3", i - 1))
                for j, dst in enumerate((q_[:, 0, :], q_[:, 1, :], k_[:, 0, :], k_[:, 1, :])):
                    e.wait_ge(unit_used, c + j + 1)
                    e.activation(dst, acc[j % 2][:, :], ACT.Copy).then_inc(*AC.done(f"r_qk{j}"))
                for n in range(2):
                    for b in range(2):
                        if b == 0:
                            e.wait_ge(*PE.at(f"r_v{n}", i))
                        else:
                            e.wait_ge(unit_used, c + 6 + 2 * n)
                        e.activation(v_[:, 2 * b:2 * b + 2, n * 256:(n + 1) * 256],
                                     acc[b][:, :].rearrange("p (t n) -> p t n", t=2), ACT.Copy)\
                         .then_inc(*AC.done(f"r_v{n}{b}"))

                def gate(n):
                    e.wait_ge(unit_used, c + 9 + n)
                    e.activation(s_[:, n, :], acc[n % 2][:, :], ACT.Tanh, scale=0.5).then_inc(*AC.done(f"r_th{n}"))

                gate(0)
                gate(1)
                for n in range(4):
                    e.wait_ge(*PE.at(f"r_o{n}", i))
                    if n >= 2:
                        e.wait_ge(*PE.at(f"r_cols{n - 2}", i))
                    e.activation(sq[:, n % 2, :], ob[n % 2][:, :], ACT.Square).then_inc(*AC.done(f"r_sq{n}"))
                    e.activation(o_[n], ob[n % 2][:, :], ACT.Copy).then_inc(*AC.done(f"r_oc{n}"))
                gate(2)
                gate(3)
                for n in range(4):
                    e.wait_ge(*V.at(f"r_y{n}", i))
                    e.activation(Yh[:, bass.ds(i * 4 + n, 1), :], o_[n].unsqueeze(1), ACT.Copy)\
                     .then_inc(*AC.done(f"r_yh{n}"))
                e.wait_ge(*V.at("r_s3", i))
                e.dma_start(dec[:, :], ins["decay"][bass.ds(i + 1, 1)].rearrange("o p n -> (o p) n"))\
                 .then_inc(decay_in, 16)
                AC.leave(RH)

            e.wait_ge(*V.after("r_yl3", RH))
            e.wait_ge(decay_in, 16 * (RH + 1))

            def load_ada1(e, i):
                for b in range(2):
                    e.wait_ge(*V.at(f"ada1sum{b}", i - 1))
                    e.dma_start(ada_w1[:, b, :], ins["ada_w"][1, bass.ds((i * 2 + b) * P, P), :])\
                     .then_inc(ada1_in[b], 16)

            out_squares(e, "ret_out", KT // 2, 2, load_ada1)
            norm_highs(e, "n1", lambda k: mod[:, 1, 0, k:k + 1])

            def load_bias(h, head):
                for p0, p1, m in ((0, CHUNK, S - CHUNK), (CHUNK, P, S)):
                    e.dma_start(ab[p0:p1, h, 0:m],
                                ins["bias"][bass.ds(head, 1), p0:p1, 0:m].rearrange("o p n -> (o p) n"))\
                     .then_inc(bias_in[h], 16)

            def att_qk(i, t, prev):
                c = U["att"] + i * 8
                for j in range(4):
                    dst = (aq, ak)[j // 2][:, j % 2, :]
                    e.wait_ge(unit_used, c + j + 1)
                    if j >= 2:
                        e.wait_ge(*PE.at(f"{t}cols{j - 2}", i))
                    e.activation(sq[:, j % 2, :], acc[j % 2][:, :], ACT.Square).then_inc(*AC.done(f"{t}sq{j}"))
                    e.activation(dst, acc[j % 2][:, :], ACT.Copy,
                                 scale=(qk_gain[:, 0:1] if j < 2 else 1.0)).then_inc(*AC.done(f"{t}qk{j}"))

            def att_vg(i, t):
                c = U["att"] + i * 8
                for b in range(2):
                    e.wait_ge(*(PE.at(f"{t}v", i) if b == 0 else (unit_used, c + 6)))
                    e.activation(av[:, 2 * b:2 * b + 2, :], acc[b][:, :].rearrange("p (t n) -> p t n", t=2),
                                 ACT.Copy).then_inc(*AC.done(f"{t}v{b}"))
                for h in range(2):
                    e.wait_ge(unit_used, c + 7 + h)
                    e.activation(ag[:, h, :], acc[h][:, :], ACT.Tanh, scale=0.5).then_inc(*AC.done(f"{t}th{h}"))
                for h in range(2):
                    e.wait_ge(*V.at(f"{t}nm{h}", i))
                    for n in range(NT):
                        x = aS[:, h, QOFF[n]:QOFF[n] + (n + 1) * P]
                        r = h * 4 + n
                        e.activation(x, x, ACT.Exp, bias=amax[:, 0, r:r + 1], accum_out=amax[:, 1, r:r + 1])\
                         .then_inc(*AC.done(f"{t}exp{h}{n}"))
                    load_bias(h, i * 2 + 2 + h)

            def att_pv(pair, i, t, w):
                for h in range(2):
                    for n in range(NT):
                        e.wait_ge(*PE.at(f"{t}pt{h}{n}", i))
                        e.activation(aP[:, h, KOFF[n]:KOFF[n] + (NT - n) * P], sc[n % 2][:, 0:(NT - n) * P],
                                     ACT.Copy).then_inc(*AC.done(f"{t}pt{h}{n}"))
                for h in range(2):
                    e.wait_ge(*V.at(f"{t}y{h}", i))
                    e.activation(Yh[:, bass.ds(pair * 2 + h, 1), :], ay[:, h, :].unsqueeze(1), ACT.Copy)\
                     .then_inc(*AC.done(f"{t}yh{h}"))

            e.wait_ge(*V.at("n1t0"))
            e.wait_ge(*V.at("mask"))
            for h in range(2):
                load_bias(h, h)
            att_qk(0, "p", None)
            att_vg(0, "p")
            with e.Fori(1, AH // 2) as i:
                AC.enter("att_scalar", i, 1)
                att_qk(i, "a", None)
                att_pv(i - 1, i, "a", None)
                att_vg(i, "a")
                AC.leave(AH // 2 - 1)
            att_pv(AH // 2 - 1, 0, "z", None)
            for h in range(2):
                e.wait_ge(bias_in[h], 32 * (AH // 2 + 1))
            out_squares(e, "att_out", KT // 2, 2)
            norm_highs(e, "nm")

            e.dma_start(wqb[:, :, :], ins["dsa_w_qb_2"][0].rearrange("(k p) n -> p k n", p=P)).then_inc(dsa_w_in, 16)
            e.dma_start(wqi[:, :, :], ins["dsa_w_qi_2"][0].rearrange("(k p) n -> p k n", p=P)).then_inc(dsa_w_in, 16)
            for a, b in ((0, 0), (DD, 0), (2 * DD, DD)):
                e.dma_start(wkvb[:, a:a + DD], ins["dsa_w_kvb_2"][0][:, b:b + DD]).then_inc(dsa_w_in, 16)
            for j in range(2):
                e.wait_ge(unit_used, U["mix"] + 2 * j + 1)
                e.activation(cg[:, j, :], acc[0][:, :], ACT.Tanh, scale=0.5).then_inc(*AC.done(f"c_th{j}"))

            e.wait_ge(unit_used, U["mix"] + 5)
            e.activation(sq[:, 0, :], acc[0][:, :], ACT.Copy).then_inc(*AC.done("d_small"))
            e.activation(kidx[0:DD, :], acc[0][0:DD, :], ACT.Copy).then_inc(*AC.done("d_kidx"))
            e.wait_ge(*AC.at("d_kidx"))
            e.dma_start(kidx[DD:P, :], kidx[0:DD, :]).then_inc(kidx_in, 16)
            for j, dst in enumerate((cq[:, 0, :], cq[:, 1, :], ckv[:, :])):
                e.wait_ge(unit_used, U["mix"] + 6 + j)
                e.activation(dst, acc[(j + 1) % 2][:, :], ACT.Copy).then_inc(*AC.done(f"d_c{j}"))
                if j == 0:
                    e.wait_ge(*PE.at("d_small_t"))
                    e.activation(tc[:, :, :], ob[0][:, :].rearrange("p (t n) -> p t n", t=NT)[:, :, DD:DD + 12],
                                 ACT.Copy).then_inc(*AC.done("tc"))
            for j in range(2):
                e.wait_ge(*PE.at(f"d_q{j}"))
                e.activation(sq[:, j, :], ob[j][:, :], ACT.Square).then_inc(*AC.done(f"d_sq{j}"))
                e.activation(dq[:, j, :], ob[j][:, :], ACT.Copy, scale=qk_gain[:, 1:2]).then_inc(*AC.done(f"d_qc{j}"))
            e.wait_ge(*PE.at("d_k"))
            e.wait_ge(*PE.at("d_cols0"))
            e.activation(sq[:, 0, :], sc[0][:, :], ACT.Square).then_inc(*AC.done("d_sq2"))
            e.activation(dk[:, :], sc[0][:, :], ACT.Copy).then_inc(*AC.done("d_kc"))
            e.wait_ge(*PE.at("d_v"))
            e.activation(dv[:, :, :], sc[1][:, 0:NT * DD].rearrange("p (t n) -> p t n", t=NT), ACT.Copy)\
             .then_inc(*AC.done("d_vc"))
            for j in range(2):
                e.wait_ge(*PE.at(f"d_qi{j}"))
                e.activation(dqi[:, j, :], ob[j][:, :], ACT.Copy).then_inc(*AC.done(f"d_qic{j}"))

            def gdn_raw(e, j):
                dst = gqkv[:, j, :] if j < 12 else gz[:, j - 12, :]
                e.wait_ge(unit_used, U["mix"] + 9 + j)
                e.activation(dst, acc[j % 2][:, :], ACT.Copy).then_inc(*AC.done(f"g_raw{j}"))

            for j in range(3):
                gdn_raw(e, j)
            e.wait_ge(*V.at("c_centered"))
            e.wait_ge(*PE.at("d_cols2"))
            for j in range(2):
                e.activation(sq[:, j, :], co[:, j, :], ACT.Square).then_inc(*AC.done(f"c_sq{j}"))
            gdn_raw(e, 3)
            gdn_raw(e, 4)
            for j in range(2):
                e.wait_ge(*V.at(f"c_t{j}"))
                step(e, e.activation(co[:, j, :], co[:, j, :], ACT.Identity, bias=sm("conv_ln_b", j, 1)), AC)
                e.activation(cg[:, j, :], co[:, j, :], ACT.Tanh, scale=0.5).then_inc(*AC.done(f"c_sth{j}"))
            gdn_raw(e, 5)
            for j in range(2):
                e.wait_ge(*V.at(f"c_y{j}"))
                e.activation(Mh[:, 6 + j, :], co[:, j, :], ACT.Copy, scale=0.5).then_inc(*AC.done(f"c_hi{j}"))
            for m in range(6):
                gdn_raw(e, 6 + m)
                for n in (2 * m, 2 * m + 1):
                    w_ = (n // DH + 2) * P
                    e.wait_ge(*PE.at(f"d_idx{n}"))
                    if n >= 2:
                        e.wait_ge(*V.at(f"d_sum{n - 2}"))
                    e.activation(drelu[:, n % 2, 0:w_], sc[n % 2][:, 0:w_], ACT.Relu).then_inc(*AC.done(f"d_relu{n}"))
            w0 = SMALL["gdn_conv"][0]

            def gdn_taps(e, *js):
                for j in js:
                    for k in range(GDN_TAPS if j < 12 else 0):
                        if k == 0:
                            if j >= 3:
                                e.wait_ge(*G.at(f"g_silu{j - 3}"))
                        elif j:
                            e.wait_ge(*G.at(f"g_add{j - 1}{k}"))
                        w_ = small[:, w0 + j * GDN_TAPS + k:w0 + j * GDN_TAPS + k + 1]
                        e.activation(gtap[k] if k else gcv[:, j % 3, :], gqkv_pad[:, j, k:k + S], ACT.Copy, scale=w_)\
                         .then_inc(*AC.done(f"g_tap{j}{k}"))
                    if j:
                        b = j - 1
                        e.wait_ge(*G.at(f"g_add{b}{GDN_TAPS - 1}"))
                        if b >= 2:
                            e.wait_ge(*G.at(f"g_silu{b - 2}"))
                        step(e, e.activation(gth[:, b % 2, :], gcv[:, b % 3, :], ACT.Tanh, scale=0.5), AC)
                        e.activation(gth[:, b % 2, :], gth[:, b % 2, :], ACT.Identity, bias=ones[:, 0:1])\
                         .then_inc(*AC.done(f"g_th{b}"))

            e.wait_ge(*V.at("c_lo1"))
            e.wait_ge(*V.at("d_kn"))
            for j in range(12, 16):
                gdn_raw(e, j)
                gdn_taps(e, j - 12)
            gdn_taps(e, 4, 5, 6, 7, 8, 9)

            e.activation(gc[:, 0, 0:GH], sm("gdn_a_log"), ACT.Exp).then_inc(*AC.done("g_ea"))
            e.wait_ge(*V.at("g_abs"))
            e.activation(gc[:, 2, :], gc[:, 2, :], ACT.Exp, scale=-1.0).then_inc(*AC.done("g_ex"))
            e.wait_ge(*AC.at("tc"))
            e.activation(gc[:, 3, :].rearrange("p (t h) -> p t h", t=NT), tc[:, :, 8:12], ACT.Tanh, scale=0.5)\
             .then_inc(*AC.done("g_bth"))
            e.wait_ge(*V.at("g_1p"))
            e.activation(gc[:, 2, :], gc[:, 2, :], ACT.Ln).then_inc(*AC.done("g_ln"))

            for g in range(2):
                for h in range(2):
                    for n in range(NT):
                        r = h * 4 + n
                        x = dS[:, h, QOFF[n]:QOFF[n] + (n + 1) * P]
                        e.wait_ge(*V.at(f"d_nm{g}{h}"))
                        e.activation(x, x, ACT.Exp, bias=amax[:, 0, r:r + 1], accum_out=amax[:, 1, r:r + 1])\
                         .then_inc(*AC.done(f"d_exp{g}{h}{n}"))
                if g == 0:
                    gdn_taps(e, 10)
                for h in range(2):
                    for n in range(NT):
                        e.wait_ge(*PE.at(f"d_pt{g}{h}{n}"))
                        e.activation(dP[:, h, KOFF[n]:KOFF[n] + (NT - n) * P], sc[n % 2][:, 0:(NT - n) * P],
                                     ACT.Copy).then_inc(*AC.done(f"d_ptc{g}{h}{n}"))
                if g == 0:
                    gdn_taps(e, 11, 12)
                e.wait_ge(*PE.at(f"d_o{g}"))
                e.activation(Mh[:, 4 + g, :], ob[g][:, :], ACT.Copy).then_inc(*AC.done(f"d_hi{g}"))

            for j in range(4):
                e.wait_ge(*(V.at(f"g_z{j - 2}") if j >= 2 else G.at(f"g_silu{10 + j}")))
                e.activation(gth[:, j % 2, :], gz[:, j, :], ACT.Tanh, scale=0.5).then_inc(*AC.done(f"g_zth{j}"))
            e.wait_ge(*V.at("g_z3"))
            e.dma_start(glev[:, :, :], ins["levels"].rearrange("p (l n) -> p l n", l=LEVELS)).then_inc(levels_in, 16)
            for j in range(8):
                e.wait_ge(*G.at(f"g_silu{j}"))
                if j >= 2:
                    e.wait_ge(*PE.at(f"g_cols{j - 2}"))
                e.activation(sq[:, j % 2, :], gqkv[:, j, :], ACT.Square).then_inc(*AC.done(f"g_sq{j}"))
            e.wait_ge(*PE.at("g_dl"))
            e.activation(gc[:, 6, :], st[:, 0:16], ACT.Copy).then_inc(*AC.done("g_d"))
            e.activation(gc[:, 7, :], st[:, 0:16], ACT.Exp).then_inc(*AC.done("g_ed"))
            e.activation(gc[:, 9, :], st[:, 16:32], ACT.Exp).then_inc(*AC.done("g_el"))
            e.wait_ge(*V.at("g_dld"))
            e.activation(gc[:, 8, :], gc[:, 8, :], ACT.Exp).then_inc(*AC.done("g_kd"))
            for t in range(NT):
                for a, (name, dst) in enumerate((("k", gktok), ("v", gvtok))):
                    e.wait_ge(*PE.at(f"g_{name}tok{t}"))
                    e.activation(dst[:, t, :, :], sc[a][:, :].rearrange("p (h n) -> p h n", h=GH), ACT.Copy)\
                     .then_inc(*AC.done(f"g_{name}tokc{t}"))
            def gdn_decay(t):
                e.wait_ge(*V.at(f"g_diff{t}"))
                e.activation(gG[:, t % 2, :, :], gG[:, t % 2, :, :], ACT.Exp).then_inc(*AC.done(f"g_G{t}"))
                e.activation(ggb[:, t % 2, :, :], ob[t % 2][:, :].rearrange("p (h n) -> p h n", h=GH), ACT.Exp)\
                 .then_inc(*AC.done(f"g_eD{t}"))

            gdn_decay(0)
            for t in range(NT):
                e.wait_ge(*PE.at(f"g_AT{t}"))
                e.activation(gAT[:, t, :, :], acc[0][:, :].rearrange("p (h n) -> p h n", h=GH), ACT.Copy)\
                 .then_inc(*AC.done(f"g_ATc{t}"))
                e.wait_ge(*PE.at(f"g_QKT{t}"))
                e.activation(gQKT[:, t, :, :], acc[1][:, :].rearrange("p (h n) -> p h n", h=GH), ACT.Copy)\
                 .then_inc(*AC.done(f"g_QKTc{t}"))
                if t < NT - 1:
                    gdn_decay(t + 1)
            for t in range(NT):
                e.wait_ge(*PE.at(f"g_T0{t}"))
                e.activation(gT[:, t, :, :], sc[t % 2][:, :].rearrange("p (h n) -> p h n", h=GH), ACT.Copy)\
                 .then_inc(*AC.done(f"g_Tc{t}"))
            for l in range(1, LEVELS):
                for t in range(NT):
                    e.wait_ge(*PE.at(f"g_X{l}{t}"))
                    e.activation(gX[:, t % 2, :, :], sc[t % 2][:, :].rearrange("p (h n) -> p h n", h=GH), ACT.Copy)\
                     .then_inc(*AC.done(f"g_Xc{l}{t}"))
            for t in range(NT):
                e.wait_ge(*PE.at(f"g_w{t}"))
                e.activation(gwT[:, t, :, :], acc[t % 2][:, :].rearrange("p (h n) -> p h n", h=GH), ACT.Copy,
                             scale=-1.0).then_inc(*AC.done(f"g_wc{t}"))
            for t in range(NT):
                e.wait_ge(*PE.at(f"g_vn{t}"))
                e.activation(gvn[:, t % 2, :, :], ob[t % 2][:, :].rearrange("p (h n) -> p h n", h=GH), ACT.Copy)\
                 .then_inc(*AC.done(f"g_vnc{t}"))
                e.wait_ge(*PE.at(f"g_o{t}"))
                e.activation(goT[:, :, t * P:(t + 1) * P], sc[t % 2][:, :].rearrange("p (h n) -> p h n", h=GH),
                             ACT.Copy).then_inc(*AC.done(f"g_oc{t}"))
            e.wait_ge(*AC.last())
            for h in range(GH):
                if h >= 2:
                    e.wait_ge(*PE.at(f"g_ocols{h - 2}"))
                e.activation(sq[:, h % 2, :], goT[:, h, :], ACT.Square).then_inc(*AC.done(f"g_osq{h}"))
            for h in range(GH):
                e.wait_ge(*V.at(f"g_y{h}"))
                e.activation(Mh[:, h, :], goT[:, h, :], ACT.Copy).then_inc(*AC.done(f"g_hi{h}"))

            e.wait_ge(*V.at(f"g_lo{GH - 1}"))
            e.dma_start(m_tok[:, :, :], ins["mem_2"].rearrange("b (t p) d -> p (b t) d", p=P)).then_inc(mem_in, 16)
            out_squares(e, "mix_out", 2, 4)
            for k in range(KT):
                e.wait_ge(*PE.at(f"m{k}"))
                e.activation(mT[:, k, :], ob[k % 2][:, 0:MEM], ACT.Copy).then_inc(*AC.done(f"m{k}"))
            norm_highs(e, "nx")
            squares(e, "nk", lambda k: AC.at(f"m{k}"), mT, MEM)
            for h in range(XH):
                if h == 0:
                    e.wait_ge(*PE.at(f"nkcols{KT - 1}"))
                if h == 2:
                    norm_highs(e, "nk", None, mn, mh)
                e.wait_ge(unit_used, U["xa_q"] + 1 + h)
                if h >= 2:
                    e.wait_ge(*PE.at(f"x_cols{h - 2}"))
                e.activation(sq[:, h % 2, :], acc[h % 2][:, :], ACT.Square).then_inc(*AC.done(f"x_sq{h}"))
                e.activation(xq[:, h, :], acc[h % 2][:, :], ACT.Copy, scale=qk_gain[:, 2:3]).then_inc(*AC.done(f"x_q{h}"))
            for h in range(XH):
                e.wait_ge(unit_used, U["xa_kv"] + 1 + h)
                e.wait_ge(*PE.at(f"x_cols{h + 2}"))
                e.activation(sq[:, h % 2, 0:MEM], acc[h % 2][:, 0:MEM], ACT.Square).then_inc(*AC.done(f"x_sq{h + 4}"))
                e.activation(xk[:, h, :], acc[h % 2][:, 0:MEM], ACT.Copy).then_inc(*AC.done(f"x_k{h}"))
            for j in range(2):
                e.wait_ge(unit_used, U["xa_kv"] + 6 + 2 * j)
                e.activation(xv[:, :, j * 256:(j + 1) * 256], acc[0][:, :].rearrange("p (t n) -> p t n", t=2),
                             ACT.Copy).then_inc(*AC.done(f"x_v{j}"))
            def cross_exp(h):
                e.wait_ge(*V.at(f"x_nm{h}"))
                for t in range(NT):
                    r = 4 * h + t
                    e.activation(xS[:, h, t, :], xS[:, h, t, :], ACT.Exp, bias=amax[:, 0, r:r + 1],
                                 accum_out=amax[:, 1, r:r + 1]).then_inc(*AC.done(f"x_exp{h}{t}"))

            cross_exp(0)
            for h in range(XH):
                if h < XH - 1:
                    cross_exp(h + 1)
                for n in range(2):
                    e.wait_ge(*PE.at(f"x_pt{h}{n}"))
                    e.activation(xP[:, h % 2, n, :], bankx[n][:, :], ACT.Copy).then_inc(*AC.done(f"x_ptc{h}{n}"))
                e.wait_ge(*PE.at(f"x_o{h}"))
                e.activation(Mh[:, h, :], ob[h % 2][:, :], ACT.Copy).then_inc(*AC.done(f"x_hi{h}"))

            out_squares(e, "xa_out", 2, 4)
            norm_highs(e, "nf")
            for half in range(2):
                if half:
                    e.wait_ge(unit_used, U["mlp_out0"] + 16)
                with e.Fori(0, 4) as i:
                    AC.enter(f"mlp{half}_scalar", i)
                    for j in range(4):
                        b = j % 2
                        e.wait_ge(unit_used, U[f"mlp_in{half}"] + j + 1 + i * 4)
                        e.wait_ge(*(V.at(f"f{half}yl{j + 2}", i - 1) if j < 2 else V.at(f"f{half}yl{j - 2}", i)))
                        e.activation(sq[:, b, :], acc[b][:, :], ACT.Relu).then_inc(*AC.done(f"f{half}r{j}"))
                        e.wait_ge(*V.at(f"f{half}y{j}", i))
                        e.activation(Yh[:, bass.ds(i * 4 + j, 1), :], sq[:, b, :].unsqueeze(1), ACT.Copy)\
                         .then_inc(*AC.done(f"f{half}yh{j}"))
                    AC.leave(4)
            for k in range(KT):
                e.wait_ge(*PE.at(f"out{k}"))
                e.activation(x_tok[:, :, k * P:(k + 1) * P], ob[k % 2][:, :].rearrange("p (t n) -> p t n", t=NT),
                             ACT.Copy).then_inc(*AC.done("out_copied" if k == KT - 1 else f"outc{k}"))

        @block.tensor
        def _(e):
            count_from(e, PE)
            e.wait_ge(const_in, 16)
            e.wait_ge(x_in, 16)
            for k in range(KT):
                if k >= 2:
                    e.wait_ge(*AC.at(f"x{k - 2}"))
                for t in range(NT):
                    last = e.transpose(ob[k % 2][:, t * P:(t + 1) * P], x_tok[:, t, k * P:(k + 1) * P], ident)
                last.then_inc(*PE.done(f"x{k}"))
            e.wait_ge(*V.at("ones"))
            square_sums(e, "n0")
            norm_spread(e, "n0")
            e.wait_ge(*V.at("ada0sum"))
            ada_columns(e, ada_acc0, 0, 16, "ada0cols")

            with e.Fori(0, RH) as i:
                PE.enter("ret_tensor", i)
                c = U["ret"] + i * 12
                for j in range(4):
                    e.wait_ge(*(V.at(f"r_g{j + 2}", i - 1) if j < 2 else AC.at(f"r_qk{j - 2}", i)))
                    feat(e, acc[j % 2], c + j, U["ret"] + j, inputs="n0" if j == 0 else None)
                tok(e, c + 4, U["ret"] + 4, "r_v0", [AC.at("r_qk2", i), AC.at("r_qk3", i)])
                tok(e, c + 6, U["ret"] + 6, "r_v1", [AC.at("r_v00", i), AC.at("r_v01", i)])
                e.wait_ge(*V.at("r_rope3", i))
                for n in range(NT):
                    if n >= 2:
                        e.wait_ge(*V.at(f"r_s{n - 2}", i))
                    for d in range(2):
                        last = e.matmul(sc[n % 2][:, 0:(NT - n) * P], k_[:, d, n * P:(n + 1) * P],
                                        q_[:, d, n * P:S], start=(d == 0), stop=(d == 1))
                    last.then_inc(*PE.done(f"r_sc{n}"))
                for n in range(2):
                    e.wait_ge(*AC.at(f"r_v1{n}", i))
                    feat(e, acc[n], c + 8 + n, U["ret"] + 8 + n)
                e.wait_ge(*V.at("r_s3", i))
                for n in range(4):
                    if n >= 2:
                        e.wait_ge(*AC.at(f"r_oc{n - 2}", i))
                    for t in range(NT):
                        last = e.matmul(ob[n % 2][:, t * P:S], v_[:, t, n * P:(n + 1) * P],
                                        t_[:, KOFF[t]:KOFF[t] + (NT - t) * P], start=(t == 0), stop=(t == NT - 1))
                    last.then_inc(*PE.done(f"r_o{n}"))
                    if n >= 1:
                        e.wait_ge(*AC.at(f"r_sq{n - 1}", i))
                        columns(e, sq[:, (n - 1) % 2, :], 0, "first" if n == 1 else False, False, f"r_cols{n - 1}")
                e.wait_ge(*V.at("r_g0", i))
                feat(e, acc[0], c + 10, U["ret"] + 10)
                e.wait_ge(*AC.at("r_sq3", i))
                columns(e, sq[:, 1, :], 0, False, "last", "r_cols3")
                e.wait_ge(*V.at("r_g1", i))
                feat(e, acc[1], c + 11, U["ret"] + 11)
                e.wait_ge(*V.at("r_diag", i))
                spread(e, "r_bc")
                PE.leave(RH)
            ada_columns(e, ada_accg, 16, 24, "ada0gate")
            out_tensor(e, "ret_out", V.after("r_yl3", RH))
            e.wait_ge(*V.after("ada1sum1", KT // 2))
            ada_columns(e, ada_acc1, 0, 24, "ada1cols")
            e.wait_ge(*V.at("mod1"))
            stream_sums(e, "n1", V.after("ret_outss1", KT // 2))
            norm_spread(e, "n1")

            def att_qk(i, t, free, inputs=None):
                c = U["att"] + i * 8
                for j in range(4):
                    e.wait_ge(*(free(j) if j < 2 else AC.at(f"{t}qk{j - 2}", i)))
                    feat(e, acc[j % 2], c + j, U["att"] + j, inputs=inputs if j == 0 else None)
                    if j >= 1:
                        e.wait_ge(*AC.at(f"{t}sq{j - 1}", i))
                        columns(e, sq[:, (j - 1) % 2, :], 4 * (j - 1), True, True, f"{t}cols{j - 1}")
                e.wait_ge(*AC.at(f"{t}sq3", i))
                columns(e, sq[:, 1, :], 12, True, True, f"{t}cols3")

            def att_vg(i, t):
                c = U["att"] + i * 8
                tok(e, c + 4, U["att"] + 4, f"{t}v", [AC.at(f"{t}qk2", i), AC.at(f"{t}qk3", i)])
                for h in range(2):
                    e.wait_ge(*V.at(f"{t}diag{h}", i))
                    spread(e, f"{t}bc{h}")
                    e.wait_ge(*AC.at(f"{t}v{h}", i))
                    feat(e, acc[h], c + 6 + h, U["att"] + 6 + h)
                for h in range(2):
                    e.wait_ge(*V.at(f"{t}k{h}", i))
                    for n in range(NT):
                        b = (h * NT + n) % 2
                        if h * NT + n >= 2:
                            r = h * NT + n - 2
                            e.wait_ge(*V.at(f"{t}s{r // NT}{r % NT}", i))
                        e.matmul(sc[b][:, 0:(n + 1) * P], aq[:, h, n * P:(n + 1) * P], ak[:, h, 0:(n + 1) * P],
                                 start=True, stop=True).then_inc(*PE.done(f"{t}sc{h}{n}"))

            def att_pv(i, t, ready):
                for h in range(2):
                    e.wait_ge(*ready(h))
                    for n in range(NT):
                        r = h * NT + n
                        if r >= 2:
                            e.wait_ge(*AC.at(f"{t}pt{(r - 2) // NT}{(r - 2) % NT}", i))
                        for m in range(n, NT):
                            last = e.transpose(sc[n % 2][:, (m - n) * P:(m - n + 1) * P],
                                               aS[:, h, QOFF[m] + n * P:QOFF[m] + (n + 1) * P], ident)
                        last.then_inc(*PE.done(f"{t}pt{h}{n}"))
                for h in range(2):
                    e.wait_ge(*AC.at(f"{t}pt{h}3", i))
                    for n in range(NT):
                        last = e.matmul(ob[h][:, n * P:S], av[:, n, h * P:(h + 1) * P],
                                        aP[:, h, KOFF[n]:KOFF[n] + (NT - n) * P], start=(n == 0), stop=(n == NT - 1))
                    last.then_inc(*PE.done(f"{t}o{h}"))

            att_qk(0, "p", lambda j: V.after("ret_outx1", KT // 2), "n1")
            att_vg(0, "p")
            with e.Fori(1, AH // 2) as i:
                PE.enter("att_tensor", i, 1)
                att_qk(i, "a", lambda j: V.at(f"ag{j}", i - 1))
                att_pv(i, "a", lambda h: V.at(f"anorm{h}", i - 1))
                att_vg(i, "a")
                PE.leave(AH // 2 - 1)
            att_pv(0, "z", lambda h: V.at(f"anorm{h}", AH // 2 - 1))
            out_tensor(e, "att_out", V.at("zyl1"))
            stream_sums(e, "nm", V.after("att_outss1", KT // 2))
            norm_spread(e, "nm")

            for j in range(4):
                if j >= 2:
                    e.wait_ge(*V.at(f"c_in{0}"))
                feat(e, acc[j % 2], U["mix"] + j, U["mix"] + j, inputs="nm" if j == 0 else None)
            u = U["mix"] + 4
            e.wait_ge(*V.at("c_in1"))
            e.wait_ge(*AC.at("c_th1"))
            feat(e, acc[0], u, u)
            for j in range(3):
                if j == 1:
                    e.wait_ge(*AC.at("d_small"))
                    for t in range(NT):
                        last = e.transpose(ob[0][:, t * P:(t + 1) * P], sq[:, 0, t * P:(t + 1) * P], ident)
                    last.then_inc(*PE.done("d_small_t"))
                if j:
                    e.wait_ge(*(AC.at("d_kidx"), AC.at("d_c0"))[j - 1])
                feat(e, acc[(j + 1) % 2], u + 1 + j, u + 1 + j)
            e.wait_ge(*AC.at("tc"))
            e.wait_ge(dsa_w_in, 80)
            e.wait_ge(*AC.at("d_c1"))
            for j in range(2):
                for k in range(2):
                    last = e.matmul(ob[j][:, :], wqb[:, k, j * P:(j + 1) * P], cq[:, k, :], start=(k == 0), stop=(k == 1))
                last.then_inc(*PE.done(f"d_q{j}"))
            e.wait_ge(*AC.at("d_c2"))
            e.matmul(sc[0][:, :], wkvb[:, 0:P], ckv[:, :], start=True, stop=True).then_inc(*PE.done("d_k"))
            for t in range(NT):
                last = e.matmul(sc[1][:, t * DD:(t + 1) * DD], ckv[:, t * P:(t + 1) * P], wkvb[:, P:P + DD],
                                start=True, stop=True)
            last.then_inc(*PE.done("d_v"))
            for j in range(2):
                e.wait_ge(*AC.at(f"d_sq{j}"))
                for t in range(NT):
                    last = e.matmul(st[:, 8 * j + 2 * t:8 * j + 2 * t + 2], sq[:, j, t * P:(t + 1) * P], cst("halves"),
                                    start=True, stop=True)
                last.then_inc(*PE.done(f"d_cols{j}"))
            for j in range(2):
                e.wait_ge(*AC.at(f"d_qc{j}"))
                for k in range(2):
                    last = e.matmul(ob[j][:, :], wqi[:, k, j * P:(j + 1) * P], cq[:, k, :], start=(k == 0), stop=(k == 1))
                last.then_inc(*PE.done(f"d_qi{j}"))
            e.wait_ge(*AC.at("d_sq2"))
            columns(e, sq[:, 0, :], 16, True, True, "d_cols2", of=cst("halves"))

            def gdn_unit(j):
                u = U["mix"] + 8 + j
                e.wait_ge(*(AC.at(f"g_raw{j - 2}") if j >= 2 else AC.at(f"d_c{2 - j}")))
                feat(e, acc[j % 2], u, u)

            gdn_unit(0)
            gdn_unit(1)
            e.wait_ge(*V.at("c_conv"))
            for j in range(2):
                columns(e, co[:, j, :], 32, "first" if j == 0 else False, "last" if j == 1 else False, f"c_cols{j}")
            gdn_unit(2)
            e.wait_ge(*V.at("c_mean"))
            spread(e, "c_mbc")
            gdn_unit(3)
            for j in range(2):
                e.wait_ge(*AC.at(f"c_sq{j}"))
                columns(e, sq[:, j, :], 32, "first" if j == 0 else False, "last" if j == 1 else False, f"c_vcols{j}")
            gdn_unit(4)
            e.wait_ge(*V.at("c_diag"))
            spread(e, "c_bc")
            gdn_unit(5)
            e.wait_ge(*AC.at("d_qic1"))
            e.wait_ge(*AC.at("d_vc"))
            e.wait_ge(kidx_in, 16)
            for m in range(6):
                gdn_unit(6 + m)
                for n in (2 * m, 2 * m + 1):
                    t, h = n // DH + 1, n % DH
                    r0 = (h % 2) * DD
                    if n >= 2:
                        e.wait_ge(*AC.at(f"d_relu{n - 2}"))
                    e.matmul(sc[n % 2][:, 0:(t + 1) * P], dqi[r0:r0 + DD, h // 2, t * P:(t + 1) * P],
                             kidx[r0:r0 + DD, 0:(t + 1) * P], start=True, stop=True).then_inc(*PE.done(f"d_idx{n}"))
                if m == 1:
                    e.wait_ge(*V.at("d_diag"))
                    spread(e, "d_bc")
            for j in range(12, 16):
                gdn_unit(j)

            e.wait_ge(*V.at("d_kn"))
            e.wait_ge(*AC.at("d_relu11"))
            for g in range(2):
                for h in range(2):
                    r0 = h * DD
                    for n in range(NT):
                        r = h * NT + n
                        if r >= 2:
                            e.wait_ge(*V.at(f"d_s{g}{r - 2}"))
                        elif g:
                            e.wait_ge(*AC.at(f"d_ptc01{n + 2}"))
                        e.matmul(sc[r % 2][:, 0:(n + 1) * P], dq[r0:r0 + DD, g, n * P:(n + 1) * P],
                                 dk[r0:r0 + DD, 0:(n + 1) * P], start=True, stop=True).then_inc(*PE.done(f"d_sc{g}{r}"))
                for h in range(2):
                    e.wait_ge(*V.at(f"d_norm{g}{h}"))
                    for n in range(NT):
                        r = h * NT + n
                        if r >= 2:
                            e.wait_ge(*AC.at(f"d_ptc{g}{(r - 2) // NT}{(r - 2) % NT}"))
                        for m in range(n, NT):
                            last = e.transpose(sc[n % 2][:, (m - n) * P:(m - n + 1) * P],
                                               dS[:, h, QOFF[m] + n * P:QOFF[m] + (n + 1) * P], ident)
                        last.then_inc(*PE.done(f"d_pt{g}{h}{n}"))
                for h in range(2):
                    e.wait_ge(*AC.at(f"d_ptc{g}{h}3"))
                    for n in range(NT):
                        last = e.matmul(ob[g][h * DD:(h + 1) * DD, n * P:S], dv[:, n, :],
                                        dP[:, h, KOFF[n]:KOFF[n] + (NT - n) * P], start=(n == 0), stop=(n == NT - 1))
                last.then_inc(*PE.done(f"d_o{g}"))

            for j in range(8):
                e.wait_ge(*AC.at(f"g_sq{j}"))
                columns(e, sq[:, j % 2, :], 4 * j, True, True, f"g_cols{j}")
            for j in range(8):
                e.wait_ge(*V.at(f"g_diag{j}"))
                if j >= 2:
                    e.wait_ge(*V.at(f"g_n{j - 2}"))
                spread(e, f"g_bc{j}", buf=sq[:, j % 2, :], bank=(bc, ob[0])[j % 2])
            e.wait_ge(*V.at("g_g"))
            e.matmul(st[:, 0:16], cst("cumsum"), gc[:, 5, :], start=True, stop=True)
            e.matmul(st[:, 16:32], ones[:, :], gc[:, 5, :], start=True, stop=True).then_inc(*PE.done("g_dl"))
            e.wait_ge(*V.at("g_n7"))
            e.wait_ge(*G.at("g_silu11"))
            for t in range(NT):
                for a, name in enumerate("kv"):
                    if t:
                        e.wait_ge(*AC.at(f"g_{name}tokc{t - 1}"))
                    for h in range(GH):
                        last = e.transpose(sc[a][:, h * P:(h + 1) * P], gqkv[:, 4 + 4 * a + h, t * P:(t + 1) * P], ident)
                    last.then_inc(*PE.done(f"g_{name}tok{t}"))
            def gdn_decay(t):
                e.wait_ge(*V.at(f"g_gb{t}"))
                if t >= 2:
                    e.wait_ge(*AC.at(f"g_eD{t - 2}"))
                for h in range(GH):
                    last = e.matmul(ob[t % 2][:, h * P:(h + 1) * P], ggb[:, t % 2, h, :], cst("cumsum"),
                                    start=True, stop=True)
                last.then_inc(*PE.done(f"g_D{t}"))

            gdn_decay(0)
            for t in range(NT):
                e.wait_ge(*(V.at(f"g_QK{t - 1}") if t else AC.at("g_vtokc3")))
                for h in range(GH):
                    k = gqkv[:, 4 + h, t * P:(t + 1) * P]
                    last = e.matmul(sc[0][:, h * P:(h + 1) * P], k, k, start=True, stop=True)
                last.then_inc(*PE.done(f"g_kk{t}"))
                for h in range(GH):
                    last = e.matmul(sc[1][:, h * P:(h + 1) * P], gqkv[:, h, t * P:(t + 1) * P],
                                    gqkv[:, 4 + h, t * P:(t + 1) * P], start=True, stop=True)
                last.then_inc(*PE.done(f"g_qk{t}"))
                if t < NT - 1:
                    gdn_decay(t + 1)
                e.wait_ge(*V.at(f"g_A{t}"))
                if t:
                    e.wait_ge(*AC.at(f"g_ATc{t - 1}"))
                for h in range(GH):
                    last = e.transpose(acc[0][:, h * P:(h + 1) * P], gA[:, h, :], ident)
                last.then_inc(*PE.done(f"g_AT{t}"))
                e.wait_ge(*V.at(f"g_QK{t}"))
                if t:
                    e.wait_ge(*AC.at(f"g_QKTc{t - 1}"))
                for h in range(GH):
                    last = e.transpose(acc[1][:, h * P:(h + 1) * P], gQK[:, h, :], ident)
                last.then_inc(*PE.done(f"g_QKT{t}"))
            for t in range(NT):
                e.wait_ge(*G.at(f"g_TT0{t}"))
                if t >= 2:
                    e.wait_ge(*AC.at(f"g_Tc{t - 2}"))
                for h in range(GH):
                    last = e.transpose(sc[t % 2][:, h * P:(h + 1) * P], gTT[:, t, h, :], ident)
                last.then_inc(*PE.done(f"g_T0{t}"))
            for l in range(1, LEVELS):
                def inverse(t):
                    if t < 2 and l > 1:
                        e.wait_ge(*V.at(f"g_TT{l - 1}{t + 2}"))
                    e.wait_ge(*AC.at(f"g_Xc{l}{t}"))
                    if l < LEVELS - 1:
                        for h in range(GH):
                            last = e.matmul(ob[t % 2][:, h * P:(h + 1) * P], gTT[:, t, h, :], gX[:, t % 2, h, :],
                                            start=True, stop=True)
                        last.then_inc(*PE.done(f"g_P{l}{t}"))
                    for h in range(GH):
                        last = e.matmul(acc[t % 2][:, h * P:(h + 1) * P], gX[:, t % 2, h, :], gTT[:, t, h, :],
                                        start=True, stop=True)
                    last.then_inc(*PE.done(f"g_R{l}{t}"))

                for t in range(NT):
                    e.wait_ge(*V.at(f"g_M{l}{t}"))
                    e.wait_ge(*(V.at(f"g_TT{l - 1}{t}") if l > 1 else AC.at(f"g_Tc{t}")))
                    if l == 1 and t < 2:
                        e.wait_ge(*AC.at(f"g_Tc{t + 2}"))
                    for h in range(GH):
                        last = e.matmul(sc[t % 2][:, h * P:(h + 1) * P], gMT[:, t % 2, h, :], gT[:, t, h, :],
                                        start=True, stop=True)
                    last.then_inc(*PE.done(f"g_X{l}{t}"))
                    if t >= 1:
                        if t >= 3:
                            e.wait_ge(*V.at(f"g_TT{l}{t - 3}"))
                        inverse(t - 1)
                e.wait_ge(*V.at(f"g_TT{l}1"))
                inverse(3)
            for t in range(NT):
                e.wait_ge(*V.at(f"g_kbe{t}"))
                e.wait_ge(*(AC.at(f"g_wc{t - 2}") if t >= 2 else V.at(f"g_TT{LEVELS - 1}3")))
                for h in range(GH):
                    last = e.matmul(acc[t % 2][:, h * P:(h + 1) * P], gkbe[:, h, :], gTT[:, t, h, :], start=True, stop=True)
                last.then_inc(*PE.done(f"g_w{t}"))
            e.wait_ge(*V.at("g_vb"))
            e.wait_ge(*AC.at("g_wc3"))
            for t in range(NT):
                if t:
                    e.wait_ge(*V.at(f"g_S{t - 1}"))
                for h in range(GH):
                    o = ob[t % 2][:, h * P:(h + 1) * P]
                    last = e.matmul(o, gTT[:, t, h, :], gvtok[:, t, h, :], start=True, stop=(t == 0))
                    if t:
                        last = e.matmul(o, gwT[:, t, h, :], gst[:, h, :], start=False, stop=True)
                last.then_inc(*PE.done(f"g_vn{t}"))
                e.wait_ge(*AC.at(f"g_vnc{t}"))
                if t == 0:
                    e.wait_ge(*G.at("g_qe3"))
                    e.wait_ge(*V.at("g_kdec"))
                if t < NT - 1:
                    for h in range(GH):
                        last = e.matmul(acc[t % 2][:, h * P:(h + 1) * P], gkdec[:, t, h, :], gvn[:, t % 2, h, :],
                                        start=True, stop=True)
                    last.then_inc(*PE.done(f"g_U{t}"))
                for h in range(GH):
                    o = sc[t % 2][:, h * P:(h + 1) * P]
                    last = e.matmul(o, gvn[:, t % 2, h, :], gQKT[:, t, h, :], start=True, stop=(t == 0))
                    if t:
                        last = e.matmul(o, gst[:, h, :], gqkv[:, h, t * P:(t + 1) * P], start=False, stop=True)
                last.then_inc(*PE.done(f"g_o{t}"))
            for h in range(GH):
                e.wait_ge(*AC.at(f"g_osq{h}"))
                columns(e, sq[:, h % 2, :], 4 * h, True, True, f"g_ocols{h}")
            for h in range(GH):
                e.wait_ge(*V.at(f"g_odiag{h}"))
                if h >= 2:
                    e.wait_ge(*V.at(f"g_y{h - 2}"))
                spread(e, f"g_obc{h}", buf=sq[:, h % 2, :], bank=(bc, ob[0])[h % 2])

            def out_flat(name, ready, k1):
                e.wait_ge(*ready)
                c = U[name]
                with e.Fori(0, 2) as i:
                    PE.enter(name, i)
                    for j in range(4):
                        e.wait_ge(*(V.at(f"{name}x{j + 2}", i - 1) if j < 2 else V.at(f"{name}x{j - 2}", i)))
                        product(e, acc[j % 2], c + j + i * 4, c + j, lambda k: Mh[:, k, :], lambda k: Ml[:, k, :], k1=k1)
                    PE.leave(2)

            out_flat("mix_out", V.at(f"g_lo{GH - 1}"), KT)

            stream_sums(e, "nx", V.after("mix_outss3", 2))
            e.wait_ge(mem_in, 16)
            for k in range(KT):
                e.wait_ge(*(AC.at(f"m{k - 2}") if k >= 2 else V.at(f"g_lo{GH - 1}")))
                for t in range(2):
                    last = e.transpose(ob[k % 2][:, t * P:(t + 1) * P], m_tok[:, t, k * P:(k + 1) * P], ident)
                last.then_inc(*PE.done(f"m{k}"))
            norm_spread(e, "nx")
            for h in range(XH):
                if h >= 2:
                    e.wait_ge(*AC.at(f"x_q{h - 2}"))
                feat(e, acc[h % 2], U["xa_q"] + h, U["xa_q"] + h, inputs="nx" if h == 0 else None)
                if h == 0:
                    square_sums(e, "nk", 2)
                if h == 1:
                    norm_spread(e, "nk", 2)
                if h >= 1:
                    e.wait_ge(*AC.at(f"x_sq{h - 1}"))
                    columns(e, sq[:, (h - 1) % 2, :], 4 * (h - 1), True, True, f"x_cols{h - 1}")
            e.wait_ge(*V.at(f"nkh{KT - 1}"))
            for h in range(XH):
                u = U["xa_kv"] + h
                e.wait_ge(*(AC.at(f"x_q{h + 2}") if h < 2 else AC.at(f"x_k{h - 2}")))
                e.wait_ge(split_done, u + 1)
                for k in range(KT):
                    o = acc[h % 2][:, 0:MEM]
                    e.matmul(o, wh[:, u % RING, k, :], mh[:, k, :], start=(k == 0), stop=False)
                    e.matmul(o, wh[:, u % RING, k, :], ml[:, k, :], start=False, stop=False)
                    last = e.matmul(o, wl[:, u % RING, k, :], mh[:, k, :], start=False, stop=(k == KT - 1))
                last.then_inc(unit_used, 1)
                if h == 0:
                    e.wait_ge(*AC.at("x_sq3"))
                    columns(e, sq[:, 1, :], 12, True, True, "x_cols3")
                else:
                    e.wait_ge(*AC.at(f"x_sq{h + 3}"))
                    columns(e, sq[:, (h - 1) % 2, :], 16 + 2 * (h - 1), True, True, f"x_cols{h + 3}", n=2)
            e.wait_ge(*AC.at("x_sq7"))
            columns(e, sq[:, 1, :], 22, True, True, "x_cols7", n=2)
            for j in range(2):
                tok(e, U["xa_kv"] + 4 + 2 * j, U["xa_kv"] + 4 + 2 * j, "", [AC.at("x_v0") if j else AC.at("x_k2")],
                    mh, ml, 2)
            for h in range(XH):
                e.wait_ge(*V.at(f"x_diag{h}"))
                spread(e, f"x_bc{h}", 2)
            e.wait_ge(*AC.at("x_v1"))

            def cross_scores(h):
                e.wait_ge(*V.at(f"x_kn{h}"))
                for n in range(2):
                    if h:
                        e.wait_ge(*V.at(f"x_s{h - 1}{n}"))
                    for t in range(2 * n, 2 * n + 2):
                        last = e.matmul(sc[n][:, (t % 2) * MEM:(t % 2 + 1) * MEM], xq[:, h, t * P:(t + 1) * P],
                                        xk[:, h, :], start=True, stop=True)
                    last.then_inc(*PE.done(f"x_sc{h}{n}"))

            cross_scores(0)
            cross_scores(1)
            for h in range(XH):
                if h < XH - 2:
                    cross_scores(h + 2)
                e.wait_ge(*V.at(f"x_norm{h}"))
                for n in range(2):
                    if h:
                        e.wait_ge(*AC.at(f"x_ptc{h - 1}{n}"))
                    for t in range(NT):
                        last = e.transpose(bankx[n][:, t * P:(t + 1) * P], xS[:, h, t, n * P:(n + 1) * P], ident)
                    last.then_inc(*PE.done(f"x_pt{h}{n}"))
                if h >= 2:
                    e.wait_ge(*V.at(f"x_lo{h - 2}"))
                for n in range(2):
                    e.wait_ge(*AC.at(f"x_ptc{h}{n}"))
                    last = e.matmul(ob[h % 2][:, :], xv[:, n, h * P:(h + 1) * P], xP[:, h % 2, n, :],
                                    start=(n == 0), stop=(n == 1))
                last.then_inc(*PE.done(f"x_o{h}"))
            out_flat("xa_out", V.at("x_lo3"), 4)

            stream_sums(e, "nf", V.after("xa_outss3", 2))
            norm_spread(e, "nf")
            for half in range(2):
                c = U[f"mlp_in{half}"]
                if half:
                    e.wait_ge(*V.after("mlp_out0x1", KT // 2))
                with e.Fori(0, 4) as i:
                    PE.enter(f"mlp_in{half}", i)
                    for j in range(4):
                        e.wait_ge(*(AC.at(f"f{half}r{j + 2}", i - 1) if j < 2 else AC.at(f"f{half}r{j - 2}", i)))
                        feat(e, acc[j % 2], c + j + i * 4, c + j, inputs="nf" if half == 0 and j == 0 else None)
                    PE.leave(4)
                out_tensor(e, f"mlp_out{half}", V.after(f"f{half}yl3", 4))
            e.wait_ge(*V.after(FINAL + "x1", KT // 2))
            for k in range(KT):
                if k >= 2:
                    e.wait_ge(*AC.at(f"outc{k - 2}"))
                for t in range(NT):
                    last = e.transpose(ob[k % 2][:, t * P:(t + 1) * P], xT[:, k, t * P:(t + 1) * P], ident)
                last.then_inc(*PE.done(f"out{k}"))

        @block.vector
        def _(e):
            count_from(e, V)
            e.memset(ones[:, :], 1.0).then_inc(*V.done("ones"))
            e.wait_ge(small_in, 16)
            e.wait_ge(*AC.at("cond_tanh"))
            step(e, e.scalar_tensor_tensor(out=cond[:, 1, :], in0=cond[:, 1, :], scalar=1.0, in1=sm("c"),
                                           op0=ALU.add, op1=ALU.mult), V)
            step(e, e.tensor_scalar(cond[:, 0, :], cond[:, 1, :], 0.5, None, ALU.mult), V)
            step(e, e.tensor_tensor(qk_gain[:, 0:1], sm("att_q_g"), sm("att_k_g"), ALU.mult), V)
            for k in range(KT):
                e.wait_ge(ada_in[k], 16)
                ada_sum(e, ada_acc0[:, 0:2 * D], ada_w0[:, k, :], k, "ada0sum" if k == KT - 1 else None)
                if k == KT - 2:
                    norm_roots(e, "n0")

            def modulation(layer, n0, n1, name):
                cols = mod[:, layer, :, :].rearrange("p a k -> p (a k)")
                step(e, e.tensor_tensor(cols[:, n0:n1], st[:, n0:n1], sm(f"ada_b{layer}", n0, n1 - n0), ALU.add),
                     V, name)

            def gains(layer):
                step(e, e.scalar_tensor_tensor(out=gain[:, layer, :], in0=mod[:, layer, 1, :], scalar=1.0,
                                               in1=sm(f"norm_g{layer}"), op0=ALU.add, op1=ALU.mult), V)

            e.wait_ge(*PE.at("ada0cols"))
            modulation(0, 0, 16, "mod0")
            gains(0)
            norm_vector(e, "n0", lambda k: gain[:, 0, k:k + 1], lambda k: mod[:, 0, 0, k:k + 1])
            e.wait_ge(pos_in, 16)
            step(e, e.tensor_copy(ang[:, :], pos[:, :]), V)
            step(e, e.tensor_scalar(ang[:, :], ang[:, :], sm("inv_freq"), None, ALU.mult), V)
            step(e, e.tensor_scalar(tmp[:, 0, :], ang[:, :], 1.0 / TURN, ROUND, ALU.mult, ALU.add), V)
            step(e, e.tensor_scalar(tmp[:, 0, :], tmp[:, 0, :], -ROUND, None, ALU.add), V)
            for part in TURN_PARTS:
                step(e, e.scalar_tensor_tensor(out=ang[:, :], in0=tmp[:, 0, :], scalar=-part, in1=ang[:, :],
                                               op0=ALU.mult, op1=ALU.add), V)
            step(e, e.tensor_scalar(ang[:, :], ang[:, :], PI_BELOW, -PI_BELOW, ALU.min, ALU.max), V)
            step(e, e.scalar_tensor_tensor(out=tmp[:, 1, :], in0=ang[:, :], scalar=-1.0, in1=ang[:, :],
                                           op0=ALU.mult, op1=ALU.max), V)
            step(e, e.tensor_scalar(tmp[:, 1, :], tmp[:, 1, :], -1.0, TURN / 4, ALU.mult, ALU.add), V, "angles")
            for k in range(KT):
                e.wait_ge(ada_in[k], 32)
                ada_sum(e, ada_accg[:, :], ada_g0[:, k, :], k, "ada0gsum" if k == KT - 1 else None)

            e.wait_ge(*AC.at("rope"))
            with e.Fori(0, RH) as i:
                V.enter("ret_vector", i)
                c = U["ret"] + i * 12
                for a, x in ((0, q_), (2, k_)):
                    e.wait_ge(*AC.at(f"r_qk{a + 1}", i))
                    x1, x2, t1, t2 = x[:, 0, :], x[:, 1, :], tmp[:, 0, :], tmp[:, 1, :]
                    e.wait_ge(*V.last())
                    e.tensor_tensor(t1, x1, sin_[:, :], ALU.mult).then_inc(*V.done())
                    step(e, e.tensor_tensor(t2, x2, sin_[:, :], ALU.mult), V)
                    e.tensor_tensor(x1, x1, cos_[:, :], ALU.mult).then_inc(*V.done())
                    step(e, e.tensor_tensor(x2, x2, cos_[:, :], ALU.mult), V)
                    e.tensor_tensor(x1, x1, t2, ALU.subtract).then_inc(*V.done(f"r_rope{a}"))
                    step(e, e.tensor_tensor(x2, x2, t1, ALU.add), V, f"r_rope{a + 1}")
                e.wait_ge(decay_in, i * 16 + 16)
                for n in range(NT):
                    e.wait_ge(*PE.at(f"r_sc{n}", i))
                    e.tensor_tensor(t_[:, KOFF[n]:KOFF[n] + (NT - n) * P], sc[n % 2][:, 0:(NT - n) * P],
                                    dec[:, 0:(NT - n) * P], ALU.mult).then_inc(*V.done(f"r_s{n}"))

                def gate(n):
                    e.wait_ge(*AC.at(f"r_th{n}", i))
                    e.scalar_tensor_tensor(out=s_[:, n, :], in0=s_[:, n, :], scalar=1.0, in1=acc[n % 2][:, :],
                                           op0=ALU.add, op1=ALU.mult).then_inc(*V.done(f"r_g{n}"))

                gate(0)
                gate(1)
                e.wait_ge(*PE.at("r_cols3", i))
                rsqrt(e, NT, 1.0 / RV)
                diagonal(e, 0, "r_diag")
                gate(2)
                gate(3)
                e.wait_ge(*PE.at("r_bc", i))

                def rest(n):
                    e.wait_ge(*AC.at(f"r_yh{n}", i))
                    e.tensor_tensor(Yl[:, bass.ds(i * 4 + n, 1), :], o_[n].unsqueeze(1),
                                    Yh[:, bass.ds(i * 4 + n, 1), :].bitcast(F32), ALU.subtract)\
                     .then_inc(*V.done(f"r_yl{n}"))

                for n in range(4):
                    g0 = SMALL["ret_gn_g"][0]
                    step(e, e.scalar_tensor_tensor(out=o_[n], in0=o_[n], scalar=small[:, bass.ds(i * 4 + n + g0, 1)],
                                                   in1=bc[:, :], op0=ALU.mult, op1=ALU.mult), V)
                    e.scalar_tensor_tensor(out=o_[n], in0=o_[n], scalar=0.5, in1=s_[:, n, :],
                                           op0=ALU.mult, op1=ALU.mult).then_inc(*V.done(f"r_y{n}"))
                    if n >= 1:
                        rest(n - 1)
                rest(3)
                V.leave(RH)
            e.wait_ge(*PE.at("ada0gate"))
            modulation(0, 16, 24, "mod0gate")
            step(e, e.memset(ada_acc1[:, :], 0.0), V)

            def ada1(e, i, after):
                if after:
                    return
                for b in range(2):
                    e.wait_ge(ada1_in[b], i * 16 + 16)
                    step(e, e.scalar_tensor_tensor(out=ada_acc1[:, :], in0=ada_w1[:, b, :],
                                                   scalar=cond[:, 0, bass.ds(i * 2 + b, 1)], in1=ada_acc1[:, :],
                                                   op0=ALU.mult, op1=ALU.add), V, f"ada1sum{b}")

            out_vector(e, "ret_out", lambda n: mod[:, 0, 2, bass.ds(n, 1)], ada1)
            e.wait_ge(*PE.at("ada1cols"))
            modulation(1, 0, 24, "mod1")
            gains(1)
            norm_roots(e, "n1")
            norm_vector(e, "n1", lambda k: gain[:, 1, k:k + 1], lambda k: mod[:, 1, 0, k:k + 1])
            for h in range(2):
                e.memset(ab[0:CHUNK, h, S - CHUNK:S], NEG).then_inc(*V.done("mask"))

            def att_vg(i, t, turn):
                e.wait_ge(*PE.at(f"{t}cols3", i))
                rsqrt(e, 16, 1.0 / AD)
                step(e, e.tensor_scalar(rs[:, 0, 0:8], rs[:, 0, 0:8], AD ** -0.5, None, ALU.mult), V)
                for h in range(2):
                    diagonal(e, 8 + 4 * h, f"{t}diag{h}")
                    e.wait_ge(*PE.at(f"{t}bc{h}", i))
                    step(e, e.tensor_tensor(ak[:, h, :], ak[:, h, :], bc[:, :], ALU.mult), V, f"{t}k{h}")
                for h in range(2):
                    e.wait_ge(*AC.at(f"{t}th{h}", i))
                    e.scalar_tensor_tensor(out=ag[:, h, :], in0=ag[:, h, :], scalar=1.0, in1=acc[h][:, :],
                                           op0=ALU.add, op1=ALU.mult).then_inc(*V.done(f"{t}g{h}"))
                for h in range(2):
                    e.wait_ge(bias_in[h], i * 32 + 32)
                    for n in range(NT):
                        x = aS[:, h, QOFF[n]:QOFF[n] + (n + 1) * P]
                        r = h * 4 + n
                        e.wait_ge(*PE.at(f"{t}sc{h}{n}", i))
                        step(e, e.scalar_tensor_tensor(out=x, in0=sc[r % 2][:, 0:(n + 1) * P], scalar=rs[:, 0, r:r + 1],
                                                       in1=ab[:, h, S - (n + 1) * P:S], op0=ALU.mult, op1=ALU.add),
                             V, f"{t}s{h}{n}")
                        e.tensor_reduce(amax[:, 2, r:r + 1], x, AX.X, ALU.max).then_inc(*V.done())
                    e.wait_ge(*V.last())
                    e.tensor_scalar(amax[:, 0, 4 * h:4 * h + 4], amax[:, 2, 4 * h:4 * h + 4], -1.0, None, ALU.mult)\
                     .then_inc(*V.done(f"{t}nm{h}"))
                for h in range(2):
                    e.wait_ge(*AC.at(f"{t}exp{h}3", i))
                    step(e, e.reciprocal(amax[:, 2, 4 * h:4 * h + 4], amax[:, 1, 4 * h:4 * h + 4]), V)
                    for n in range(NT):
                        x = aS[:, h, QOFF[n]:QOFF[n] + (n + 1) * P]
                        e.tensor_scalar(x, x, amax[:, 2, 4 * h + n:4 * h + n + 1], None, ALU.mult)\
                         .then_inc(*V.done(f"{t}norm{h}" if n == NT - 1 else None))

            def att_pv(pair, i, t):
                for h in range(2):
                    e.wait_ge(*PE.at(f"{t}o{h}", i))
                    e.scalar_tensor_tensor(out=ay[:, h, :], in0=ob[h][:, :], scalar=0.5, in1=ag[:, h, :],
                                           op0=ALU.mult, op1=ALU.mult).then_inc(*V.done(f"{t}y{h}"))
                for h in range(2):
                    e.wait_ge(*AC.at(f"{t}yh{h}", i))
                    e.tensor_tensor(Yl[:, bass.ds(pair * 2 + h, 1), :], ay[:, h, :].unsqueeze(1),
                                    Yh[:, bass.ds(pair * 2 + h, 1), :].bitcast(F32), ALU.subtract)\
                     .then_inc(*V.done(f"{t}yl{h}"))

            att_vg(0, "p", 0)
            with e.Fori(1, AH // 2) as i:
                V.enter("att_vector", i, 1)
                att_pv(i - 1, i, "a")
                att_vg(i, "a", i)
                V.leave(AH // 2 - 1)
            att_pv(AH // 2 - 1, 0, "z")
            out_vector(e, "att_out", lambda n: mod[:, 1, 2, bass.ds(n, 1)])
            norm_roots(e, "nm")
            norm_vector(e, "nm", lambda k: sm("norm_mix", k, 1))

            step(e, e.tensor_scalar(negs[:, :], cst("causal"), -1.0, -NEG, ALU.add, ALU.mult), V)
            step(e, e.tensor_tensor(strict[:, :], cst("causal"), ident, ALU.subtract), V)
            step(e, e.tensor_tensor(qk_gain[:, 1:2], sm("dsa_q_norm"), sm("dsa_k_norm"), ALU.mult), V)
            step(e, e.tensor_tensor(qk_gain[:, 2:3], sm("xa_q_norm"), sm("xa_k_norm"), ALU.mult), V)
            e.memset(cy[:, :, 0:CONVW - 1], 0.0).then_inc(*V.done())
            e.memset(gqkv_pad[:, :, 0:PAD], 0.0).then_inc(*V.done())
            for j in range(2):
                e.wait_ge(*AC.at(f"c_th{j}"))
                e.wait_ge(unit_used, U["mix"] + 2 * j + 2)
                e.scalar_tensor_tensor(out=cy[:, j, CONVW - 1:], in0=cg[:, j, :], scalar=1.0, in1=acc[1][:, :],
                                       op0=ALU.add, op1=ALU.mult).then_inc(*V.done(f"c_in{j}"))
            e.wait_ge(*V.last())
            cw = SMALL["conv_dw"][0]
            for k in range(CONVW):
                for j in range(2):
                    w_ = small[:, cw + j * CONVW + k:cw + j * CONVW + k + 1]
                    if k == 0:
                        e.tensor_scalar(co[:, j, :], cy[:, j, 0:S], w_, None, ALU.mult).then_inc(*V.done(f"c_{k}{j}"))
                    else:
                        e.wait_ge(*V.at(f"c_{k - 1}{j}"))
                        e.scalar_tensor_tensor(out=co[:, j, :], in0=cy[:, j, k:k + S], scalar=w_, in1=co[:, j, :],
                                               op0=ALU.mult, op1=ALU.add).then_inc(*V.done(f"c_{k}{j}"))
            e.wait_ge(*V.last())
            for j in range(2):
                e.tensor_scalar(co[:, j, :], co[:, j, :], 0.5, sm("conv_dw_b", j, 1), ALU.mult, ALU.add)\
                 .then_inc(*V.done("c_conv"))
            e.wait_ge(*PE.at("c_cols1"))
            step(e, e.tensor_scalar(rs[:, 0, 0:NT], st[:, 32:32 + NT], 1.0 / (2 * P), None, ALU.mult), V)
            diagonal(e, 0, "c_mean")
            e.wait_ge(*PE.at("c_mbc"))
            for j in range(2):
                e.tensor_tensor(co[:, j, :], co[:, j, :], bc[:, :], ALU.subtract).then_inc(*V.done("c_centered"))
            e.wait_ge(*PE.at("c_vcols1"))
            rsqrt(e, NT, 1.0 / (2 * P), c0=32)
            diagonal(e, 0, "c_diag")
            e.wait_ge(*PE.at("c_bc"))
            for j in range(2):
                e.scalar_tensor_tensor(out=co[:, j, :], in0=co[:, j, :], scalar=sm("conv_ln_g", j, 1), in1=bc[:, :],
                                       op0=ALU.mult, op1=ALU.mult).then_inc(*V.done(f"c_t{j}"))
            for j in range(2):
                e.wait_ge(*AC.at(f"c_sth{j}"))
                e.scalar_tensor_tensor(out=co[:, j, :], in0=cg[:, j, :], scalar=1.0, in1=co[:, j, :],
                                       op0=ALU.add, op1=ALU.mult).then_inc(*V.done(f"c_y{j}"))
            for j in range(2):
                e.wait_ge(*AC.at(f"c_hi{j}"))
                e.scalar_tensor_tensor(out=Ml[:, 6 + j, :], in0=co[:, j, :], scalar=0.5,
                                       in1=Mh[:, 6 + j, :].bitcast(F32), op0=ALU.mult, op1=ALU.subtract)\
                 .then_inc(*V.done(f"c_lo{j}"))

            e.wait_ge(*PE.at("d_cols2"))
            rsqrt(e, 20, 1.0 / DD)
            step(e, e.tensor_scalar(rs[:, 0, 0:16], rs[:, 0, 0:16], DD ** -0.5, None, ALU.mult), V)
            diagonal(e, 16, "d_diag")
            e.wait_ge(*AC.at("tc"))
            step(e, e.tensor_scalar(gc[:, 1, :].rearrange("p (t h) -> p t h", t=NT), tc[:, :, 0:4],
                                    DH ** -0.5 * DD ** -0.5, None, ALU.mult), V)
            WOFF = [0, 0, 2 * P, 5 * P]
            for t in range(1, NT):
                w_ = (t + 1) * P
                x = score[:, WOFF[t]:WOFF[t] + w_]
                for h in range(DH):
                    n = (t - 1) * DH + h
                    wcol = gc[:, 1, t * 4 + h:t * 4 + h + 1]
                    e.wait_ge(*AC.at(f"d_relu{n}"))
                    if h == 0:
                        step(e, e.tensor_scalar(x, drelu[:, n % 2, 0:w_], wcol, None, ALU.mult), V, f"d_sum{n}")
                    else:
                        step(e, e.scalar_tensor_tensor(out=x, in0=drelu[:, n % 2, 0:w_], scalar=wcol, in1=x,
                                                       op0=ALU.mult, op1=ALU.add), V, f"d_sum{n}")
                d = score[:, WOFF[t] + t * P:WOFF[t] + w_]
                step(e, e.tensor_tensor(d, d, cst("causal"), ALU.mult), V)
                step(e, e.tensor_tensor(d, d, negs[:, :], ALU.add), V)
            e.wait_ge(*PE.at("d_bc"))
            e.wait_ge(*AC.at("d_kc"))
            e.tensor_tensor(dk[:, :], dk[:, :], bc[:, :], ALU.mult).then_inc(*V.done("d_kn"))
            for r in range(TOPK // 8):
                for t in range(1, NT):
                    src = (work if r else score)[:, WOFF[t]:WOFF[t] + (t + 1) * P]
                    if r:
                        e.wait_ge(*V.at(f"d_rep{r - 1}{t}"))
                    e.max(best[:, t - 1, :], src).then_inc(*V.done(f"d_max{r}{t}"))
                for t in range(1, NT):
                    keys = slice(WOFF[t], WOFF[t] + (t + 1) * P)
                    e.wait_ge(*V.at(f"d_max{r}{t}"))
                    e.match_replace(work[:, keys], best[:, t - 1, :], (work if r else score)[:, keys], -3.0e38)\
                     .then_inc(*V.done(f"d_rep{r}{t}"))
            for t in range(1, NT):
                keys = slice(WOFF[t], WOFF[t] + (t + 1) * P)
                e.wait_ge(*V.last())
                step(e, e.tensor_tensor(work[:, keys], work[:, keys], score[:, keys], ALU.not_equal), V)
                step(e, e.tensor_scalar(work[:, keys], work[:, keys], -1.0, -NEG, ALU.add, ALU.mult), V)

            def by_head(x):
                return x.unsqueeze(1).to_broadcast([P, NT, GH])

            def grid(n):
                return gc[:, n, :].rearrange("p (t h) -> p t h", t=NT)

            step(e, e.tensor_tensor(grid(1), tc[:, :, 4:8], by_head(sm("gdn_dt_bias")), ALU.add), V)
            step(e, e.scalar_tensor_tensor(out=gc[:, 2, :], in0=gc[:, 1, :], scalar=-1.0, in1=gc[:, 1, :],
                                           op0=ALU.mult, op1=ALU.max), V, "g_abs")
            e.wait_ge(*AC.at("g_ex"))
            step(e, e.tensor_scalar(gc[:, 2, :], gc[:, 2, :], 1.0, None, ALU.add), V, "g_1p")
            e.wait_ge(*AC.at("g_bth"))
            step(e, e.tensor_scalar(gc[:, 4, :], gc[:, 3, :], 1.0, 0.5, ALU.add, ALU.mult), V)
            e.wait_ge(*AC.at("g_ln"))
            step(e, e.scalar_tensor_tensor(out=gc[:, 1, :], in0=gc[:, 1, :], scalar=0.0, in1=gc[:, 2, :],
                                           op0=ALU.max, op1=ALU.add), V)
            step(e, e.scalar_tensor_tensor(out=grid(5), in0=grid(1), scalar=-1.0, in1=by_head(gc[:, 0, 0:GH]),
                                           op0=ALU.mult, op1=ALU.mult), V, "g_g")
            for g in range(2):
                for h in range(2):
                    for n in range(NT):
                        r = h * 4 + n
                        x = dS[:, h, QOFF[n]:QOFF[n] + (n + 1) * P]
                        m = negs[:, :] if n == 0 else work[:, WOFF[n]:WOFF[n] + (n + 1) * P]
                        col = g * 8 + 2 * n + h
                        e.wait_ge(*PE.at(f"d_sc{g}{r}"))
                        step(e, e.scalar_tensor_tensor(out=x, in0=sc[r % 2][:, 0:(n + 1) * P],
                                                       scalar=rs[:, 0, col:col + 1],
                                                       in1=m,
                                                       op0=ALU.mult, op1=ALU.add), V, f"d_s{g}{r}")
                        e.tensor_reduce(amax[:, 2, r:r + 1], x, AX.X, ALU.max).then_inc(*V.done())
                    e.wait_ge(*V.last())
                    e.tensor_scalar(amax[:, 0, 4 * h:4 * h + 4], amax[:, 2, 4 * h:4 * h + 4], -1.0, None, ALU.mult)\
                     .then_inc(*V.done(f"d_nm{g}{h}"))
                for h in range(2):
                    e.wait_ge(*AC.at(f"d_exp{g}{h}3"))
                    step(e, e.reciprocal(amax[:, 2, 4 * h:4 * h + 4], amax[:, 1, 4 * h:4 * h + 4]), V)
                    for n in range(NT):
                        x = dS[:, h, QOFF[n]:QOFF[n] + (n + 1) * P]
                        e.tensor_scalar(x, x, amax[:, 2, 4 * h + n:4 * h + n + 1], None, ALU.mult)\
                         .then_inc(*V.done(f"d_norm{g}{h}"))
            for g in range(2):
                e.wait_ge(*AC.at(f"d_hi{g}"))
                e.tensor_tensor(Ml[:, 4 + g, :], ob[g][:, :], Mh[:, 4 + g, :].bitcast(F32), ALU.subtract)\
                 .then_inc(*V.done(f"d_lo{g}"))

            for j in range(4):
                e.wait_ge(*AC.at(f"g_zth{j}"))
                e.scalar_tensor_tensor(out=gz[:, j, :], in0=gth[:, j % 2, :], scalar=1.0, in1=gz[:, j, :],
                                       op0=ALU.add, op1=ALU.mult).then_inc(*V.done(f"g_z{j}"))

            e.wait_ge(*PE.at("g_cols7"))
            rsqrt(e, 32, 0.25)
            step(e, e.tensor_scalar(rs[:, 0, 0:16], rs[:, 0, 0:16], 0.5 * GD ** -0.5, None, ALU.mult), V)
            step(e, e.tensor_scalar(rs[:, 0, 16:32], rs[:, 0, 16:32], 0.5, None, ALU.mult), V)
            diagonal(e, 0, "g_diag0", buf=sq[:, 0, :])
            for j in range(8):
                if j:
                    e.wait_ge(*PE.at(f"g_bc{j - 1}"))
                if j < 7:
                    diagonal(e, 4 * j + 4, f"g_diag{j + 1}", buf=sq[:, (j + 1) % 2, :])
                e.wait_ge(*PE.at(f"g_bc{j}"))
                e.tensor_tensor(gqkv[:, j, :], gqkv[:, j, :], (bc, ob[0])[j % 2][:, :], ALU.mult)\
                 .then_inc(*V.done(f"g_n{j}"))
            e.wait_ge(*AC.at("g_el"))
            step(e, e.tensor_tensor(gc[:, 8, :], st[:, 16:32], gc[:, 6, :], ALU.subtract), V, "g_dld")

            def wide(n, t):
                return gc[:, n, 4 * t:4 * t + 4].unsqueeze(2).to_broadcast([P, GH, P])

            def every(x):
                return x.unsqueeze(1).to_broadcast([P, GH, P])

            def bank(x):
                return x[:, :].rearrange("p (h n) -> p h n", h=GH)

            def decay_rows(t):
                if t >= 2:
                    e.wait_ge(*G.at(f"g_qe{t - 2}"))
                e.wait_ge(*V.last())
                e.tensor_copy(ggb[:, t % 2, :, :], wide(5, t)).then_inc(*V.done(f"g_gb{t}"))

            def decay_differences(t):
                g = gG[:, t % 2, :, :]
                e.wait_ge(*PE.at(f"g_D{t}"))
                step(e, e.tensor_tensor(g, wide(6, t), bank(ob[t % 2]), ALU.subtract), V)
                step(e, e.tensor_tensor(g, g, every(negs[:, :]), ALU.add), V, f"g_diff{t}")

            decay_rows(0)
            decay_differences(0)
            for t in range(NT):
                if t < NT - 1:
                    decay_rows(t + 1)
                g = gG[:, t % 2, :, :]
                e.wait_ge(*AC.at(f"g_G{t}"))
                e.wait_ge(*PE.at(f"g_kk{t}"))
                if t:
                    e.wait_ge(*PE.at(f"g_QKT{t - 1}"))
                step(e, e.tensor_tensor(gA, bank(sc[0]), g, ALU.mult), V)
                step(e, e.tensor_tensor(gA, gA, every(strict[:, :]), ALU.mult), V)
                step(e, e.tensor_tensor(gA, gA, wide(4, t), ALU.mult), V, f"g_A{t}")
                e.wait_ge(*PE.at(f"g_qk{t}"))
                e.tensor_tensor(gQK, bank(sc[1]), g, ALU.mult).then_inc(*V.done(f"g_QK{t}"))
                if t < NT - 1:
                    e.wait_ge(*V.last())
                    decay_differences(t + 1)
            e.wait_ge(*V.last())
            e.wait_ge(*G.at("g_TT03"))
            e.wait_ge(levels_in, 16)
            for l in range(1, LEVELS):
                def update(t):
                    if l < LEVELS - 1:
                        e.wait_ge(*PE.at(f"g_P{l}{t}"))
                        e.tensor_tensor(gT[:, t, :, :], gT[:, t, :, :], bank(ob[t % 2]), ALU.subtract)\
                         .then_inc(*V.done(f"g_T{l}{t}"))
                    e.wait_ge(*PE.at(f"g_R{l}{t}"))
                    e.tensor_tensor(gTT[:, t, :, :], gTT[:, t, :, :], bank(acc[t % 2]), ALU.subtract)\
                     .then_inc(*V.done(f"g_TT{l}{t}"))

                for t in range(NT):
                    if t >= 2:
                        e.wait_ge(*PE.at(f"g_X{l}{t - 2}"))
                    elif l > 1:
                        e.wait_ge(*PE.at(f"g_X{l - 1}{t + 2}"))
                    e.tensor_tensor(gMT[:, t % 2, :, :], gAT[:, t, :, :], every(glev[:, l, :]), ALU.mult)\
                     .then_inc(*V.done(f"g_M{l}{t}"))
                    if t >= 2:
                        update(t - 2)
                update(2)
                update(3)
            e.wait_ge(*V.last())
            step(e, e.tensor_tensor(gc[:, 7, :], gc[:, 7, :], gc[:, 4, :], ALU.mult), V)
            step(e, e.tensor_scalar(gc[:, 3, :], gc[:, 4, :], 0.5, None, ALU.mult), V)
            for t in range(NT):
                if t:
                    e.wait_ge(*PE.at(f"g_w{t - 1}"))
                e.tensor_tensor(gkbe[:, :, :], gktok[:, t, :, :], wide(7, t), ALU.mult).then_inc(*V.done(f"g_kbe{t}"))
            for t in range(NT):
                e.tensor_tensor(gvtok[:, t, :, :], gvtok[:, t, :, :], wide(3, t), ALU.mult).then_inc(*V.done("g_vb"))
            for t in range(NT):
                e.tensor_tensor(gkdec[:, t, :, :], gktok[:, t, :, :], wide(8, t), ALU.mult).then_inc(*V.done("g_kdec"))
            for t in range(NT - 1):
                e.wait_ge(*PE.at(f"g_U{t}"))
                if t == 0:
                    e.tensor_copy(gst[:, :, :], bank(acc[0])).then_inc(*V.done("g_S0"))
                    continue
                e.wait_ge(*PE.at(f"g_o{t}"))
                step(e, e.tensor_tensor(gst[:, :, :], gst[:, :, :], wide(9, t), ALU.mult), V)
                e.tensor_tensor(gst[:, :, :], gst[:, :, :], bank(acc[t % 2]), ALU.add).then_inc(*V.done(f"g_S{t}"))
            e.wait_ge(*PE.at("g_ocols3"))
            rsqrt(e, 16, 1.0 / GD)
            diagonal(e, 0, "g_odiag0", buf=sq[:, 0, :])
            for h in range(GH):
                if h:
                    e.wait_ge(*PE.at(f"g_obc{h - 1}"))
                if h < GH - 1:
                    diagonal(e, 4 * h + 4, f"g_odiag{h + 1}", buf=sq[:, (h + 1) % 2, :])
                e.wait_ge(*PE.at(f"g_obc{h}"))
                step(e, e.scalar_tensor_tensor(out=goT[:, h, :], in0=goT[:, h, :], scalar=sm("gdn_norm"),
                                               in1=(bc, ob[0])[h % 2][:, :], op0=ALU.mult, op1=ALU.mult), V)
                e.scalar_tensor_tensor(out=goT[:, h, :], in0=goT[:, h, :], scalar=0.5, in1=gz[:, h, :],
                                       op0=ALU.mult, op1=ALU.mult).then_inc(*V.done(f"g_y{h}"))
            for h in range(GH):
                e.wait_ge(*AC.at(f"g_hi{h}"))
                e.tensor_tensor(Ml[:, h, :], goT[:, h, :], Mh[:, h, :].bitcast(F32), ALU.subtract)\
                 .then_inc(*V.done(f"g_lo{h}"))

            def add_flat(name):
                step(e, e.memset(dg[:, :], 0.0), V)
                with e.Fori(0, 2) as i:
                    V.enter(name, i)
                    for j in range(4):
                        x = xT[:, bass.ds(i * 4 + j, 1), :]
                        e.wait_ge(unit_used, U[name] + j + 1 + i * 4)
                        e.tensor_tensor(x, acc[j % 2][:, :].unsqueeze(1), x, ALU.add).then_inc(*V.done(f"{name}x{j}"))
                        add_squares(e, name, j, i)
                    V.leave(2)

            add_flat("mix_out")

            norm_roots(e, "nx")
            norm_vector(e, "nx", lambda k: sm("norm_cross", k, 1))
            norm_roots(e, "nk", MEM)
            norm_vector(e, "nk", lambda k: sm("norm_mem", k, 1), None, mT, mn, mh, ml, MEM)
            e.wait_ge(*PE.at("x_cols7"))
            rsqrt(e, 24, 1.0 / XD)
            step(e, e.tensor_scalar(rs[:, 0, 0:16], rs[:, 0, 0:16], XD ** -0.5, None, ALU.mult), V)
            for h in range(XH):
                if h:
                    e.wait_ge(*PE.at(f"x_bc{h - 1}"))
                diagonal(e, 16 + 2 * h, f"x_diag{h}", 2)
                e.wait_ge(*PE.at(f"x_bc{h}"))
                e.tensor_tensor(xk[:, h, :], xk[:, h, :], bc[:, 0:MEM], ALU.mult).then_inc(*V.done(f"x_kn{h}"))
            def cross_softmax(h):
                for t in range(NT):
                    e.wait_ge(*PE.at(f"x_sc{h}{t // 2}"))
                    r = 4 * h + t
                    e.tensor_scalar(xS[:, h, t, :], sc[t // 2][:, (t % 2) * MEM:(t % 2 + 1) * MEM],
                                    rs[:, 0, r:r + 1], None, ALU.mult)\
                     .then_inc(*V.done(f"x_s{h}{t // 2}"))
                e.wait_ge(*V.last())
                step(e, e.tensor_reduce(amax[:, 2, 4 * h:4 * h + 4], xS[:, h, :, :], AX.X, ALU.max), V)
                e.tensor_scalar(amax[:, 0, 4 * h:4 * h + 4], amax[:, 2, 4 * h:4 * h + 4], -1.0, None, ALU.mult)\
                 .then_inc(*V.done(f"x_nm{h}"))

            def cross_low(h):
                e.wait_ge(*AC.at(f"x_hi{h}"))
                e.tensor_tensor(Ml[:, h, :], ob[h % 2][:, :], Mh[:, h, :].bitcast(F32), ALU.subtract)\
                 .then_inc(*V.done(f"x_lo{h}"))

            cross_softmax(0)
            cross_softmax(1)
            for h in range(XH):
                e.wait_ge(*AC.at(f"x_exp{h}3"))
                step(e, e.reciprocal(amax[:, 2, 4 * h:4 * h + 4], amax[:, 1, 4 * h:4 * h + 4]), V)
                for t in range(NT):
                    x = xS[:, h, t, :]
                    e.tensor_scalar(x, x, amax[:, 2, 4 * h + t:4 * h + t + 1], None, ALU.mult)\
                     .then_inc(*V.done(f"x_norm{h}"))
                if h < XH - 2:
                    cross_softmax(h + 2)
                if h:
                    cross_low(h - 1)
            cross_low(XH - 1)
            add_flat("xa_out")

            norm_roots(e, "nf")
            norm_vector(e, "nf", lambda k: sm("norm_mlp", k, 1))
            for half in range(2):
                with e.Fori(0, 4) as i:
                    V.enter(f"mlp{half}_vector", i)
                    for j in range(4):
                        x = sq[:, j % 2, :]
                        y = bass.ds(i * 4 + j, 1)
                        e.wait_ge(*AC.at(f"f{half}r{j}", i))
                        e.tensor_tensor(x, x, x, ALU.mult).then_inc(*V.done(f"f{half}y{j}"))
                        e.wait_ge(*AC.at(f"f{half}yh{j}", i))
                        e.tensor_tensor(Yl[:, y, :], x.unsqueeze(1), Yh[:, y, :].bitcast(F32), ALU.subtract)\
                         .then_inc(*V.done(f"f{half}yl{j}"))
                    V.leave(4)
                out_vector(e, f"mlp_out{half}", None, sums=False)

    return {"PE": (PE.marks), "AC": AC.marks, "V": V.marks, "G": G.marks}


def constants():
    import numpy as np
    const = np.zeros((P, NCONST), np.float32)
    i, j = np.arange(P)[:, None], np.arange(P)[None, :]

    def put(name, table):
        c, w = CONST[name]
        const[:, c:c + w] = table

    put("ident", i == j)
    put("causal", i >= j)
    put("cumsum", i <= j)
    put("halves", (i // DD) == np.arange(2)[None, :])
    level = [(i // (2 * b) == j // (2 * b)) & (i // b % 2 == 1) & (j // b % 2 == 0) for b in (1 << n for n in range(LEVELS))]
    levels = np.concatenate([m.T for m in level], axis=1).astype(np.float32)
    key, query = np.arange(P)[:, None], np.arange(S)[None, :]
    gamma = 1.0 - 2.0 ** (-5.0 - np.arange(RH))
    decay = np.where(key // CHUNK <= query // CHUNK, gamma[:, None, None] ** np.abs(query - key), 0.0) * RQK ** -0.5
    decay = np.concatenate([decay, decay[-1:]]).astype(np.float32)
    inv_freq = (np.float32(1) / np.power(np.float32(10000), np.arange(0, RQK, 2, dtype=np.float32) / np.float32(RQK)))
    return const, levels, decay, inv_freq.astype(np.float32)


def lay_out(x):
    import numpy as np
    const, levels, decay, inv_freq = constants()
    a = {name: np.asarray(value) for name, value in x.items()}

    def cols(v):
        return np.ascontiguousarray(v).reshape(-1, P).T

    def twice(v):
        return np.concatenate([v.reshape(-1), v.reshape(-1)])[:, None]

    def taps(w):
        t, c = w.shape
        return w.T.reshape(c // P, P, t).transpose(1, 0, 2).reshape(P, -1)

    small = {
        "c": cols(a["c"]), "norm_g0": cols(a["norm_g"][0]), "norm_g1": cols(a["norm_g"][1]),
        "ada_b0": cols(a["ada_b"][0]), "ada_b1": cols(a["ada_b"][1]), "ret_gn_g": cols(a["ret_gn_g"]),
        "att_q_g": cols(a["att_q_g"]), "att_k_g": cols(a["att_k_g"]), "norm_mix": cols(a["norm_mix_2"]),
        "norm_mem": cols(a["norm_mem_2"]), "norm_cross": cols(a["norm_cross_2"]), "norm_mlp": cols(a["norm_mlp_2"]),
        "gdn_conv": taps(a["gdn_conv_2"][0]), "gdn_a_log": np.repeat(a["gdn_a_log_2"], P, 0),
        "gdn_dt_bias": np.repeat(a["gdn_dt_bias_2"], P, 0), "gdn_norm": cols(a["gdn_norm_2"]),
        "dsa_q_norm": twice(a["dsa_q_norm_2"]), "dsa_k_norm": twice(a["dsa_k_norm_2"]),
        "conv_dw": taps(a["conv_dw_2"][0]), "conv_dw_b": cols(a["conv_dw_b_2"]),
        "conv_ln_g": cols(a["conv_ln_g_2"]), "conv_ln_b": cols(a["conv_ln_b_2"]),
        "xa_q_norm": cols(a["xa_q_norm_2"]), "xa_k_norm": cols(a["xa_k_norm_2"]), "inv_freq": inv_freq[:, None],
    }
    packed = np.concatenate([small[name] for name, _ in SMALL_WIDTHS], axis=1)
    reach = 2 * CHUNK
    distance = np.arange(P)[:, None] - np.arange(S)[None, :] + S - P
    bias = a["att_rel_bias"][0][:, np.clip(distance, -reach, reach) + reach]
    bias = np.concatenate([bias, bias[-2:]])
    w = a["w_in_2"][0]
    w_small = np.concatenate([w[:, 2440:2508], w[:, 2048:2056], w[:, :P - 76]], axis=1)
    given = {"w_small": w_small, "small": packed, "const": const, "levels": levels, "decay": decay, "bias": bias}
    for name in DIRECT:
        given[name] = a[name]
    return {name: np.ascontiguousarray(v) for name, v in given.items()}


DIRECT = ["x", "positions", "ada_w", "ret_w_in", "ret_w_out", "att_w_in", "att_w_out"] + DIRECT_2


def program(nc, given):
    ins = {name: nc.dram_tensor(f"in_{name}", list(v.shape), mybir.dt.from_np(v.dtype), kind="ExternalInput").ap()
           for name, v in given.items()}
    out = nc.dram_tensor("out", [1, S, D], F32, kind="ExternalOutput").ap()
    return ins, out


def kernel(**inputs):
    import numpy as np
    import concourse.bacc as bacc
    from concourse.bass_utils import run_bass_kernel_spmd

    given = lay_out(inputs)
    known = {}
    for _ in range(2):
        nc = bacc.Bacc("TRN2", target_bir_lowering=False, num_devices=1, dynamic_dma_scratch_size=1024)
        ins, out = program(nc, given)
        known = build(nc, ins, out, known)
    r = run_bass_kernel_spmd(nc, [{f"in_{name}": v for name, v in given.items()}], core_ids=[0])
    return r.results[0]["out"]
```
